# Optimizing a Trainium2 kernel written in Bass

```python
import jax, jax.numpy as jnp
from jax import lax
import numpy as np
import math

D_MODEL = 2048
BATCH = 1
SEQ = 256
DEPTH = 2

D_CONV = 512
D_HGRN = 768
D_RET = 768
D_MIX = D_CONV + D_HGRN + D_RET
CONV_WIDTH = 31
HGRN_HEAD_DIM = 128
HGRN_HEADS = D_HGRN // HGRN_HEAD_DIM
RET_HEAD_DIM = 128
RET_HEADS = D_RET // RET_HEAD_DIM
CHUNK = 64
D_FF = 4 * D_MODEL
ROPE_BASE = 10000.0
LN_EPS = 1e-5
DEEPNORM_ALPHA = (2.0 * DEPTH) ** 0.25
DEEPNORM_BETA = (8.0 * DEPTH) ** -0.25
SPLITS = (D_CONV, D_CONV,
          D_HGRN, D_HGRN, D_HGRN, D_HGRN,
          D_RET, D_RET, D_RET, D_RET)
D_IN = sum(SPLITS)


def layer_norm(x, g, b):
    xf = x.astype(jnp.float32)
    mu = jnp.mean(xf, axis=-1, keepdims=True)
    var = jnp.mean(jnp.square(xf - mu), axis=-1, keepdims=True)
    return (xf - mu) * lax.rsqrt(var + LN_EPS) * g + b

def rope(x, positions):
    half = x.shape[-1] // 2
    inv = ROPE_BASE ** (-jnp.arange(half, dtype=jnp.float32) / half)
    ang = positions.astype(jnp.float32)[..., None] * inv
    cos = jnp.cos(ang)[:, :, None, :]
    sin = jnp.sin(ang)[:, :, None, :]
    x1, x2 = x[..., :half], x[..., half:]
    return jnp.concatenate([x1 * cos - x2 * sin, x1 * sin + x2 * cos], axis=-1)

def to_chunks(x):
    b, t, h, d = x.shape
    return x.reshape(b, t // CHUNK, CHUNK, h, d).transpose(1, 0, 3, 2, 4)

def from_chunks(x):
    n, b, h, c, d = x.shape
    return x.transpose(1, 0, 3, 2, 4).reshape(b, n * c, h, d)

def conv_mixer(a_in, gate_in, w_dw, b_dw, ln_g, ln_b):
    u = a_in.astype(jnp.float32) * jax.nn.sigmoid(gate_in.astype(jnp.float32))
    y = lax.conv_general_dilated(u, w_dw.astype(jnp.float32)[:, None, :], window_strides=(1,),
                                 padding=[(CONV_WIDTH - 1, 0)],
                                 dimension_numbers=('NWC', 'WIO', 'NWC'),
                                 feature_group_count=D_CONV) + b_dw
    return jax.nn.silu(layer_norm(y, ln_g, ln_b))

def hgrn2_mixer(q_in, f_in, i_in, g_in, lb, norm_g):
    b, t, _ = q_in.shape
    shp = (b, t, HGRN_HEADS, HGRN_HEAD_DIM)
    q = jax.nn.silu(q_in.astype(jnp.float32)).reshape(shp)
    inp = i_in.astype(jnp.float32).reshape(shp)
    lb = lb.astype(jnp.float32)
    log_sig = jax.nn.log_sigmoid(f_in.astype(jnp.float32))
    pos_lb = lb > 0
    log_lb = jnp.log(jnp.where(pos_lb, lb, 1.0))
    log_f = jnp.where(pos_lb, jnp.logaddexp(log_lb, jnp.log1p(-lb) + log_sig), log_sig)
    k = (-jnp.expm1(log_f)).reshape(shp)
    log_f = log_f.reshape(shp)
    causal = jnp.tril(jnp.ones((CHUNK, CHUNK), dtype=bool))[:, :, None]

    def step(S, xs):
        qc, kc, ic, lfc = xs
        cum = jnp.cumsum(lfc, axis=2)
        rel = cum[:, :, :, None, :] - cum[:, :, None, :, :]
        decay = jnp.where(causal, jnp.exp(jnp.where(causal, rel, 0.0)), 0.0)
        scores = jnp.einsum('bhtd,bhsd,bhtsd->bhts', qc, kc, decay)
        o = (jnp.einsum('bhts,bhse->bhte', scores, ic)
             + jnp.einsum('bhtd,bhde->bhte', qc * jnp.exp(cum), S))
        last = cum[:, :, -1:, :]
        S = (jnp.exp(last[:, :, 0, :])[..., None] * S
             + jnp.einsum('bhsd,bhse->bhde', kc * jnp.exp(last - cum), ic))
        return S, o

    S0 = jnp.zeros((b, HGRN_HEADS, HGRN_HEAD_DIM, HGRN_HEAD_DIM), jnp.float32)
    _, o = lax.scan(step, S0, (to_chunks(q), to_chunks(k), to_chunks(inp), to_chunks(log_f)))
    o = from_chunks(o)
    o = o * lax.rsqrt(jnp.mean(jnp.square(o), axis=-1, keepdims=True) + LN_EPS)
    return o.reshape(b, t, D_HGRN) * norm_g * jax.nn.sigmoid(g_in.astype(jnp.float32))

def retention_mixer(q_in, k_in, v_in, g_in, positions, gn_g, gn_b):
    b, t, _ = q_in.shape
    shp = (b, t, RET_HEADS, RET_HEAD_DIM)
    q = rope(q_in.astype(jnp.float32).reshape(shp), positions)
    k = rope(k_in.astype(jnp.float32).reshape(shp), positions) * RET_HEAD_DIM ** -0.5
    v = v_in.astype(jnp.float32).reshape(shp)
    log_gamma = jnp.log1p(-(2.0 ** (-5.0 - jnp.arange(RET_HEADS, dtype=jnp.float32))))
    idx = jnp.arange(CHUNK, dtype=jnp.float32)
    diff = idx[:, None] - idx[None, :]
    intra = jnp.where(diff >= 0, jnp.exp(log_gamma[:, None, None] * jnp.maximum(diff, 0.0)), 0.0)
    q_decay = jnp.exp(log_gamma[:, None] * (idx + 1.0))
    k_decay = jnp.exp(log_gamma[:, None] * (CHUNK - 1.0 - idx))
    chunk_decay = jnp.exp(log_gamma * CHUNK)

    def step(S, xs):
        qc, kc, vc = xs
        scores = jnp.einsum('bhtd,bhsd->bhts', qc, kc) * intra
        o = (jnp.einsum('bhts,bhse->bhte', scores, vc)
             + jnp.einsum('bhtd,bhde->bhte', qc * q_decay[:, :, None], S))
        S = (chunk_decay[:, None, None] * S
             + jnp.einsum('bhsd,bhse->bhde', kc * k_decay[:, :, None], vc))
        return S, o

    S0 = jnp.zeros((b, RET_HEADS, RET_HEAD_DIM, RET_HEAD_DIM), jnp.float32)
    _, o = lax.scan(step, S0, (to_chunks(q), to_chunks(k), to_chunks(v)))
    o = from_chunks(o)
    mu = jnp.mean(o, axis=-1, keepdims=True)
    var = jnp.mean(jnp.square(o - mu), axis=-1, keepdims=True)
    o = ((o - mu) * lax.rsqrt(var + LN_EPS)).reshape(b, t, D_RET) * gn_g + gn_b
    return jax.nn.silu(g_in.astype(jnp.float32)) * o

def first_inputs(seed: int = 0) -> dict:
    key = jax.random.key(seed)
    ks = jax.random.split(key, 20)
    f32 = jnp.float32

    def nrm(k, shape, scale):
        return jax.random.normal(k, shape, f32) * scale

    x = nrm(ks[0], (BATCH, SEQ, D_MODEL), 1.0)
    positions = (jnp.arange(SEQ, dtype=jnp.int32)[None, :]
                 + jax.random.randint(ks[1], (BATCH, 1), 0, 1024, dtype=jnp.int32))
    return {
        'x': x,
        'positions': positions,
        'w_in': nrm(ks[2], (DEPTH, D_MODEL, D_IN), D_MODEL ** -0.5),
        'w_dw': nrm(ks[3], (DEPTH, CONV_WIDTH, D_CONV), CONV_WIDTH ** -0.5),
        'b_dw': nrm(ks[4], (DEPTH, D_CONV), 0.02),
        'conv_ln_g': 1.0 + nrm(ks[5], (DEPTH, D_CONV), 0.02),
        'conv_ln_b': nrm(ks[6], (DEPTH, D_CONV), 0.02),
        'hgrn_lb': nrm(ks[7], (DEPTH, D_HGRN), 0.1),
        'hgrn_norm_g': 1.0 + nrm(ks[8], (DEPTH, D_HGRN), 0.02),
        'ret_gn_g': 1.0 + nrm(ks[9], (DEPTH, D_RET), 0.02),
        'ret_gn_b': nrm(ks[10], (DEPTH, D_RET), 0.02),
        'w_out': nrm(ks[11], (DEPTH, D_MIX, D_MODEL), D_MIX ** -0.5 * DEEPNORM_BETA),
        'ln1_g': 1.0 + nrm(ks[12], (DEPTH, D_MODEL), 0.02),
        'ln1_b': nrm(ks[13], (DEPTH, D_MODEL), 0.02),
        'w_ff1': nrm(ks[14], (DEPTH, D_MODEL, D_FF), D_MODEL ** -0.5),
        'w_ff2': nrm(ks[15], (DEPTH, D_FF, D_MODEL), D_FF ** -0.5 * DEEPNORM_BETA),
        'ln2_g': 1.0 + nrm(ks[16], (DEPTH, D_MODEL), 0.02),
        'ln2_b': nrm(ks[17], (DEPTH, D_MODEL), 0.02),
    }

def first_block(x, positions, w_in, w_dw, b_dw, conv_ln_g, conv_ln_b, hgrn_lb, hgrn_norm_g,
              ret_gn_g, ret_gn_b, w_out, ln1_g, ln1_b, w_ff1, w_ff2, ln2_g, ln2_b):
    dtype = x.dtype
    lbp = jax.nn.softmax(hgrn_lb.astype(jnp.float32), axis=0)
    lower_bounds = jnp.clip(jnp.cumsum(lbp, axis=0) - lbp[0], 0.0, 1.0 - 1e-6)
    split_idx = np.cumsum(SPLITS)[:-1].tolist()
    for l in range(DEPTH):
        proj = jnp.einsum('btd,de->bte', x, w_in[l])
        ca, cg, hq, hf, hi, hg, rq, rk, rv, rg = jnp.split(proj, split_idx, axis=-1)
        y_conv = conv_mixer(ca, cg, w_dw[l], b_dw[l], conv_ln_g[l], conv_ln_b[l])
        y_hgrn = hgrn2_mixer(hq, hf, hi, hg, lower_bounds[l], hgrn_norm_g[l])
        y_ret = retention_mixer(rq, rk, rv, rg, positions, ret_gn_g[l], ret_gn_b[l])
        mix = jnp.concatenate([y_conv, y_hgrn, y_ret], axis=-1).astype(dtype)
        h = jnp.einsum('bte,ed->btd', mix, w_out[l])
        x = layer_norm(DEEPNORM_ALPHA * x + h, ln1_g[l], ln1_b[l]).astype(dtype)
        f = jnp.square(jax.nn.relu(jnp.einsum('btd,df->btf', x, w_ff1[l])))
        h = jnp.einsum('btf,fd->btd', f, w_ff2[l])
        x = layer_norm(DEEPNORM_ALPHA * x + h, ln2_g[l], ln2_b[l]).astype(dtype)
    return x


HEAD_DIM = 128
GRID_W = 64
NA_HEADS = 6
NA_WIN_H = 8
NA_WIN_W = 16
DN_HEADS = 6
DN_CONV = 5
DN_CHUNK = 64
MEM_HEADS = 4
MEM_LEN = 256
DIFF_HEADS = 6
DIFF_VDIM = 2 * HEAD_DIM
Q_BLOCK = 128
ROPE_THETA = 10000.0
EPS = 1e-6
N_EVEN = (DEPTH + 1) // 2
N_ODD = DEPTH // 2

NA_W = NA_HEADS * HEAD_DIM
DN_W = DN_HEADS * HEAD_DIM
MEM_W = MEM_HEADS * HEAD_DIM
DIFF_W = DIFF_HEADS * DIFF_VDIM
MIX_W = NA_W + DN_W + MEM_W
EVEN_IN = 4 * NA_W + 4 * DN_W + 4 * DN_HEADS + 2 * MEM_W
ODD_IN = 4 * DIFF_W + 2 * MEM_W


def rmsnorm(x, g):
    xf = x.astype(jnp.float32)
    y = xf * lax.rsqrt(jnp.mean(xf * xf, axis=-1, keepdims=True) + EPS)
    return (y * g.astype(jnp.float32)).astype(x.dtype)

def l2norm(x):
    xf = x.astype(jnp.float32)
    return (xf * lax.rsqrt(jnp.sum(xf * xf, axis=-1, keepdims=True) + EPS)).astype(x.dtype)

def rope_2(x, pos):
    d = x.shape[-1]
    inv = ROPE_THETA ** (-jnp.arange(0, d, 2, dtype=jnp.float32) / d)
    ang = pos.astype(jnp.float32)[:, None] * inv[None, :]
    cos, sin = jnp.cos(ang), jnp.sin(ang)
    x1, x2 = jnp.split(x.astype(jnp.float32), 2, axis=-1)
    return jnp.concatenate([x1 * cos - x2 * sin, x1 * sin + x2 * cos], axis=-1).astype(x.dtype)

def split_cols(t, sizes):
    out, start = [], 0
    for s in sizes:
        out.append(t[..., start:start + s])
        start += s
    return out

def to_heads(t, n_heads):
    B, T, _ = t.shape
    return t.reshape(B, T, n_heads, -1).transpose(0, 2, 1, 3)

def merge_heads(o):
    B, H, T, d = o.shape
    return o.transpose(0, 2, 1, 3).reshape(B, T, H * d)

def dwconv_centred(x, w):
    K, C = w.shape
    pad = K // 2
    return lax.conv_general_dilated(x, w[:, None, :], window_strides=(1,), padding=[(pad, pad)],
                                    dimension_numbers=('NWC', 'WIO', 'NWC'), feature_group_count=C)

def neighbourhood_attention(q, k, v, rpb):
    B, H, T, d = q.shape
    rows = T // GRID_W
    kh = min(NA_WIN_H, rows)
    r = jnp.arange(rows)
    r0 = jnp.clip(r - kh // 2, 0, rows - kh)
    key_rows = r0[:, None] + jnp.arange(kh)[None, :]
    c = jnp.arange(GRID_W)
    c0 = jnp.clip(c - NA_WIN_W // 2, 0, GRID_W - NA_WIN_W)
    col_ok = (c[None, :] >= c0[:, None]) & (c[None, :] < c0[:, None] + NA_WIN_W)
    qg = q.reshape(B, H, rows, GRID_W, d)
    kg = k.reshape(B, H, rows, GRID_W, d)[:, :, key_rows]
    vg = v.reshape(B, H, rows, GRID_W, d)[:, :, key_rows]
    s = jnp.einsum('bhrqd,bhrikd->bhrqik', qg, kg, preferred_element_type=jnp.float32) * (d ** -0.5)
    dr = key_rows - r[:, None] + (NA_WIN_H - 1)
    dc = jnp.clip(c[None, :] - c[:, None], -(NA_WIN_W - 1), NA_WIN_W - 1) + (NA_WIN_W - 1)
    bias = rpb[:, dr[:, None, :, None], dc[None, :, None, :]]
    s = s + bias[None].astype(jnp.float32)
    s = jnp.where(col_ok[None, None, None, :, None, :], s, -jnp.inf)
    p = jax.nn.softmax(s.reshape(B, H, rows, GRID_W, kh * GRID_W), axis=-1).reshape(s.shape)
    o = jnp.einsum('bhrqik,bhrikd->bhrqd', p.astype(v.dtype), vg)
    return o.reshape(B, H, T, d)

def gated_delta_rule_chunked(q, k, v, g, beta):
    out_dtype = v.dtype
    f32 = jnp.float32
    B, H, T, dk = q.shape
    dv = v.shape[-1]
    C = DN_CHUNK
    N = T // C
    q = q.astype(f32).reshape(B, H, N, C, dk)
    k = k.astype(f32).reshape(B, H, N, C, dk)
    v = v.astype(f32).reshape(B, H, N, C, dv)
    g = g.astype(f32).reshape(B, H, N, C)
    beta = beta.astype(f32).reshape(B, H, N, C)
    G = jnp.cumsum(g, axis=-1)
    lower_incl = jnp.tril(jnp.ones((C, C), bool))
    lower_strict = jnp.tril(jnp.ones((C, C), bool), -1)
    decay = jnp.exp(jnp.where(lower_incl, G[..., :, None] - G[..., None, :], -jnp.inf))
    kb = k * beta[..., None]
    a_mat = jnp.where(lower_strict, jnp.einsum('bhnid,bhnjd->bhnij', kb, k) * decay, 0.0)
    rhs = jnp.concatenate([v * beta[..., None], kb * jnp.exp(G)[..., None]], axis=-1)
    sol = lax.linalg.triangular_solve(a_mat + jnp.eye(C, dtype=f32), rhs, left_side=True, lower=True)
    u, w = sol[..., :dv], sol[..., dv:]
    qk = jnp.einsum('bhnid,bhnjd->bhnij', q, k) * decay
    q_dec = q * jnp.exp(G)[..., None]
    k_dec = k * jnp.exp(G[..., -1:] - G)[..., None]
    g_end = jnp.exp(G[..., -1])

    def step(S, xs):
        u_c, w_c, qk_c, qd_c, kd_c, ge = xs
        v_new = u_c - jnp.einsum('bhcd,bhde->bhce', w_c, S)
        o = jnp.einsum('bhcd,bhde->bhce', qd_c, S) + jnp.einsum('bhij,bhje->bhie', qk_c, v_new)
        S = S * ge[..., None, None] + jnp.einsum('bhcd,bhce->bhde', kd_c, v_new)
        return S, o

    xs = tuple(jnp.moveaxis(a, 2, 0) for a in (u, w, qk, q_dec, k_dec, g_end))
    S0 = jnp.zeros((B, H, dk, dv), f32)
    _, o = lax.scan(step, S0, xs)
    return jnp.moveaxis(o, 0, 2).reshape(B, H, T, dv).astype(out_dtype)

def deltanet_branch(qkv, ba, conv_w, a_log, dt_bias, out_norm):
    qkv = jax.nn.silu(dwconv_centred(qkv, conv_w))
    q, k, v = [to_heads(t, DN_HEADS) for t in jnp.split(qkv, 3, axis=-1)]
    q = l2norm(q) * (HEAD_DIM ** -0.5)
    k = l2norm(k)
    b_f, b_b, a_f, a_b = [t.transpose(0, 2, 1).astype(jnp.float32) for t in jnp.split(ba, 4, axis=-1)]
    al = a_log.astype(jnp.float32)
    dtb = dt_bias.astype(jnp.float32)
    g_f = -jnp.exp(al[0])[None, :, None] * jax.nn.softplus(a_f + dtb[0][None, :, None])
    g_b = -jnp.exp(al[1])[None, :, None] * jax.nn.softplus(a_b + dtb[1][None, :, None])
    o_f = gated_delta_rule_chunked(q, k, v, g_f, jax.nn.sigmoid(b_f))
    flip = lambda t: jnp.flip(t, axis=2)
    o_b = flip(gated_delta_rule_chunked(flip(q), flip(k), flip(v), flip(g_b), flip(jax.nn.sigmoid(b_b))))
    return merge_heads(rmsnorm(o_f + o_b, out_norm))

def memory_branch(mem_q, mem_n, w_kv, q_norm, k_norm):
    q = rmsnorm(to_heads(mem_q, MEM_HEADS), q_norm)
    k, v = jnp.split(mem_n @ w_kv, 2, axis=-1)
    k = rmsnorm(to_heads(k, MEM_HEADS), k_norm)
    v = to_heads(v, MEM_HEADS)
    s = jnp.einsum('bhtd,bhmd->bhtm', q, k, preferred_element_type=jnp.float32) * (HEAD_DIM ** -0.5)
    p = jax.nn.softmax(s, axis=-1)
    return merge_heads(jnp.einsum('bhtm,bhmd->bhtd', p.astype(v.dtype), v))

def diff_attention(q, k, v, lam):
    B, H, _, T, d = q.shape
    nb = T // Q_BLOCK
    qb = jnp.moveaxis(q.reshape(B, H, 2, nb, Q_BLOCK, d), 3, 0)

    def block(qi):
        s = jnp.einsum('bhmqd,bhmkd->bhmqk', qi, k, preferred_element_type=jnp.float32) * (d ** -0.5)
        p = jax.nn.softmax(s, axis=-1)
        attn = p[:, :, 0] - lam * p[:, :, 1]
        return jnp.einsum('bhqk,bhke->bhqe', attn.astype(v.dtype), v)

    o = lax.map(block, qb)
    return jnp.moveaxis(o, 0, 2).reshape(B, H, T, v.shape[-1])

def even_layer(x, mem_n, ln_g, w_in, w_mem_kv, w_out, na_q_norm, na_k_norm, na_rpb,
               dn_conv_w, dn_a_log, dn_dt_bias, dn_out_norm, mem_q_norm, mem_k_norm):
    h = rmsnorm(x, ln_g)
    proj = h @ w_in
    na_qkv, na_gate, dn_qkv, dn_gate, dn_ba, mem_q, mem_gate = split_cols(
        proj, [3 * NA_W, NA_W, 3 * DN_W, DN_W, 4 * DN_HEADS, MEM_W, MEM_W])
    q, k, v = [to_heads(t, NA_HEADS) for t in jnp.split(na_qkv, 3, axis=-1)]
    q = rmsnorm(q, na_q_norm)
    k = rmsnorm(k, na_k_norm)
    na_o = merge_heads(neighbourhood_attention(q, k, v, na_rpb)) * jax.nn.silu(na_gate)
    dn_o = deltanet_branch(dn_qkv, dn_ba, dn_conv_w, dn_a_log, dn_dt_bias, dn_out_norm) * jax.nn.silu(dn_gate)
    mem_o = memory_branch(mem_q, mem_n, w_mem_kv, mem_q_norm, mem_k_norm) * jax.nn.silu(mem_gate)
    return x + jnp.concatenate([na_o, dn_o, mem_o], axis=-1) @ w_out

def odd_layer(x, mem_n, layer_idx, ln_g, w_in, w_mem_kv, w_out, q_norm, k_norm, lam_vecs, subln_g,
              mem_q_norm, mem_k_norm):
    B, T, _ = x.shape
    h = rmsnorm(x, ln_g)
    proj = h @ w_in
    q, k, v, gate, mem_q, mem_gate = split_cols(proj, [DIFF_W, DIFF_W, DIFF_W, DIFF_W, MEM_W, MEM_W])
    pos = jnp.arange(T)
    q = q.reshape(B, T, DIFF_HEADS, 2, HEAD_DIM).transpose(0, 2, 3, 1, 4)
    k = k.reshape(B, T, DIFF_HEADS, 2, HEAD_DIM).transpose(0, 2, 3, 1, 4)
    q = rope_2(rmsnorm(q, q_norm), pos)
    k = rope_2(rmsnorm(k, k_norm), pos)
    v = to_heads(v, DIFF_HEADS)
    lam_init = 0.8 - 0.6 * math.exp(-0.3 * layer_idx)
    lv = lam_vecs.astype(jnp.float32)
    lam = jnp.exp(jnp.sum(lv[0] * lv[1])) - jnp.exp(jnp.sum(lv[2] * lv[3])) + lam_init
    o = rmsnorm(diff_attention(q, k, v, lam), subln_g) * (1.0 - lam_init)
    diff_o = merge_heads(o) * jax.nn.silu(gate)
    mem_o = memory_branch(mem_q, mem_n, w_mem_kv, mem_q_norm, mem_k_norm) * jax.nn.silu(mem_gate)
    return x + jnp.concatenate([diff_o, mem_o], axis=-1) @ w_out

def second_inputs(seed: int = 0) -> dict:
    key = jax.random.key(seed)
    keys = iter(jax.random.split(key, 40))

    def nrm(shape, scale):
        return jax.random.normal(next(keys), shape, jnp.float32) * scale

    def gain(shape):
        return 1.0 + nrm(shape, 0.05)

    D = D_MODEL
    return {
        'x': nrm((BATCH, SEQ, D), 1.0),
        'mem': nrm((BATCH, MEM_LEN, D), 1.0),
        'mem_norm_g': gain((D,)),
        'e_ln_g': gain((N_EVEN, D)),
        'e_w_in': nrm((N_EVEN, D, EVEN_IN), D ** -0.5),
        'e_w_mem_kv': nrm((N_EVEN, D, 2 * MEM_W), D ** -0.5),
        'e_w_out': nrm((N_EVEN, MIX_W, D), MIX_W ** -0.5),
        'na_q_norm': gain((N_EVEN, HEAD_DIM)),
        'na_k_norm': gain((N_EVEN, HEAD_DIM)),
        'na_rpb': nrm((N_EVEN, NA_HEADS, 2 * NA_WIN_H - 1, 2 * NA_WIN_W - 1), 0.1),
        'dn_conv_w': nrm((N_EVEN, DN_CONV, 3 * DN_W), DN_CONV ** -0.5),
        'dn_a_log': jnp.log(jax.random.uniform(next(keys), (N_EVEN, 2, DN_HEADS), jnp.float32, 1.0, 16.0)),
        'dn_dt_bias': nrm((N_EVEN, 2, DN_HEADS), 0.1),
        'dn_out_norm': gain((N_EVEN, HEAD_DIM)),
        'e_mem_q_norm': gain((N_EVEN, HEAD_DIM)),
        'e_mem_k_norm': gain((N_EVEN, HEAD_DIM)),
        'o_ln_g': gain((N_ODD, D)),
        'o_w_in': nrm((N_ODD, D, ODD_IN), D ** -0.5),
        'o_w_mem_kv': nrm((N_ODD, D, 2 * MEM_W), D ** -0.5),
        'o_w_out': nrm((N_ODD, MIX_W, D), MIX_W ** -0.5),
        'df_q_norm': gain((N_ODD, HEAD_DIM)),
        'df_k_norm': gain((N_ODD, HEAD_DIM)),
        'df_lambda': nrm((N_ODD, 4, HEAD_DIM), 0.1),
        'df_subln': gain((N_ODD, DIFF_VDIM)),
        'o_mem_q_norm': gain((N_ODD, HEAD_DIM)),
        'o_mem_k_norm': gain((N_ODD, HEAD_DIM)),
    }

def second_block(x, mem, mem_norm_g, e_ln_g, e_w_in, e_w_mem_kv, e_w_out, na_q_norm, na_k_norm, na_rpb,
              dn_conv_w, dn_a_log, dn_dt_bias, dn_out_norm, e_mem_q_norm, e_mem_k_norm,
              o_ln_g, o_w_in, o_w_mem_kv, o_w_out, df_q_norm, df_k_norm, df_lambda, df_subln,
              o_mem_q_norm, o_mem_k_norm):
    mem_n = rmsnorm(mem, mem_norm_g)
    for layer in range(DEPTH):
        i = layer // 2
        if layer % 2 == 0:
            x = even_layer(x, mem_n, e_ln_g[i], e_w_in[i], e_w_mem_kv[i], e_w_out[i], na_q_norm[i], na_k_norm[i],
                           na_rpb[i], dn_conv_w[i], dn_a_log[i], dn_dt_bias[i], dn_out_norm[i],
                           e_mem_q_norm[i], e_mem_k_norm[i])
        else:
            x = odd_layer(x, mem_n, layer, o_ln_g[i], o_w_in[i], o_w_mem_kv[i], o_w_out[i], df_q_norm[i],
                          df_k_norm[i], df_lambda[i], df_subln[i], o_mem_q_norm[i], o_mem_k_norm[i])
    return x


def setup_inputs(seed=0):
    out = dict(first_inputs(seed))
    for name, value in second_inputs(seed + 1).items():
        if name != "x":
            out[name + "_2"] = value
    return out


def reference(
    x, positions, w_in, w_dw, b_dw, conv_ln_g, conv_ln_b, hgrn_lb, hgrn_norm_g, ret_gn_g,
    ret_gn_b, w_out, ln1_g, ln1_b, w_ff1, w_ff2, ln2_g, ln2_b, mem_2, mem_norm_g_2, e_ln_g_2,
    e_w_in_2, e_w_mem_kv_2, e_w_out_2, na_q_norm_2, na_k_norm_2, na_rpb_2, dn_conv_w_2,
    dn_a_log_2, dn_dt_bias_2, dn_out_norm_2, e_mem_q_norm_2, e_mem_k_norm_2, o_ln_g_2, o_w_in_2,
    o_w_mem_kv_2, o_w_out_2, df_q_norm_2, df_k_norm_2, df_lambda_2, df_subln_2, o_mem_q_norm_2,
    o_mem_k_norm_2,
):
    x = first_block(
        x, positions, w_in, w_dw, b_dw, conv_ln_g, conv_ln_b, hgrn_lb, hgrn_norm_g, ret_gn_g,
        ret_gn_b, w_out, ln1_g, ln1_b, w_ff1, w_ff2, ln2_g, ln2_b,
    )
    return second_block(
        x, mem_2, mem_norm_g_2, e_ln_g_2, e_w_in_2, e_w_mem_kv_2, e_w_out_2, na_q_norm_2,
        na_k_norm_2, na_rpb_2, dn_conv_w_2, dn_a_log_2, dn_dt_bias_2, dn_out_norm_2,
        e_mem_q_norm_2, e_mem_k_norm_2, o_ln_g_2, o_w_in_2, o_w_mem_kv_2, o_w_out_2,
        df_q_norm_2, df_k_norm_2, df_lambda_2, df_subln_2, o_mem_q_norm_2, o_mem_k_norm_2,
    )


_drawn_inputs = setup_inputs


def setup_inputs(seed=0):
    import zlib

    import numpy as np

    out = dict(_drawn_inputs(seed))
    spreads = {}
    factors = {'b_dw': 5.812,
     'conv_ln_g': 8.0,
     'conv_ln_b': 8.0,
     'hgrn_lb': 8.0,
     'hgrn_norm_g': 8.0,
     'ret_gn_g': 8.0,
     'ret_gn_b': 8.0,
     'mem_norm_g_2': 8.0,
     'na_q_norm_2': 8.0,
     'na_k_norm_2': 8.0,
     'na_rpb_2': 8.0,
     'dn_dt_bias_2': 8.0,
     'dn_out_norm_2': 3.271,
     'e_mem_q_norm_2': 8.0,
     'e_mem_k_norm_2': 8.0,
     'df_q_norm_2': 7.211,
     'df_k_norm_2': 8.0,
     'df_subln_2': 12.714,
     'o_mem_q_norm_2': 8.0,
     'o_mem_k_norm_2': 8.0}
    for name, (base, spread) in spreads.items():
        noise = np.random.default_rng([zlib.crc32(name.encode()), seed]).standard_normal(out[name].shape)
        drawn = base * np.exp(spread * noise) if base else spread * noise
        out[name] = __import__('jax').numpy.asarray(drawn.astype(out[name].dtype))
    for name, factor in factors.items():
        out[name] = (out[name] * factor).astype(out[name].dtype)
    return out
```

```python
import math

import numpy as np

import concourse.bass as bass
from concourse import mybir

F32 = mybir.dt.float32
F32R = mybir.dt.float32r
I32 = mybir.dt.int32
ACT = mybir.ActivationFunctionType
ALU = mybir.AluOpType
AX_X = mybir.AxisListType.X

P = 128
SEQ = 256
TT = SEQ // P
D = 2048
KT = D // P
NC = 512
D_FF = 8192
DEPTH = 2
HEADS = 6
HD = 128
HALF = HD // 2
HW = HEADS * HD
CONV_C = 512
CONV_W = 31
D_IN = 2 * CONV_C + 8 * HW
LN_EPS = 1e-5
EPS = 1e-6
ALPHA = (2.0 * DEPTH) ** 0.25

BLOCKS = 8
KB = KT // BLOCKS
HI_SLOTS = 4


class Count:

    def __init__(self, sem, made=0):
        self.sem = sem
        self.made = self.first = made
        self.seen = {}

    def up(self, n=1):
        self.made += n
        return self.sem, n

    def now(self):
        return self.sem, self.made

    def next(self, who, n=1):
        self.seen[who] = self.seen.get(who, self.first) + n
        return self.sem, self.seen[who]


class Core:
    pass


def level_masks():
    s, t = np.arange(P)[:, None], np.arange(P)[None, :]
    out = []
    for n in range(7):
        h = 64 >> n
        out.append((s // (2 * h) == t // (2 * h)) & (s % (2 * h) < h) & (t % (2 * h) >= h))
    return np.stack(out, 1).astype(np.float32)


def retention_mask():
    s, t = np.arange(P)[:, None], np.arange(SEQ)[None, :]
    log_gamma = np.log1p(-(2.0 ** (-5.0 - np.arange(HEADS))))
    m = np.where(t >= s, np.exp(log_gamma[:, None, None] * np.maximum(t - s, 0)), 0.0) * HD ** -0.5
    return m.transpose(1, 0, 2).astype(np.float32)


def constants():
    f32 = np.float32
    eye = np.eye(P, dtype=f32)
    tri = np.triu(np.ones((P, P), f32))
    lev = level_masks()
    inv = (f32(10000.0) ** (-np.arange(HALF, dtype=f32) / f32(HALF))).astype(f32)
    inv2 = (f32(10000.0) ** (-np.arange(0, HD, 2, dtype=f32) / f32(HD))).astype(f32)
    ang = np.arange(SEQ, dtype=f32)[:, None] * inv2[None, :]
    rope = np.stack([np.cos(ang), np.sin(ang)], 1).astype(f32)
    j, v = np.arange(31)[:, None], np.arange(63 + P)[None, :]
    band = ((63 - v + 15) % 64 == j).astype(f32)
    c, k = np.arange(64)[:, None], np.arange(64)[None, :]
    c0 = np.clip(c - 8, 0, 48)
    window = np.where((k >= c0) & (k < c0 + 16), 0.0, -1e30).astype(f32)
    return {
        "c_square": np.concatenate([eye, tri, np.ascontiguousarray(tri.T), np.ones((P, P), f32)], 1),
        "c_levels": np.ascontiguousarray(lev.reshape(P, 7 * P)),
        "c_retention": np.ascontiguousarray(retention_mask().reshape(P, HEADS * SEQ)),
        "c_inv_freq": inv.reshape(1, HALF),
        "c_rope": rope.reshape(SEQ, HD),
        "c_band": band,
        "c_window": np.concatenate([window, window], 0),
        "c_pairs": np.ascontiguousarray((lev + lev.transpose(2, 1, 0)).reshape(P, 7 * P)),
    }


def set_up(nc, dram, out):
    k = Core()
    k.nc, k.dram, k.out = nc, dram, out
    k.at = {}

    def sb(name, address, shape, dtype=F32):
        size = 4 * int(np.prod(shape[1:]))
        return nc.alloc_sbuf_tensor_at("sb_" + name, shape, dtype, offset=base + address)

    def small(name, shape, dtype=F32):
        at = k.small
        k.small += (4 * int(np.prod(shape[1:])) + 31) // 32 * 32
        assert k.small <= k.small_end, name
        return sb(name, at, shape, dtype)

    k.sb, k.sb_small = sb, small
    K = 1024
    base = k.base = 33 * 512
    k.raw = sb("raw", 0, [P, BLOCKS, KB, NC])
    k.w_hi = sb("w_hi", 32 * K, [P, HI_SLOTS, KB, NC], F32R)
    k.w_lo = sb("w_lo", 48 * K, [P, HI_SLOTS, KB, NC], F32R)
    k.x = sb("x", 64 * K, [P, TT, D])
    k.a_hi = sb("a_hi", 80 * K, [P, KT, SEQ], F32R)
    k.a_lo = sb("a_lo", 96 * K, [P, KT, SEQ], F32R)
    k.scratch = 80 * K
    k.p0 = 112 * K
    k.proj = sb("proj", k.p0, [P, TT, D_IN])
    k.f_hi = sb("f_hi", k.p0, [P, KT, SEQ], F32R)
    k.f_lo = sb("f_lo", k.p0 + 16 * K, [P, KT, SEQ], F32R)
    k.relu = sb("relu", k.p0 + 32 * K, [P, 2, TT, NC])
    k.relu2 = sb("relu2", k.p0 + 40 * K, [P, 2, TT, NC])
    t0 = 168 * K
    k.square = sb("square", t0, [P, 4, P])
    k.ident, k.tri, k.tri_t, k.ones = (k.square[:, n, :] for n in range(4))
    k.small, k.small_end = t0 + 2 * K, t0 + 4 * K
    k.stats = small("stats", [P, TT, D // NC, 6])
    k.mv = small("mv", [P, TT, 2])
    k.rstd = small("rstd", [P, TT])
    k.eps = small("eps", [P, 2])
    k.mixer_small = k.small
    k.cos = sb("cos", t0 + 4 * K, [P, TT, HALF])
    k.sin = sb("sin", t0 + 4 * K + 512, [P, TT, HALF])
    k.inv_freq = sb("inv_freq", k.p0, [P, HALF])
    k.turns = sb("turns", k.p0 + 256, [P, TT, HALF])
    k.pos_i = sb("pos_i", k.p0 + 768, [P, TT], I32)
    k.pos_f = sb("pos_f", k.p0 + 800, [P, TT])
    k.gain = sb("gain", t0 + 5 * K, [P, D])
    k.shift = sb("shift", t0 + 13 * K, [P, D])
    k.t1 = t0 + 5 * K
    k.t2 = t0 + 21 * K

    k.ps_unit = nc.alloc_psum_tensor("ps_unit", [P, 2, TT, NC], F32)
    k.ps = nc.alloc_psum_tensor("ps_mix", [P, 4, NC], F32)

    def count(*names):
        return (Count(nc.alloc_semaphore(name)) for name in names)

    def later(made, *earlier):
        for old in earlier:
            k.taken_over.append((old, made))
        return (Count(old.sem, made) for old in earlier)

    k.count, k.later, k.taken_over = count, later, []
    k.raw_ready = [nc.alloc_semaphore(f"raw_ready{j}") for j in range(BLOCKS)]
    k.hi_ready = nc.alloc_semaphore("hi_ready")
    k.lo_ready = nc.alloc_semaphore("lo_ready")
    k.block_done = nc.alloc_semaphore("block_done")
    k.evacuated = nc.alloc_semaphore("evacuated")
    k.block0 = dict.fromkeys(("sp", "act", "dve", "pe", "pool"), 0)
    k.relu2_ready = nc.alloc_semaphore("relu2_ready")
    k.f_turned = nc.alloc_semaphore("f_turned")
    k.f_lo_ready = nc.alloc_semaphore("f_lo_ready")
    k.f_hi_ready = nc.alloc_semaphore("f_hi_ready")
    k.stats_ready = nc.alloc_semaphore("stats_ready")
    k.stats_units = 0
    k.consts_in, k.x_in, k.row_in, k.eps_set, k.turn_source = count("consts_in", "x_in", "row_in", "eps_set", "turn_source")
    k.turned, k.turn_hi, k.turn_lo, k.pos_in, k.angles = count("turned", "turn_hi", "turn_lo", "pos_in", "angles")
    k.rotary, k.aggregated, k.root, k.normed, k.dve_step = count("rotary", "aggregated", "root", "normed", "dve_step")
    k.act_step, k.pool_step, k.stored = count("act_step", "pool_step", "stored")
    return k



def sp_units(sp, k, weights, units, column=0):
    first = k.block0["sp"]
    k.block0["sp"] += units * BLOCKS
    with sp.Fori(0, units // 2) as i:
        for s in range(2):
            sp_unit(sp, k, weights, 0, i * (2 * BLOCKS) + first, s, i * (2 * NC) + (column + s * NC))


def sp_unit(sp, k, weights, row, b0, s, column):
    w = weights[row:row + D, :].rearrange("(kt p) n -> p kt n", p=P)
    for j in range(BLOCKS):
        sp.wait_ge(k.lo_ready, b0 + (s * BLOCKS + j + 1))
        sp.dma_start(k.raw[:, j], w[:, KB * j:KB * (j + 1), bass.ds(column, NC)]).then_inc(k.raw_ready[j], 16)


def act_split(act, k, b0, c):
    j, slot = c % BLOCKS, c % HI_SLOTS
    act.wait_ge(k.raw_ready[j], b0 * 2 + 16 * (c // BLOCKS + 1))
    act.wait_ge(k.block_done, b0 + (c + 1))
    k.nc.scalar.activation(k.w_hi[:, slot], k.raw[:, j], ACT.Copy).then_inc(k.hi_ready, 1)


def dve_split(dve, k, b0, c):
    j, slot = c % BLOCKS, c % HI_SLOTS
    dve.wait_ge(k.hi_ready, b0 + (c + 1))
    k.nc.vector.tensor_tensor(k.w_lo[:, slot], k.raw[:, j], k.w_hi[:, slot].bitcast(F32),
                              ALU.subtract).then_inc(k.lo_ready, 1)


def pe_block(pe, k, b0, c, hi, lo):
    s, j, slot = c // BLOCKS % 2, c % BLOCKS, c % HI_SLOTS
    if j == 0:
        pe.wait_ge(k.evacuated, b0 + (c + BLOCKS))
    pe.wait_ge(k.lo_ready, b0 + (BLOCKS + c + 1))
    for n in range(KB):
        kt = KB * j + n
        for t in range(TT):
            tokens = slice(t * P, (t + 1) * P)
            acc = k.ps_unit[:, s, t, :]
            w_hi, w_lo = k.w_hi[:, slot, n, :], k.w_lo[:, slot, n, :]
            k.nc.tensor.matmul(acc, hi[:, kt, tokens], w_hi, start=kt == 0, stop=False)
            k.nc.tensor.matmul(acc, hi[:, kt, tokens], w_lo, start=False, stop=False)
            last = k.nc.tensor.matmul(acc, lo[:, kt, tokens], w_hi, start=False, stop=kt == KT - 1)
    last.then_inc(k.block_done, 1)


def pe_units(pe, k, units):
    first = k.block0["pe"]
    k.block0["pe"] += units * BLOCKS
    with pe.Fori(0, units // 2) as i:
        for c in range(2 * BLOCKS):
            pe_block(pe, k, i * (2 * BLOCKS) + first, c, k.a_hi, k.a_lo)


def split_units(eng, k, who, split, units, take=None, last=False):
    first = k.block0[who]
    k.block0[who] += units * BLOCKS
    pairs = units // 2

    def pair(b0, i, ending):
        for s in range(2):
            for c in range(HI_SLOTS, HI_SLOTS + BLOCKS):
                if not (ending and s == 1 and c >= BLOCKS):
                    split(eng, k, b0, s * BLOCKS + c)
            if take:
                take(b0, s, i)

    loops = pairs - 1 if last else pairs
    if loops:
        with eng.Fori(0, loops) as i:
            pair(i * (2 * BLOCKS) + first, i, False)
    if last:
        pair(first + loops * 2 * BLOCKS, loops, True)


def wait_unit(eng, k, b0, s):
    eng.wait_ge(k.block_done, b0 + (HI_SLOTS + (s + 1) * BLOCKS))


def act_take_proj(act, k, column=0):
    def take(b0, s, i):
        wait_unit(act, k, b0, s)
        k.nc.scalar.activation(k.proj[:, :, bass.ds(i * (2 * NC) + (column + s * NC), NC)], k.ps_unit[:, s],
                               ACT.Copy).then_inc(k.evacuated, BLOCKS)
    return take


def dve_take_residual(dve, k):
    def take(b0, s, i):
        residual(dve, k, b0, s, i * 2 + s)
    return take


def residual(dve, k, b0, u, chunk):
    wait_unit(dve, k, b0, u)
    cols = bass.ds(chunk * NC, NC)
    k.nc.vector.tensor_tensor(k.x[:, :, cols], k.x[:, :, cols], k.ps_unit[:, u % 2],
                              ALU.add).then_inc(k.evacuated, BLOCKS)
    dve.wait_ge(k.evacuated, b0 + (u + 3) * BLOCKS)
    for t in range(TT):
        last = k.nc.vector.bn_stats(k.stats[:, t, bass.ds(chunk, 1), :].rearrange("p c s -> p (c s)"), k.x[:, t, cols])
    last.then_inc(k.stats_ready, 1)


def pe_turn(pe, k, tile):
    for g in range(BLOCKS):
        pe.wait_ge(*k.turn_source.next("pe"))
        if g >= 4:
            pe.wait_ge(*k.turn_lo.next("pe"))
        bank = k.ps[:, g % 4, :].rearrange("p (a s) -> p a s", a=KB)
        for n in range(KB):
            for t in range(TT):
                last = k.nc.tensor.transpose(bank[:, n, t * P:(t + 1) * P], tile(KB * g + n, t), k.ident)
        last.then_inc(*k.turned.up())
    pe.wait_ge(*k.turn_lo.next("pe", 4))


def act_turn(act, k):
    for g in range(BLOCKS):
        act.wait_ge(*k.turned.next("act"))
        k.nc.scalar.activation(k.a_hi[:, KB * g:KB * (g + 1), :],
                               k.ps[:, g % 4, :].rearrange("p (a s) -> p a s", a=KB), ACT.Copy).then_inc(*k.turn_hi.up())


def dve_turn(dve, k):
    for g in range(BLOCKS):
        dve.wait_ge(*k.turn_hi.next("dve"))
        part = slice(KB * g, KB * (g + 1))
        k.nc.vector.tensor_tensor(k.a_lo[:, part, :], k.ps[:, g % 4, :].rearrange("p (a s) -> p a s", a=KB),
                                  k.a_hi[:, part, :].bitcast(F32), ALU.subtract).then_inc(*k.turn_lo.up())


def pool_rows(pool, k, *rows):
    for row, to in zip(rows, (k.gain, k.shift)):
        pool.dma_start(to[:], row.partition_broadcast(P)).then_inc(*k.row_in.up(16))


def dve_layer_norm(dve, k, units, done):
    v = k.nc.vector
    k.stats_units += units
    dve.wait_ge(k.stats_ready, k.stats_units)
    for t in range(TT):
        last = v.bn_aggr(k.mv[:, t, :], k.stats[:, t].rearrange("p c s -> p (c s)"))
    last.then_inc(*k.aggregated.up())
    dve.wait_ge(*k.root.next("dve"))
    v.reciprocal(k.rstd[:], k.rstd[:]).then_inc(*k.dve_step.up())
    dve.wait_ge(*k.row_in.next("dve", 32))
    dve.wait_ge(*k.dve_step.now())
    for c in range(D // NC):
        cols = slice(c * NC, (c + 1) * NC)
        for t in range(TT):
            last = v.scalar_tensor_tensor(k.x[:, t, cols], k.x[:, t, cols], k.mv[:, t, 0:1], k.gain[:, cols],
                                          ALU.subtract, ALU.mult)
        last.then_inc(*k.dve_step.up())
        dve.wait_ge(*k.dve_step.now())
        for t in range(TT):
            last = v.scalar_tensor_tensor(k.x[:, t, cols], k.x[:, t, cols], k.rstd[:, t:t + 1], k.shift[:, cols],
                                          ALU.mult, ALU.add)
        last.then_inc(*done.up(2))


def act_layer_norm(act, k):
    act.wait_ge(*k.aggregated.next("act"))
    k.nc.scalar.activation(k.rstd[:], k.mv[:, :, 1], ACT.Sqrt, bias=k.eps[:, 0:1]).then_inc(*k.root.up())


def dve_scale_residual(dve, k):
    dve.wait_ge(*k.turn_lo.now())
    k.nc.vector.tensor_scalar(k.x[:], k.x[:], ALPHA, None, ALU.mult).then_inc(*k.dve_step.up())
    dve.wait_ge(*k.dve_step.now())


FF_GROUPS = D_FF // D
FF_UNITS = 2 * (D // NC)


def sp_feed_forward(sp, k, w1, w2):
    first = k.block0["sp"]
    k.block0["sp"] += FF_GROUPS * FF_UNITS * BLOCKS
    w2_groups = w2.rearrange("(q kt p) n -> p q kt n", kt=KT, p=P)
    w1_rows = w1.rearrange("(kt p) n -> p kt n", p=P)
    with sp.Fori(0, FF_GROUPS) as q:
        b0 = q * (FF_UNITS * BLOCKS) + first
        for u in range(FF_UNITS):
            for j in range(BLOCKS):
                rows = slice(KB * j, KB * (j + 1))
                if u < 4:
                    src = w1_rows[:, rows, bass.ds(q * D + u * NC, NC)]
                else:
                    src = w2_groups[:, bass.ds(q, 1), rows, (u - 4) * NC:(u - 3) * NC].rearrange("p q kt n -> p (q kt) n")
                sp.wait_ge(k.lo_ready, b0 + (u * BLOCKS + j + 1))
                sp.dma_start(k.raw[:, j], src).then_inc(k.raw_ready[j], 16)


def pe_feed_forward(pe, k, layer):
    first = k.block0["pe"]
    k.block0["pe"] += FF_GROUPS * FF_UNITS * BLOCKS
    done = layer * FF_GROUPS * 4

    def turn(n, u):
        pe.wait_ge(k.relu2_ready, n + (u + 3))
        pe.wait_ge(k.f_lo_ready, n + (u + 1))
        for kt in range(4):
            bank = k.ps[:, 2 * (u % 2) + kt // 2, :].rearrange("p (a s) -> p a s", a=2)
            for t in range(TT):
                last = k.nc.tensor.transpose(bank[:, kt % 2, t * P:(t + 1) * P],
                                             k.relu2[:, u % 2, t, kt * P:(kt + 1) * P], k.ident)
        last.then_inc(k.f_turned, 1)

    with pe.Fori(0, FF_GROUPS) as q:
        b0 = q * (FF_UNITS * BLOCKS) + first
        n = q * 4 + done
        for u in range(FF_UNITS):
            hi, lo = (k.a_hi, k.a_lo) if u < 4 else (k.f_hi, k.f_lo)
            for j in range(BLOCKS):
                if u == 4 and j == 0:
                    pe.wait_ge(k.f_lo_ready, n + 5)
                if j == 4 and 1 <= u <= 4:
                    turn(n, u - 1)
                if u == 4 and j == 6:
                    pe.wait_ge(k.f_lo_ready, n + 6)
                pe_block(pe, k, b0, u * BLOCKS + j, hi, lo)


def turned_unit(k, u):
    return k.ps[:, 2 * (u % 2):2 * (u % 2) + 2, :].rearrange("p b (a s) -> p (b a) s", a=2)


def act_feed_forward(act, k, layer):
    first = k.block0["act"]
    k.block0["act"] += FF_GROUPS * FF_UNITS * BLOCKS
    done = layer * FF_GROUPS * 4
    with act.Fori(0, FF_GROUPS) as q:
        b0 = q * (FF_UNITS * BLOCKS) + first
        n = q * 4 + done
        for u in range(FF_UNITS):
            for j in range(4, 8):
                act_split(act, k, b0, u * BLOCKS + j)
            if 1 <= u <= 4:
                act.wait_ge(k.f_turned, n + (u + 2))
                k.nc.scalar.activation(k.f_hi[:, 4 * (u - 1):4 * u, :], turned_unit(k, u - 1),
                                       ACT.Copy).then_inc(k.f_hi_ready, 1)
            for j in range(8, 12):
                act_split(act, k, b0, u * BLOCKS + j)
            if u < 4:
                wait_unit(act, k, b0, u)
                act.wait_ge(k.relu2_ready, n + (u + 1))
                k.nc.scalar.activation(k.relu[:, u % 2], k.ps_unit[:, u % 2], ACT.Relu).then_inc(k.evacuated, BLOCKS)


def pool_feed_forward(pool, k, layer):
    first = k.block0["pool"]
    k.block0["pool"] += FF_GROUPS * FF_UNITS * BLOCKS
    done = layer * FF_GROUPS * 4
    with pool.Fori(0, FF_GROUPS) as q:
        b0 = q * (FF_UNITS * BLOCKS) + first
        n = q * 4 + done
        for u in range(4):
            pool.wait_ge(k.evacuated, b0 + (u + 3) * BLOCKS)
            pool.wait_ge(k.f_turned, n + (u + 1))
            k.nc.gpsimd.tensor_tensor(k.relu2[:, u % 2], k.relu[:, u % 2], k.relu[:, u % 2],
                                      ALU.mult).then_inc(k.relu2_ready, 1)


def dve_feed_forward(dve, k, layer):
    first = k.block0["dve"]
    k.block0["dve"] += FF_GROUPS * FF_UNITS * BLOCKS
    done = layer * FF_GROUPS * 4
    with dve.Fori(0, FF_GROUPS) as q:
        b0 = q * (FF_UNITS * BLOCKS) + first
        n = q * 4 + done
        for u in range(FF_UNITS):
            for j in range(4, 8):
                dve_split(dve, k, b0, u * BLOCKS + j)
            if 1 <= u <= 4:
                dve.wait_ge(k.f_hi_ready, n + u)
                part = slice(4 * (u - 1), 4 * u)
                k.nc.vector.tensor_tensor(k.f_lo[:, part, :], turned_unit(k, u - 1), k.f_hi[:, part, :].bitcast(F32),
                                          ALU.subtract).then_inc(k.f_lo_ready, 1)
            for j in range(8, 12):
                dve_split(dve, k, b0, u * BLOCKS + j)
            if u >= 4:
                residual(dve, k, b0, u, u - 4)


CA, CG = 0, CONV_C
HQ, HF, HI, HG = (2 * CONV_C + n * HW for n in range(4))
RQ, RK, RV, RG = (2 * CONV_C + (4 + n) * HW for n in range(4))
LEVELS = 7
LOG_LB_MAX = math.log(1 - 1e-6)
LOG_1M_LB_MIN = math.log(1e-6)
CONV_T = CONV_W - 1 + SEQ


def first_mix_tile(k):
    def tile(kt, t):
        at = P * kt if kt < 4 else HQ + P * (kt - 4) if kt < 10 else RQ + P * (kt - 10)
        return k.proj[:, t, at:at + P]
    return tile


def first_buffers(k):
    K = 1024
    w, t1, t2 = k.scratch, k.t1, k.t2
    k.conv_rows = k.sb("conv_rows", t1, [CONV_W + 1, CONV_C])
    k.conv_gain = k.sb("conv_gain", t1 + 2 * K, [P, CONV_C])
    k.conv_shift = k.sb("conv_shift", t1 + 4 * K, [P, CONV_C])
    k.conv_u = k.sb("conv_u", t1 + 6 * K, [P, CONV_C // P, CONV_T])
    k.conv_y = k.sb("conv_y", t1 + 11 * K, [P, CONV_C // P, SEQ])
    k.conv_w = k.sb("conv_w", t1 + 15 * K, [P, CONV_C // P, CONV_W + 1])
    n = HEADS * SEQ
    k.h_cum, k.h_k, k.h_q, k.h_d0, k.h_d1 = (k.sb(f"h_{x}", w + 4 * n * a, [P, n])
                                             for a, x in enumerate(("cum", "k", "q", "d0", "d1")))
    k.h_s = k.sb("h_s", t2, [P, 3 * HEADS, P])
    k.h_lf = k.sb("h_lf", t2, [P, n])
    k.h_mask = k.sb("h_mask", t2 + 9 * K, [P, LEVELS, P])
    k.h_gain = k.sb("h_gain", t2 + 12 * K + 512, [P, HW])
    k.h_lb_rows = k.sb("h_lb_rows", t2 + 6 * K, [DEPTH, HW])
    k.h_lb = k.sb_small("h_lb", [P, HEADS, DEPTH])
    k.h_log = k.sb_small("h_log", [P, 4, HEADS])
    k.h_ms = k.sb_small("h_ms", [P, TT * HEADS])
    k.conv_stats = k.sb_small("conv_stats", [P, TT, 6])
    k.conv_mv = k.sb_small("conv_mv", [P, TT, 2])
    k.conv_rstd = k.sb_small("conv_rstd", [P, TT])
    k.r_qk = k.sb("r_qk", w, [P, 2, TT, HW])
    k.r_t = k.sb("r_t", w + 12 * K, [P, 2, HEADS, SEQ])
    k.r_work = k.sb("r_work", w + 24 * K, [P, 2, TT, HEADS, HALF])
    k.r_s = k.sb("r_s", w, [P, HEADS, 3 * P])
    k.r_mask = k.sb("r_mask", t2, [P, HEADS, SEQ])
    k.r_gain = k.sb("r_gain", t2 + 6 * K, [P, HW])
    k.r_shift = k.sb("r_shift", t2 + 9 * K, [P, HW])
    k.r_stats = k.sb_small("r_stats", [P, TT * HEADS, 6])
    k.r_mv = k.sb_small("r_mv", [P, TT * HEADS, 2])
    k.r_rstd = k.sb_small("r_rstd", [P, TT * HEADS])
    count = k.count
    k.conv_pad, k.conv_gate, k.h_gate, k.h_qsilu, k.r_gate = count("conv_pad", "conv_gate", "h_gate", "h_qsilu", "r_gate")
    k.conv_weights, k.conv_gated, k.conv_turned, k.conv_back, k.conv_var = \
        count("conv_weights", "conv_gated", "conv_turned", "conv_back", "conv_var")
    k.conv_root, k.conv_linear, k.conv_done, k.h_fT, k.h_f_read = \
        count("conv_root", "conv_linear", "conv_done", "h_fT", "h_f_read")
    k.h_kx, k.h_key, k.h_qT, k.h_query, k.h_cumulated = count("h_kx", "h_key", "h_qT", "h_query", "h_cumulated")
    k.h_o, k.h_square, k.h_msq, k.h_root, k.h_gated = count("h_o", "h_square", "h_msq", "h_root", "h_gated")
    k.r_roped, k.r_rope_free, k.r_qT, k.r_q, k.r_kT = count("r_roped", "r_rope_free", "r_qT", "r_q", "r_kT")
    k.r_k, k.r_o, k.r_var, k.r_root, k.r_key_roped = count("r_k", "r_o", "r_var", "r_root", "r_key_roped")
    k.conv_tap, k.h_rel, k.h_decay, k.h_factors, k.h_scores = count("conv_tap", "h_rel", "h_decay", "h_factors", "h_scores")
    k.h_score_kept, k.r_scores, k.r_kept, k.conv_rows_in, k.conv_norm_in = \
        count("h_score_kept", "r_scores", "r_kept", "conv_rows_in", "conv_norm_in")
    k.h_gain_in, k.h_mask_in, k.r_rows_in, k.h_lb_in, k.h_softplus = \
        count("h_gain_in", "h_mask_in", "r_rows_in", "h_lb_in", "h_softplus")
    k.h_softplus2, k.h_delta, k.h_lb_log, k.h_lbT = count("h_softplus2", "h_delta", "h_lb_log", "h_lbT")


def head_view(ap):
    return ap.rearrange("p (h s) -> p h s", h=HEADS)


def dve_positions(dve, k):
    v = k.nc.vector

    def step(ins):
        ins.then_inc(*k.dve_step.up())
        dve.wait_ge(*k.dve_step.now())

    dve.wait_ge(k.pos_in.sem, 32)
    step(v.tensor_copy(k.pos_f[:], k.pos_i[:]))
    for t in range(TT):
        last = v.tensor_scalar(k.cos[:, t, :], k.inv_freq[:], k.pos_f[:, t:t + 1], None, ALU.mult)
    step(last)
    near = 1.5 * 2.0 ** 23
    step(v.tensor_scalar(k.turns[:], k.cos[:], 1 / (2 * math.pi), None, ALU.mult))
    step(v.tensor_scalar(k.turns[:], k.turns[:], near, None, ALU.add))
    step(v.tensor_scalar(k.turns[:], k.turns[:], near, None, ALU.subtract))
    first, second = 6.28125, 2029 / 2.0 ** 20
    for part in (first, second, 2 * math.pi - first - second):
        step(v.scalar_tensor_tensor(k.cos[:], k.turns[:], -part, k.cos[:], ALU.mult, ALU.add))
    pi = 3.1415925
    step(v.tensor_scalar(k.sin[:], k.cos[:], pi, -pi, ALU.min, ALU.max))
    step(v.tensor_scalar(k.cos[:], k.cos[:], math.pi / 2, None, ALU.add))
    step(v.tensor_scalar(k.turns[:], k.cos[:], math.pi, -2 * math.pi, ALU.is_gt, ALU.mult))
    step(v.tensor_tensor(k.cos[:], k.cos[:], k.turns[:], ALU.add))
    v.tensor_scalar(k.cos[:], k.cos[:], pi, -pi, ALU.min, ALU.max).then_inc(*k.angles.up())


def act_positions(act, k):
    act.wait_ge(*k.angles.next("act"))
    k.nc.scalar.activation(k.sin[:], k.sin[:], ACT.Sin)
    k.nc.scalar.activation(k.cos[:], k.cos[:], ACT.Sin).then_inc(*k.rotary.up())


def pool_first_rows(pool, k, l):
    d = k.dram
    with k.nc.allow_non_contiguous_dma(reason="short rows"):
        pool.dma_start(k.conv_rows[0:CONV_W, :], d["w_dw"][l]).then_inc(*k.conv_rows_in.up(16))
        pool.dma_start(k.conv_rows[CONV_W:CONV_W + 1, :], d["b_dw"][l:l + 1, :]).then_inc(*k.conv_rows_in.up(16))
        pool.dma_start(k.conv_gain[:], d["conv_ln_g"][l].partition_broadcast(P)).then_inc(*k.conv_norm_in.up(16))
        pool.dma_start(k.conv_shift[:], d["conv_ln_b"][l].partition_broadcast(P)).then_inc(*k.conv_norm_in.up(16))
        pool.dma_start(k.h_mask[:], d["c_levels"].rearrange("p (n t) -> p n t", n=LEVELS)).then_inc(*k.h_mask_in.up(16))
        pool.dma_start(k.h_gain[:], d["hgrn_norm_g"][l].partition_broadcast(P)).then_inc(*k.h_gain_in.up(16))
        if l:
            pool.dma_start(k.h_lb_rows[:], d["hgrn_lb"]).then_inc(*k.h_lb_in.up(16))
    k.nc.gpsimd.memset(k.conv_u[:, :, 0:CONV_W - 1], 0.0).then_inc(*k.conv_pad.up())


def act_first_gates(act, k):
    a = k.nc.scalar
    act.wait_ge(k.evacuated, 2 * BLOCKS + k.block0["act"])
    a.activation(k.proj[:, :, CG:CG + CONV_C], k.proj[:, :, CG:CG + CONV_C], ACT.Sigmoid).then_inc(*k.conv_gate.up())
    a.activation(k.proj[:, :, HG:HG + HW], k.proj[:, :, HG:HG + HW], ACT.Sigmoid).then_inc(*k.h_gate.up())
    a.activation(k.proj[:, :, HQ:HQ + HW], k.proj[:, :, HQ:HQ + HW], ACT.Silu).then_inc(*k.h_qsilu.up())
    a.activation(k.proj[:, :, RG:RG + HW], k.proj[:, :, RG:RG + HW], ACT.Silu).then_inc(*k.r_gate.up())


def pe_conv(pe, k):
    pe.wait_ge(*k.conv_rows_in.next("pe", 32))
    for c in range(4):
        last = k.nc.tensor.transpose(k.ps[:, 0, c * 32:(c + 1) * 32], k.conv_rows[:, c * P:(c + 1) * P],
                                     k.ident[0:CONV_W + 1, 0:CONV_W + 1])
    last.then_inc(*k.conv_weights.up())
    pe.wait_ge(*k.conv_gated.next("pe"))
    for c in range(4):
        for t in range(TT):
            last = k.nc.tensor.transpose(k.ps[:, 1 + c // 2, (c % 2) * SEQ + t * P:(c % 2) * SEQ + (t + 1) * P],
                                         k.proj[:, t, CA + c * P:CA + (c + 1) * P], k.ident)
    last.then_inc(*k.conv_turned.up())
    pe.wait_ge(*k.conv_tap.next("pe", 4 * CONV_W))
    for t in range(TT):
        for c in range(4):
            last = k.nc.tensor.transpose(k.ps[:, 1 + t, c * P:(c + 1) * P], k.conv_y[:, c, t * P:(t + 1) * P], k.ident)
    last.then_inc(*k.conv_back.up())


def dve_conv(dve, k):
    v = k.nc.vector
    ca = k.proj[:, :, CA:CA + CONV_C]
    dve.wait_ge(*k.conv_gate.next("dve"))
    v.tensor_tensor(ca, ca, k.proj[:, :, CG:CG + CONV_C], ALU.mult).then_inc(*k.conv_gated.up())
    dve.wait_ge(*k.conv_weights.next("dve"))
    v.tensor_copy(k.conv_w[:], k.ps[:, 0, 0:P].rearrange("p (c k) -> p c k", c=4)).then_inc(*k.dve_step.up())
    dve.wait_ge(*k.conv_turned.next("dve"))
    v.tensor_copy(k.conv_u[:, :, CONV_W - 1:CONV_T],
                  k.ps[:, 1:3, :].rearrange("p b (a s) -> p (b a) s", a=2)).then_inc(*k.dve_step.up())
    dve.wait_ge(*k.conv_pad.next("dve"))
    dve.wait_ge(*k.dve_step.now())
    sem, done = k.conv_tap.now()
    for tap in range(CONV_W):
        for c in range(4):
            u, y = k.conv_u[:, c, tap:tap + SEQ], k.conv_y[:, c, :]
            if tap == 0:
                ins = v.tensor_scalar(y, u, k.conv_w[:, c, 0:1], k.conv_w[:, c, CONV_W:CONV_W + 1], ALU.mult, ALU.add)
            else:
                dve.wait_ge(sem, done + 4 * (tap - 1) + c + 1)
                ins = v.scalar_tensor_tensor(y, u, k.conv_w[:, c, tap:tap + 1], y, ALU.mult, ALU.add)
            ins.then_inc(*k.conv_tap.up())
    dve.wait_ge(*k.conv_back.next("dve"))
    for t in range(TT):
        v.bn_stats(k.conv_stats[:, t, :], k.ps[:, 1 + t, :]).then_inc(*k.dve_step.up())
    dve.wait_ge(*k.dve_step.now())
    for t in range(TT):
        last = v.bn_aggr(k.conv_mv[:, t, :], k.conv_stats[:, t, :])
    last.then_inc(*k.conv_var.up())
    dve.wait_ge(*k.conv_norm_in.next("dve", 32))
    dve.wait_ge(*k.conv_var.now())
    for t in range(TT):
        v.scalar_tensor_tensor(k.proj[:, t, CA:CA + CONV_C], k.ps[:, 1 + t, :], k.conv_mv[:, t, 0:1], k.conv_gain[:],
                               ALU.subtract, ALU.mult).then_inc(*k.dve_step.up())
    dve.wait_ge(*k.conv_root.next("dve"))
    v.reciprocal(k.conv_rstd[:], k.conv_rstd[:]).then_inc(*k.dve_step.up())
    dve.wait_ge(*k.dve_step.now())
    for t in range(TT):
        y = k.proj[:, t, CA:CA + CONV_C]
        last = v.scalar_tensor_tensor(y, y, k.conv_rstd[:, t:t + 1], k.conv_shift[:], ALU.mult, ALU.add)
    last.then_inc(*k.conv_linear.up())


def act_conv_root(act, k):
    act.wait_ge(*k.conv_var.next("act"))
    k.nc.scalar.activation(k.conv_rstd[:], k.conv_mv[:, :, 1], ACT.Sqrt, bias=k.eps[:, 0:1]).then_inc(*k.conv_root.up())


def act_conv_silu(act, k):
    act.wait_ge(*k.conv_linear.next("act"))
    ca = k.proj[:, :, CA:CA + CONV_C]
    k.nc.scalar.activation(ca, ca, ACT.Silu).then_inc(*k.conv_done.up())



def pe_hgrn(pe, k, l):
    tensor = k.nc.tensor

    def turn(at):
        for h in range(HEADS):
            for t in range(TT):
                last = tensor.transpose(k.ps[:, h // 2, (h % 2) * SEQ + t * P:(h % 2) * SEQ + (t + 1) * P],
                                        k.proj[:, t, at + h * P:at + (h + 1) * P], k.ident)
        return last

    pe.wait_ge(*k.conv_linear.next("pe"))
    turn(HF).then_inc(*k.h_fT.up())
    pe.wait_ge(*k.h_kx.next("pe"))
    if l:
        pe.wait_ge(*k.h_lb_in.next("pe", 16))
        for h in range(HEADS):
            last = tensor.transpose(k.ps[:, 3, h * DEPTH:(h + 1) * DEPTH], k.h_lb_rows[:, h * P:(h + 1) * P],
                                    k.ident[0:DEPTH, 0:DEPTH])
        last.then_inc(*k.h_lbT.up())
    pe.wait_ge(*k.h_qsilu.next("pe"))
    turn(HQ).then_inc(*k.h_qT.up())

    pe.wait_ge(*k.h_query.next("pe"))
    pe.wait_ge(*k.h_key.next("pe"))
    scores = k.ps[:, 0:3, :].rearrange("p b (a t) -> p (b a) t", a=4)
    for level in range(-1, LEVELS + 1):
        if level < 0:
            left, right = k.h_k, k.h_q
        else:
            left = right = (k.h_d0, k.h_d1)[level % 2]
            pe.wait_ge(*k.h_factors.next("pe"))
            pe.wait_ge(*k.h_score_kept.next("pe"))
        for n in range(HEADS if level == LEVELS else 2 * HEADS):
            if level == LEVELS:
                s0, t0 = n * SEQ, n * SEQ + P
            else:
                s0 = t0 = n * P
            last = tensor.matmul(scores[:, n, :], left[:, s0:s0 + P], right[:, t0:t0 + P], start=True, stop=True)
        last.then_inc(*k.h_scores.up())
    pe.wait_ge(*k.h_score_kept.next("pe"))
    for t in range(TT):
        for h in range(HEADS):
            o = scores[:, t * HEADS + h, :]
            v = slice(HI + h * HD, HI + (h + 1) * HD)
            last = tensor.matmul(o, k.h_s[:, TT * h + t, :], k.proj[:, t, v], start=True, stop=t == 0)
            if t:
                last = tensor.matmul(o, k.h_s[:, TT * HEADS + h, :], k.proj[:, 0, v], start=False, stop=True)
    last.then_inc(*k.h_o.up())


def act_hgrn(act, k, l):
    a = k.nc.scalar

    def step(ins):
        ins.then_inc(*k.act_step.up())
        act.wait_ge(*k.act_step.now())

    act.wait_ge(*k.h_f_read.next("act"))
    step(a.activation(k.h_d0[:].rearrange("p (b s) -> p b s", b=3), k.ps[:, 0:3, :], ACT.Abs))
    step(a.activation(k.h_d0[:], k.h_d0[:], ACT.Exp, scale=-1.0))
    a.activation(k.h_d0[:], k.h_d0[:], ACT.Ln, bias=1.0).then_inc(*k.h_softplus.up())
    if l:
        act.wait_ge(*k.h_lb_log.next("act"))
        step(a.activation(k.h_log[:, 3, :], k.h_log[:, 2, :], ACT.Abs))
        step(a.activation(k.h_log[:, 3, :], k.h_log[:, 3, :], ACT.Exp, scale=-1.0))
        a.activation(k.h_log[:, 3, :], k.h_log[:, 3, :], ACT.Ln, bias=1.0).then_inc(*k.h_softplus.up())
    act.wait_ge(*k.h_kx.next("act"))
    if l == 0:
        a.activation(k.h_k[:], k.h_k[:], ACT.Exp).then_inc(*k.h_key.up())
    else:
        act.wait_ge(*k.h_delta.next("act"))
        for h in range(HEADS):
            last = a.activation(head_view(k.h_k[:])[:, h, :], head_view(k.h_k[:])[:, h, :], ACT.Exp,
                                bias=k.h_log[:, 1, h:h + 1])
        last.then_inc(*k.h_key.up())
        step(a.activation(k.h_d1[:], k.h_d0[:], ACT.Abs))
        step(a.activation(k.h_d1[:], k.h_d1[:], ACT.Exp, scale=-1.0))
        a.activation(k.h_d1[:], k.h_d1[:], ACT.Ln, bias=1.0).then_inc(*k.h_softplus2.up())
    for level in range(LEVELS + 1):
        d = (k.h_d0, k.h_d1)[level % 2]
        act.wait_ge(*k.h_rel.next("act"))
        a.activation(d[:], d[:], ACT.Exp).then_inc(*k.h_decay.up())
    act.wait_ge(*k.h_o.next("act"))
    a.activation(k.h_d0[:].rearrange("p (b s) -> p b s", b=3), k.ps[:, 0:3, :], ACT.Square).then_inc(*k.h_square.up())
    act.wait_ge(*k.h_msq.next("act"))
    a.activation(k.h_ms[:], k.h_ms[:], ACT.Sqrt, scale=1.0 / HD, bias=k.eps[:, 0:1]).then_inc(*k.h_root.up())


def pool_hgrn(pool, k):
    g = k.nc.gpsimd
    hg = k.proj[:, :, HG:HG + HW]
    pool.wait_ge(*k.h_gain_in.next("pool", 16))
    pool.wait_ge(*k.h_gate.next("pool"))
    g.tensor_tensor(hg, hg, k.h_gain[:].unsqueeze(1).to_broadcast([P, TT, HW]), ALU.mult).then_inc(*k.h_gated.up())
    pool.wait_ge(*k.h_cumulated.next("pool"))
    for level in range(LEVELS + 1):
        half = 128 if level == LEVELS else 64 >> level
        blocks = HEADS * SEQ // (2 * half)
        if level >= 2:
            pool.wait_ge(*k.h_scores.next("pool", 2 if level == 2 else 1))
        c = k.h_cum[:].rearrange("p (b x s) -> p b x s", b=blocks, x=2)
        d = (k.h_d0, k.h_d1)[level % 2][:].rearrange("p (b x s) -> p b x s", b=blocks, x=2)
        middle = c[:, :, 0, half - 1:half].to_broadcast([P, blocks, half])
        g.tensor_tensor(d[:, :, 0, :], middle, c[:, :, 0, :], ALU.subtract)
        if level == LEVELS:
            last = g.tensor_copy(d[:, :, 1, :], c[:, :, 1, :])
        else:
            last = g.tensor_tensor(d[:, :, 1, :], c[:, :, 1, :], middle, ALU.subtract)
        last.then_inc(*k.h_rel.up())
    k.h_scores.next("pool", 2)


def dve_hgrn(dve, k, l):
    v = k.nc.vector

    def step(ins):
        ins.then_inc(*k.dve_step.up())
        dve.wait_ge(*k.dve_step.now())

    f = k.ps[:, 0:3, :].rearrange("p b s -> p (b s)")
    dve.wait_ge(*k.h_fT.next("dve"))
    v.tensor_scalar(k.h_lf[:], f, 0.0, None, ALU.min)
    v.tensor_scalar(k.h_k[:], f, 0.0, None, ALU.max).then_inc(*k.h_f_read.up())
    dve.wait_ge(*k.h_f_read.now())
    dve.wait_ge(*k.h_softplus.next("dve"))
    step(v.tensor_tensor(k.h_lf[:], k.h_lf[:], k.h_d0[:], ALU.subtract))
    v.scalar_tensor_tensor(k.h_k[:], k.h_k[:], -1.0, k.h_d0[:], ALU.mult, ALU.subtract).then_inc(*k.h_kx.up())
    if l:
        log_lb, log_1m, delta, work = (k.h_log[:, n, :] for n in range(4))
        dve.wait_ge(*k.h_lbT.next("dve"))
        step(v.tensor_copy(k.h_lb[:], k.ps[:, 3, 0:HEADS * DEPTH].rearrange("p (h n) -> p h n", h=HEADS)))
        v.tensor_tensor(delta, k.h_lb[:, :, 1], k.h_lb[:, :, 0], ALU.subtract).then_inc(*k.h_lb_log.up())
        dve.wait_ge(*k.h_softplus.next("dve"))
        v.scalar_tensor_tensor(log_lb, delta, 0.0, work, ALU.min, ALU.subtract)
        step(v.tensor_scalar(log_1m, delta, 0.0, -1.0, ALU.max, ALU.mult))
        step(v.tensor_tensor(log_1m, log_1m, work, ALU.subtract))
        v.tensor_scalar(log_lb, log_lb, LOG_LB_MAX, None, ALU.min)
        step(v.tensor_scalar(log_1m, log_1m, LOG_1M_LB_MIN, None, ALU.max))
        step(v.tensor_tensor(delta, log_1m, log_lb, ALU.subtract))
        for h in range(HEADS):
            last = v.tensor_scalar(head_view(k.h_d0[:])[:, h, :], head_view(k.h_lf[:])[:, h, :], delta[:, h:h + 1], None,
                                   ALU.add)
        last.then_inc(*k.h_delta.up())
        dve.wait_ge(*k.h_softplus2.next("dve"))
        step(v.tensor_scalar(k.h_d0[:], k.h_d0[:], 0.0, None, ALU.max))
        for h in range(HEADS):
            last = v.scalar_tensor_tensor(head_view(k.h_lf[:])[:, h, :], head_view(k.h_d1[:])[:, h, :],
                                          log_lb[:, h:h + 1], head_view(k.h_d0[:])[:, h, :], ALU.add, ALU.add)
        step(last)
    dve.wait_ge(*k.h_kx.now())
    v.memset(k.h_d0[:], 1.0).then_inc(*k.dve_step.up())
    dve.wait_ge(*k.dve_step.now())
    step(v.memset(k.h_d0[:].rearrange("p (n s) -> p n s", s=P)[:, :, 0:1], 0.0))
    v.tensor_tensor_scan(k.h_cum[:], k.h_d0[:], k.h_lf[:], 0.0, ALU.mult, ALU.add).then_inc(*k.h_cumulated.up())
    dve.wait_ge(*k.h_qT.next("dve"))
    v.tensor_copy(k.h_q[:], f).then_inc(*k.h_query.up())
    dve.wait_ge(*k.h_query.now())
    dve.wait_ge(*k.h_key.next("dve"))
    dve.wait_ge(*k.h_mask_in.next("dve", 16))

    scores = k.ps[:, 0:3, :].rearrange("p b (a t) -> p (b a) t", a=4)
    dve.wait_ge(*k.h_cumulated.now())

    def factors(level):
        half = 128 if level == LEVELS else 64 >> level
        d, q, key = (x[:].rearrange("p (b x s) -> p b x s", x=2, s=half)
                     for x in ((k.h_d0, k.h_d1)[level % 2], k.h_q, k.h_k))
        dve.wait_ge(*k.h_decay.next("dve"))
        v.tensor_tensor(d[:, :, 0, :], d[:, :, 0, :], key[:, :, 0, :], ALU.mult)
        v.tensor_tensor(d[:, :, 1, :], d[:, :, 1, :], q[:, :, 1, :], ALU.mult).then_inc(*k.h_factors.up())

    def keep(level):
        dve.wait_ge(*k.h_scores.next("dve"))
        kept = k.h_s[:, 0:2 * HEADS, :]
        if level < 0:
            ins = v.tensor_tensor(kept, scores, k.ident.unsqueeze(1).to_broadcast([P, 2 * HEADS, P]), ALU.mult)
        elif level == LEVELS:
            ins = v.tensor_copy(k.h_s[:, 2 * HEADS:, :], scores[:, 0:HEADS, :])
        else:
            mask = k.h_mask[:, level:level + 1, :].to_broadcast([P, 2 * HEADS, P])
            ins = v.copy_predicated(kept, mask.bitcast(I32), scores)
        ins.then_inc(*k.h_score_kept.up())
        dve.wait_ge(*k.h_score_kept.now())

    for level in range(-1, LEVELS):
        factors(level + 1)
        keep(level)
    keep(LEVELS)
    dve.wait_ge(*k.h_square.next("dve"))
    v.tensor_reduce(k.h_ms[:], k.h_d0[:].rearrange("p (n e) -> p n e", e=HD), AX_X, ALU.add).then_inc(*k.h_msq.up())
    dve.wait_ge(*k.h_gated.next("dve"))
    y = k.proj[:, :, HQ:HQ + HW]
    step(v.tensor_tensor(y, k.ps[:, 0:3, :].rearrange("p b s -> p (b s)").rearrange("p (t n) -> p t n", t=TT),
                         k.proj[:, :, HG:HG + HW], ALU.mult))
    dve.wait_ge(*k.h_root.next("dve"))
    step(v.reciprocal(k.h_ms[:], k.h_ms[:]))
    for t in range(TT):
        yt = head_view(k.proj[:, t, HQ:HQ + HW])
        last = v.tensor_tensor(yt, yt, k.h_ms[:, t * HEADS:(t + 1) * HEADS].unsqueeze(2).to_broadcast([P, HEADS, HD]),
                               ALU.mult)
    step(last)


def pool_retention_rows(pool, k, l):
    d = k.dram
    pool.wait_ge(*k.r_rope_free.next("pool"))
    pool.dma_start(k.r_mask[:], d["c_retention"].rearrange("p (h t) -> p h t", h=HEADS)).then_inc(*k.r_rows_in.up(16))
    pool.dma_start(k.r_gain[:], d["ret_gn_g"][l].partition_broadcast(P)).then_inc(*k.r_rows_in.up(16))
    pool.dma_start(k.r_shift[:], d["ret_gn_b"][l].partition_broadcast(P)).then_inc(*k.r_rows_in.up(16))


def rotate(eng, own, k, which, at, step):
    src = k.proj[:, :, at:at + HW].rearrange("p t (h x s) -> p t h x s", h=HEADS, x=2)
    dst = k.r_qk[:, which].rearrange("p t (h x s) -> p t h x s", h=HEADS, x=2)
    cos, sin = (x[:].unsqueeze(2).to_broadcast([P, TT, HEADS, HALF]) for x in (k.cos, k.sin))
    work = k.r_work[:, which]
    own.tensor_tensor(work, src[:, :, :, 1, :], sin, ALU.mult)
    step(own.tensor_tensor(dst[:, :, :, 0, :], src[:, :, :, 0, :], cos, ALU.mult))
    step(own.tensor_tensor(dst[:, :, :, 0, :], dst[:, :, :, 0, :], work, ALU.subtract))
    own.tensor_tensor(work, src[:, :, :, 1, :], cos, ALU.mult)
    step(own.tensor_tensor(dst[:, :, :, 1, :], src[:, :, :, 0, :], sin, ALU.mult))
    return own.tensor_tensor(dst[:, :, :, 1, :], dst[:, :, :, 1, :], work, ALU.add)


def pool_retention(pool, k):
    def step(ins):
        ins.then_inc(*k.pool_step.up())
        pool.wait_ge(*k.pool_step.now())
    pool.wait_ge(k.rotary.sem, 1)
    rotate(pool, k.nc.gpsimd, k, 1, RK, step).then_inc(*k.r_key_roped.up())


def pe_retention(pe, k):
    tensor = k.nc.tensor

    def turn(which):
        for h in range(HEADS):
            for t in range(TT):
                last = tensor.transpose(k.ps[:, h // 2, (h % 2) * SEQ + t * P:(h % 2) * SEQ + (t + 1) * P],
                                        k.r_qk[:, which, t, h * P:(h + 1) * P], k.ident)
        return last

    pe.wait_ge(*k.r_roped.next("pe"))
    turn(0).then_inc(*k.r_qT.up())
    pe.wait_ge(*k.r_key_roped.next("pe"))
    pe.wait_ge(*k.r_q.next("pe"))
    turn(1).then_inc(*k.r_kT.up())
    pe.wait_ge(*k.r_k.next("pe"))
    for h in range(HEADS):
        if h >= 4:
            pe.wait_ge(*k.r_kept.next("pe"))
        q, key = k.r_t[:, 0, h, :], k.r_t[:, 1, h, :]
        tensor.matmul(k.ps[:, h % 4, 0:SEQ], key[:, 0:P], q, start=True, stop=True)
        tensor.matmul(k.ps[:, h % 4, SEQ:3 * P], key[:, P:SEQ], q[:, P:SEQ], start=True, stop=True)\
            .then_inc(*k.r_scores.up())
    pe.wait_ge(*k.r_kept.next("pe", 4))
    o = k.ps[:, 0:3, :].rearrange("p b (a e) -> p (b a) e", a=4)
    for t in range(TT):
        for h in range(HEADS):
            v = slice(RV + h * HD, RV + (h + 1) * HD)
            last = tensor.matmul(o[:, t * HEADS + h, :], k.r_s[:, h, t * P:(t + 1) * P], k.proj[:, 0, v],
                                 start=True, stop=t == 0)
            if t:
                last = tensor.matmul(o[:, t * HEADS + h, :], k.r_s[:, h, SEQ:3 * P], k.proj[:, 1, v],
                                     start=False, stop=True)
    last.then_inc(*k.r_o.up())


def act_retention(act, k):
    act.wait_ge(*k.r_var.next("act"))
    k.nc.scalar.activation(k.r_rstd[:], k.r_mv[:, :, 1], ACT.Sqrt, bias=k.eps[:, 0:1]).then_inc(*k.r_root.up())


def dve_retention(dve, k):
    v = k.nc.vector

    def step(ins):
        ins.then_inc(*k.dve_step.up())
        dve.wait_ge(*k.dve_step.now())

    v.memset(k.r_rstd[:], 0.0).then_inc(*k.r_rope_free.up())
    dve.wait_ge(k.rotary.sem, 1)
    rotate(dve, v, k, 0, RQ, step).then_inc(*k.r_roped.up())
    turned = k.ps[:, 0:3, :].rearrange("p b (a s) -> p (b a) s", a=2)
    dve.wait_ge(*k.r_qT.next("dve"))
    v.tensor_copy(k.r_t[:, 0], turned).then_inc(*k.r_q.up())
    dve.wait_ge(*k.r_kT.next("dve"))
    v.tensor_copy(k.r_t[:, 1], turned).then_inc(*k.r_k.up())
    dve.wait_ge(*k.r_rows_in.next("dve", 48))
    for h in range(HEADS):
        dve.wait_ge(*k.r_scores.next("dve"))
        v.tensor_tensor(k.r_s[:, h, 0:SEQ], k.ps[:, h % 4, 0:SEQ], k.r_mask[:, h, :], ALU.mult)
        v.tensor_tensor(k.r_s[:, h, SEQ:3 * P], k.ps[:, h % 4, SEQ:3 * P], k.r_mask[:, h, 0:P], ALU.mult)\
            .then_inc(*k.r_kept.up())
    dve.wait_ge(*k.r_o.next("dve"))
    o = k.ps[:, 0:3, :].rearrange("p b (a e) -> p (b a) e", a=4)
    for n in range(TT * HEADS):
        last = v.bn_stats(k.r_stats[:, n, :], o[:, n, :])
    step(last)
    for n in range(TT * HEADS):
        last = v.bn_aggr(k.r_mv[:, n, :], k.r_stats[:, n, :])
    last.then_inc(*k.r_var.up())
    dve.wait_ge(*k.r_root.next("dve"))
    step(v.reciprocal(k.r_rstd[:], k.r_rstd[:]))
    for t in range(TT):
        for h in range(HEADS):
            n = t * HEADS + h
            last = v.tensor_scalar(k.proj[:, t, RQ + h * HD:RQ + (h + 1) * HD], o[:, n, :], k.r_mv[:, n, 0:1],
                                   k.r_rstd[:, n:n + 1], ALU.subtract, ALU.mult)
    step(last)
    y = k.proj[:, :, RQ:RQ + HW]
    step(v.tensor_tensor(y, y, k.r_gain[:].unsqueeze(1).to_broadcast([P, TT, HW]), ALU.mult))
    step(v.tensor_tensor(y, y, k.r_shift[:].unsqueeze(1).to_broadcast([P, TT, HW]), ALU.add))
    dve.wait_ge(*k.r_gate.next("dve"))
    dve.wait_ge(*k.conv_done.next("dve"))
    v.tensor_tensor(y, y, k.proj[:, :, RG:RG + HW], ALU.mult).then_inc(*k.turn_source.up(BLOCKS))


GRID = 64
GRID_ROWS = SEQ // GRID
RPB_ROWS, RPB_COLS = 15, 31
DELTAS = 2 * GRID_ROWS - 1
BIAS_COLS = HEADS * DELTAS
BIAS_PER_BANK = NC // BIAS_COLS
BIAS_ROUND = GRID // 2
MEM_HEADS = 4
MW = MEM_HEADS * HD
DN_TAPS = 5
DN_C = 3 * HW
DN_TILES = DN_C // P
DN_GATES = 4 * HEADS
DIRS = 2 * HEADS
DN_T = SEQ + DN_TAPS - 1
DIFF_MAPS = 2 * HEADS
DIFF_W = DIFF_MAPS * HD
LAM_INIT = 0.8 - 0.6 * math.exp(-0.3)
NQ, NK, NV, NG = (n * HW for n in range(4))
DQ, DK, DV, DG = (4 * HW + n * HW for n in range(4))
MQ, MG = 8 * HW, 8 * HW + MW
W_GATES, W_MEM = 8 * HW, 8 * HW + DN_GATES
OQ, OK, OV, OG = (n * DIFF_W for n in range(4))


def second_buffers(k):
    K = 1024
    w, t1 = k.scratch, k.t1
    end = (229368 - k.base) // 32 * 32
    k.kv = k.sb("kv", end - 16 * K, [P, TT, 4 * MW])
    free = end - 16 * K - t1
    k.normed_x = k.sb("normed_x", k.p0, [P, TT, D])
    k.mem = k.sb("mem", k.p0 + 16 * K, [P, TT, D])
    k.mem_normed = k.sb("mem_normed", k.p0 + 32 * K, [P, TT, D])
    k.gw_raw = k.sb("gw_raw", t1 + 8 * K, [P, KT, DN_GATES])
    k.gw_hi = k.sb("gw_hi", t1 + 10 * K, [P, KT, DN_GATES], F32R)
    k.gw_lo = k.sb("gw_lo", t1 + 12 * K, [P, KT, DN_GATES], F32R)
    k.small = k.mixer_small
    k.small_end = t1
    small = k.sb_small
    k.ss = small("ss", [P, TT, 2])
    k.head_ss = small("head_ss", [P, TT, 32])
    k.att_gain = small("att_gain", [P, 4])
    k.att_max = small("att_max", [P, 16, TT])
    k.att_sum = small("att_sum", [P, 16, TT])
    k.lam = small("lam", [P, 4])
    after_common = k.small
    k.dn_x = small("dn_x", [P, TT, DN_GATES])
    k.dn_sp = small("dn_sp", [P, TT, DN_GATES])
    k.dn_beta = small("dn_beta", [P, TT, DIRS])
    k.dn_g = small("dn_g", [P, TT, DIRS])
    k.dn_cum = small("dn_cum", [P, TT, DIRS])
    k.dn_total = small("dn_total", [P, TT, DIRS])
    k.dn_tail = small("dn_tail", [P, TT, DIRS])
    k.dn_ecum = small("dn_ecum", [P, TT, DIRS])
    k.dn_rate = small("dn_rate", [P, DIRS])
    k.dn_shift = small("dn_shift", [P, DIRS])
    k.dn_w = small("dn_w", [P, DN_TILES, DN_TAPS])
    k.dn_norm = small("dn_norm", [P, HD])
    k.dn_ms = small("dn_ms", [P, TT, HEADS])
    k.small = after_common
    k.o_subln = small("o_subln", [P, 2 * HD])
    k.o_mem_gain = small("o_mem_gain", [P, HD])
    k.o_ss = small("o_ss", [P, TT, HEADS])
    k.sq = k.sb("sq", w, [P, TT, 20, HD])
    k.na_t = k.sb("na_t", w, [P, 20, SEQ])
    k.na_bias = k.sb("na_bias", w + 20 * K, [P, HEADS, TT, GRID_ROWS, GRID])
    k.att_s = k.sb("att_s", t1, [P, 2, TT, SEQ])
    k.att_e = k.sb("att_e", t1 + 4 * K, [P, 2, TT, SEQ])
    k.att_t = k.sb("att_t", t1 + 8 * K, [P, 2, TT, SEQ])
    k.na_rows = k.sb("na_rows", t1 + 12 * K, [HEADS * RPB_ROWS, RPB_COLS])
    k.na_band = k.sb("na_band", t1 + 12 * K + 128, [RPB_COLS, GRID - 1 + P])
    k.na_window = k.sb("na_window", t1 + 12 * K + 896, [P, GRID])
    k.na_table = k.sb("na_table", t1 + 12 * K + 1152, [RPB_COLS, HEADS * RPB_ROWS])
    k.gain_rows = k.sb("gain_rows", t1 + 13 * K + 512, [4, HD])
    k.dn_u = k.sb("dn_u", w, [P, DN_TILES, DN_T])
    k.dn_rows = k.sb("dn_rows", w + 19 * K, [DN_TAPS, DN_C])
    k.dn_y = k.sb("dn_y", t1, [P, DN_TILES, SEQ])
    k.dn_sq = k.sb("dn_sq", w, [P, TT, 2 * HW])
    m = 6 * K
    k.dn_t = k.sb("dn_t", w, [P, 2, HEADS, SEQ])
    k.dn_rows_t = k.sb("dn_rows_t", w + 2 * m, [P, TT, DIRS, P])
    k.dn_inv = k.sb("dn_inv", w + 4 * m, [P, DIRS, P])
    k.dn_inv2 = k.sb("dn_inv2", t1 + 2 * m, [P, DIRS, P])
    k.dn_m = k.sb("dn_m", t1, [P, DIRS, P])
    k.dn_off = k.sb("dn_off", t1 + m, [P, DIRS, P])
    k.dn_dec = k.sb("dn_dec", t1, [P, DIRS, P])
    k.dn_rhs = k.sb("dn_rhs", t1 + m, [P, DIRS, P])
    k.dn_a = k.proj[:, :, NK:NK + 2 * HW].rearrange("p t (n i) -> p t n i", n=DIRS)
    k.dn_qk = k.proj[:, :, NG:NG + 2 * HW].rearrange("p t (n i) -> p t n i", n=DIRS)
    k.dn_v1 = k.sb("dn_v1", w + 4 * m, [P, DIRS, P])
    k.dn_vs = k.sb("dn_vs", t1, [P, DIRS, P])
    k.dn_state = k.sb("dn_state", t1 + m, [P, DIRS, P])
    k.dn_r = k.sb("dn_r", t1 + 2 * m, [P, DIRS, P])
    k.dn_qs = k.sb("dn_qs", t1, [P, DIRS, P])
    k.dn_v2 = k.sb("dn_v2", t1 + 2 * m, [P, DIRS, P])
    k.o_sq = k.sb("o_sq", w, [P, TT, 2 * DIFF_MAPS + 2 * MEM_HEADS, HD])
    k.o_t = k.sb("o_t", w, [P, 2 * DIFF_MAPS + 2 * MEM_HEADS, SEQ])
    k.o_tables = k.sb("o_tables", t1, [P, 2, 4, TT, HALF])
    k.o_work = k.sb("o_work", t1 + 4 * K, [P, 2, 2, DIFF_MAPS, HALF])
    k.o_lam_rows = k.sb("o_lam_rows", t1 + 4 * K, [P, 2, 2, HD])
    k.o_gain = k.sb("o_gain", t1 + 10 * K, [P, 4, HD])
    k.o_rope = k.sb("o_rope", t1 + 16 * K, [P, TT, 2, HALF])
    k.o_junk = k.sb("o_junk", t1 + 12 * K, [P, 2, TT, 2 * HD])
    assert free >= max(3 * m, 17 * K)
    count, later = k.count, k.later
    k.mem_in, k.gw_in, k.even_rows_in, k.dn_rows_in, k.dn_pairs_in = \
        count("mem_in", "gw_in", "even_rows_in", "dn_rows_in", "dn_pairs_in")
    k.o_rows_in, k.dn_tv, k.dn_vs_kept, k.dn_s_done, k.dn_s_kept = \
        count("o_rows_in", "dn_tv", "dn_vs_kept", "dn_s_done", "dn_s_kept")
    k.dn_ks, k.dn_ks_kept, k.dn_qs_done, k.dn_qs_kept, k.dn_tv2 = \
        count("dn_ks", "dn_ks_kept", "dn_qs_done", "dn_qs_kept", "dn_tv2")
    k.dn_v2_kept, k.dn_o, k.dn_o_kept, k.dn_osq, k.dn_oms = count("dn_v2_kept", "dn_o", "dn_o_kept", "dn_osq", "dn_oms")
    k.dn_oroot, = count("dn_oroot")
    k.square_sum, k.rms_root, k.gw_hi_ready, k.gw_lo_ready, k.gates_done = \
        later(DEPTH, k.conv_pad, k.conv_gate, k.h_gate, k.h_qsilu, k.r_gate)
    k.gates_kept, k.even_gated, k.att_squared, k.att_ss, k.att_root = \
        later(DEPTH, k.conv_weights, k.conv_gated, k.conv_turned, k.conv_back, k.conv_var)
    k.att_scaled, k.att_gainT, k.att_gained, k.na_tableT, k.na_table_kept = \
        later(DEPTH, k.conv_root, k.conv_linear, k.conv_done, k.h_fT, k.h_f_read)
    k.na_toeplitz, k.na_bias_kept, k.att_turned, k.att_turn_kept, k.at_s = \
        later(DEPTH, k.h_kx, k.h_key, k.h_qT, k.h_query, k.h_cumulated)
    k.at_max, k.at_e, k.at_t, k.at_c, k.at_o = \
        later(DEPTH, k.h_o, k.h_square, k.h_msq, k.h_root, k.h_gated)
    k.at_y, k.dn_wT, k.dn_w_kept, k.dn_turned, k.dn_turn_kept = \
        later(DEPTH, k.r_roped, k.r_rope_free, k.r_qT, k.r_q, k.r_kT)
    k.dn_tap, k.dn_silu, k.dn_back, k.dn_back_kept, k.dn_squared = \
        later(DEPTH, k.r_k, k.r_o, k.r_var, k.r_root, k.r_key_roped)
    k.dn_summed, = \
        later(DEPTH * 4 * CONV_W, k.conv_tap)
    k.dn_rooted, k.dn_scaled, k.dn_qkT = \
        later(DEPTH * (LEVELS + 1), k.h_rel, k.h_decay, k.h_factors)
    k.dn_qkT_kept, k.dn_abs = \
        later(DEPTH * (LEVELS + 2), k.h_scores, k.h_score_kept)
    k.dn_soft, k.dn_lnb = \
        later(DEPTH * HEADS, k.r_scores, k.r_kept)
    k.dn_beta_done, k.dn_g_done, k.dn_cums, k.dn_cum_kept, k.dn_tri_g = \
        count("dn_beta_done", "dn_g_done", "dn_cums", "dn_cum_kept", "dn_tri_g")
    k.dn_row, k.dn_rel, k.dn_decay, k.dn_decay_masked, k.dn_kk = \
        count("dn_row", "dn_rel", "dn_decay", "dn_decay_masked", "dn_kk")
    k.dn_qk_kept, k.dn_off_ready, k.dn_m_done, k.dn_m_kept, k.dn_up_done = \
        count("dn_qk_kept", "dn_off_ready", "dn_m_done", "dn_m_kept", "dn_up_done")
    k.dn_up_kept, k.dn_rows_kept, k.dn_pad, k.dn_it_done, k.dn_it_kept = \
        count("dn_up_kept", "dn_rows_kept", "dn_pad", "dn_it_done", "dn_it_kept")
    k.dn_e, = count("dn_e")
    k.o_tables_done, k.o_lam_sums, k.o_lam_exp, k.o_queries, k.o_keys = \
        later(1, k.dn_tv, k.dn_vs_kept, k.dn_s_done, k.dn_s_kept, k.dn_ks)
    k.o_gated, k.o_gate_done, k.o_turned, k.o_turn_kept, k.d_s = \
        later(1, k.dn_ks_kept, k.dn_qs_done, k.dn_qs_kept, k.dn_tv2, k.dn_v2_kept)
    k.d_max, k.d_e, k.d_a, k.d_t, k.d_c = \
        later(1, k.dn_o, k.dn_o_kept, k.dn_osq, k.dn_oms, k.dn_oroot)
    k.d_o, k.d_sq, k.d_y, k.o_root = count("d_o", "d_sq", "d_y", "o_root")
    return free


def act_rms(act, k, src, junk):
    for t in range(TT):
        last = k.nc.scalar.activation(junk[:, t, :], src[:, t, :], ACT.Square, accum_out=k.ss[:, t, 0:1])
    last.then_inc(*k.square_sum.up())
    act.wait_ge(*k.square_sum.now())
    k.nc.scalar.activation(k.ss[:, :, 1], k.ss[:, :, 0], ACT.Sqrt, scale=1.0 / D, bias=k.eps[:, 1:2])\
        .then_inc(*k.rms_root.up())


def dve_rms(dve, k, src, dst, gain):
    v = k.nc.vector
    dve.wait_ge(*k.rms_root.next("dve"))
    v.reciprocal(k.ss[:, :, 1], k.ss[:, :, 1]).then_inc(*k.dve_step.up())
    dve.wait_ge(*k.dve_step.now())
    for c in range(D // NC):
        cols = slice(c * NC, (c + 1) * NC)
        for t in range(TT):
            last = v.scalar_tensor_tensor(dst[:, t, cols], src[:, t, cols], k.ss[:, t, 1:2], gain[:, cols],
                                          ALU.mult, ALU.mult)
        last.then_inc(*k.turn_source.up(2))


def pe_gate_columns(pe, k):
    pe.wait_ge(*k.gw_lo_ready.next("pe"))
    for t in range(TT):
        tokens = slice(t * P, (t + 1) * P)
        out = k.ps[:, t, 0:DN_GATES]
        for kt in range(KT):
            k.nc.tensor.matmul(out, k.a_hi[:, kt, tokens], k.gw_hi[:, kt, :], start=kt == 0, stop=False)
            k.nc.tensor.matmul(out, k.a_hi[:, kt, tokens], k.gw_lo[:, kt, :], start=False, stop=False)
            last = k.nc.tensor.matmul(out, k.a_lo[:, kt, tokens], k.gw_hi[:, kt, :], start=False, stop=kt == KT - 1)
    last.then_inc(*k.gates_done.up())


def act_gate_columns(act, k):
    act.wait_ge(*k.gw_in.next("act", 16))
    k.nc.scalar.activation(k.gw_hi[:], k.gw_raw[:], ACT.Copy).then_inc(*k.gw_hi_ready.up())


def dve_gate_columns(dve, k):
    dve.wait_ge(*k.gw_hi_ready.next("dve"))
    k.nc.vector.tensor_tensor(k.gw_lo[:], k.gw_raw[:], k.gw_hi[:].bitcast(F32), ALU.subtract)\
        .then_inc(*k.gw_lo_ready.up())
    dve.wait_ge(*k.gates_done.next("dve"))
    k.nc.vector.tensor_copy(k.dn_x[:], k.ps[:, 0:TT, 0:DN_GATES]).then_inc(*k.gates_kept.up())


def act_take_memory(act, k):
    def take(b0, s, i):
        wait_unit(act, k, b0, s)
        k.nc.scalar.activation(k.kv[:, :, bass.ds(i * (2 * NC) + s * NC, NC)], k.ps_unit[:, s],
                               ACT.Copy).then_inc(k.evacuated, BLOCKS)
    return take


def pe_attention(pe, k, maps):
    tensor = k.nc.tensor

    def turn(n):
        pe.wait_ge(*k.at_e.next("pe"))
        if n >= 1:
            pe.wait_ge(*k.at_c.next("pe free"))
        for t in range(TT):
            for kt in range(TT):
                last = tensor.transpose(k.ps[:, 2, kt * SEQ + t * P:kt * SEQ + (t + 1) * P],
                                        k.att_e[:, n % 2, t, kt * P:(kt + 1) * P], k.ident)
        last.then_inc(*k.at_t.up())

    def weigh(n):
        pe.wait_ge(*k.at_c.next("pe"))
        if n >= 1:
            pe.wait_ge(*k.at_y.next("pe"))
        value = maps[n][3]
        for t in range(TT):
            for kt in range(TT):
                last = tensor.matmul(k.ps[:, 3, t * HD:(t + 1) * HD], k.att_t[:, n % 2, kt, t * P:(t + 1) * P], value(kt),
                                     start=kt == 0, stop=kt == TT - 1)
        last.then_inc(*k.at_o.up())

    for n in range(len(maps) + 2):
        if n < len(maps):
            if n >= 2:
                pe.wait_ge(*k.at_e.next("pe free"))
            q, key = maps[n][0], maps[n][1]
            for t in range(TT):
                last = tensor.matmul(k.ps[:, n % 2, t * SEQ:(t + 1) * SEQ], q[:, t * P:(t + 1) * P], key,
                                     start=True, stop=True)
            last.then_inc(*k.at_s.up())
        if 1 <= n <= len(maps):
            turn(n - 1)
        if n >= 2:
            weigh(n - 2)
    pe.wait_ge(*k.at_y.next("pe"))
    k.at_c.next("pe free")
    k.at_e.next("pe free", 2)


def act_attention(act, k, maps):
    a = k.nc.scalar

    def copy(n):
        act.wait_ge(*k.at_t.next("act"))
        if n >= 2:
            act.wait_ge(*k.at_o.next("act"))
        a.activation(k.att_t[:, n % 2], k.ps[:, 2, :].rearrange("p (a s) -> p a s", a=TT), ACT.Copy)\
            .then_inc(*k.at_c.up())

    for n, (_, _, bias, *_) in enumerate(maps):
        act.wait_ge(*k.at_max.next("act"))
        scores = k.att_s[:, n % 2] if bias is not None else k.ps[:, n % 2, :].rearrange("p (a s) -> p a s", a=TT)
        if n >= 2:
            act.wait_ge(*k.at_t.next("act free"))
        for t in range(TT):
            last = a.activation(k.att_e[:, n % 2, t, :], scores[:, t, :], ACT.Exp, bias=k.att_max[:, n, t:t + 1],
                                accum_out=k.att_sum[:, n, t:t + 1])
        last.then_inc(*k.at_e.up())
        if n >= 1:
            copy(n - 1)
    copy(len(maps) - 1)
    k.at_t.next("act free", 2)
    k.at_o.next("act", 2)


def dve_attention(dve, k, maps):
    v = k.nc.vector

    def output(n):
        _, _, _, _, gate, out = maps[n]
        dve.wait_ge(*k.at_e.next("dve"))
        v.reciprocal(k.att_sum[:, n, :], k.att_sum[:, n, :]).then_inc(*k.dve_step.up())
        dve.wait_ge(*k.at_o.next("dve"))
        dve.wait_ge(*k.dve_step.now())
        for t in range(TT):
            last = v.scalar_tensor_tensor(out(t), k.ps[:, 3, t * HD:(t + 1) * HD], k.att_sum[:, n, t:t + 1], gate(t),
                                          ALU.mult, ALU.mult)
        last.then_inc(*k.at_y.up())

    for n in range(len(maps) + 2):
        if n < len(maps):
            bias = maps[n][2]
            dve.wait_ge(*k.at_s.next("dve"))
            scores = k.ps[:, n % 2, :].rearrange("p (a s) -> p a s", a=TT)
            if bias is not None:
                v.tensor_tensor(k.att_s[:, n % 2], scores, bias, ALU.add).then_inc(*k.dve_step.up())
                scores = k.att_s[:, n % 2]
                dve.wait_ge(*k.dve_step.now())
            v.tensor_reduce(k.att_max[:, n, :], scores, AX_X, ALU.max, negate=True).then_inc(*k.at_max.up())
        if n >= 2:
            output(n - 2)


def even_maps(k):
    def cols(buffer, at):
        return lambda t: buffer[:, t, at:at + HD]

    maps = [(k.na_t[:, h, :], k.na_t[:, HEADS + h, :], k.na_bias[:, h].rearrange("p t r c -> p t (r c)"),
             cols(k.proj, NV + h * HD), cols(k.proj, NG + h * HD), cols(k.proj, NQ + h * HD)) for h in range(HEADS)]
    m0 = 2 * HEADS
    return maps + [(k.na_t[:, m0 + h, :], k.na_t[:, m0 + MEM_HEADS + h, :], None,
                    cols(k.kv, MW + h * HD), cols(k.proj, MG + h * HD), cols(k.proj, MQ + h * HD))
                   for h in range(MEM_HEADS)]


def pool_even_rows(pool, k):
    d = k.dram
    pool.wait_ge(*k.gates_done.next("pool"))
    for to, src in ((k.na_rows[:], d["na_rpb_2"][0].rearrange("h a b -> (h a) b")), (k.na_band[:], d["c_band"]),
                    (k.na_window[:], d["c_window"]), (k.gain_rows[0:1, :], d["na_q_norm_2"]),
                    (k.gain_rows[1:2, :], d["na_k_norm_2"]), (k.gain_rows[2:3, :], d["e_mem_q_norm_2"]),
                    (k.gain_rows[3:4, :], d["e_mem_k_norm_2"]),
                    (k.dn_rate[:], d["dn_a_log_2"].rearrange("a b c -> (a b c)").partition_broadcast(P)),
                    (k.dn_shift[:], d["dn_dt_bias_2"].rearrange("a b c -> (a b c)").partition_broadcast(P)),
                    (k.dn_norm[:], d["dn_out_norm_2"][0].partition_broadcast(P))):
        pool.dma_start(to, src).then_inc(*k.even_rows_in.up(16))


EVEN_ROWS = 10 * 16


def even_sources(k):
    def heads(buffer, at, n):
        return lambda t: buffer[:, t, at:at + n * HD].rearrange("p (n d) -> p n d", n=n)
    return [(0, 2 * HEADS, heads(k.proj, NQ, 2 * HEADS)), (2 * HEADS, MEM_HEADS, heads(k.proj, MQ, MEM_HEADS)),
            (2 * HEADS + MEM_HEADS, MEM_HEADS, heads(k.kv, 0, MEM_HEADS))]


def act_head_squares(act, k, sources, squares):
    for first, n, src in sources:
        for t in range(TT):
            last = k.nc.scalar.activation(squares[:, t, first:first + n, :], src(t), ACT.Square)
    last.then_inc(*k.att_squared.up())
    n = first + n
    act.wait_ge(*k.att_ss.next("act"))
    k.nc.scalar.activation(k.head_ss[:, :, 0:n], k.head_ss[:, :, 0:n], ACT.Sqrt, scale=1.0 / HD, bias=k.eps[:, 1:2])\
        .then_inc(*k.att_root.up())


def dve_head_norm(dve, k, sources, squares):
    v = k.nc.vector
    n = sources[-1][0] + sources[-1][1]
    dve.wait_ge(*k.att_squared.next("dve"))
    for t in range(TT):
        last = v.tensor_reduce(k.head_ss[:, t, 0:n], squares[:, t, 0:n, :], AX_X, ALU.add)
    last.then_inc(*k.att_ss.up())
    dve.wait_ge(*k.att_root.next("dve"))
    v.reciprocal(k.head_ss[:, :, 0:n], k.head_ss[:, :, 0:n]).then_inc(*k.dve_step.up())
    dve.wait_ge(*k.dve_step.now())
    for first, n, src in sources:
        for t in range(TT):
            last = v.tensor_tensor(src(t), src(t), k.head_ss[:, t, first:first + n].unsqueeze(2).to_broadcast([P, n, HD]),
                                   ALU.mult)
    last.then_inc(*k.att_scaled.up())


def act_even_attention(act, k):
    a = k.nc.scalar
    act.wait_ge(k.evacuated, 2 * BLOCKS + k.block0["act"])
    for at, n in ((NG, HW), (DG, HW), (MG, MW)):
        cols = k.proj[:, :, at:at + n]
        last = a.activation(cols, cols, ACT.Silu)
    last.then_inc(*k.even_gated.up())
    act_head_squares(act, k, even_sources(k), k.sq)
    act.wait_ge(*k.even_gated.now())
    act_attention(act, k, even_maps(k))


def pe_even_attention(pe, k):
    tensor = k.nc.tensor
    pe.wait_ge(*k.even_rows_in.next("pe", EVEN_ROWS))
    pe.wait_ge(*k.gates_kept.next("pe"))
    tensor.transpose(k.ps[:, 0, 0:4], k.gain_rows[:], k.ident[0:4, 0:4]).then_inc(*k.att_gainT.up())
    tensor.transpose(k.ps[0:RPB_COLS, 1, 0:HEADS * RPB_ROWS], k.na_rows[:],
                     k.ident[0:HEADS * RPB_ROWS, 0:HEADS * RPB_ROWS]).then_inc(*k.na_tableT.up())
    pe.wait_ge(*k.na_table_kept.next("pe"))
    table = k.na_table[:].rearrange("j (h a) -> j h a", h=HEADS)[:, :, RPB_ROWS // 2 - (GRID_ROWS - 1):
                                                                  RPB_ROWS // 2 + GRID_ROWS]
    for half in range(2):
        if half:
            pe.wait_ge(*k.na_bias_kept.next("pe"))
        for n in range(BIAS_ROUND):
            first = GRID - 1 - (half * BIAS_ROUND + n)
            pick = k.na_band[:, first:first + P]
            at = n % BIAS_PER_BANK * BIAS_COLS
            last = tensor.matmul(k.ps[:, n // BIAS_PER_BANK, at:at + BIAS_COLS], pick, table, start=True, stop=True)
        last.then_inc(*k.na_toeplitz.up())
    pe.wait_ge(*k.na_bias_kept.next("pe"))
    pe.wait_ge(*k.att_scaled.next("pe"))
    slot = 0
    for first, n, src in even_sources(k):
        for h in range(0, n, 2):
            if slot >= 4:
                pe.wait_ge(*k.att_turn_kept.next("pe"))
            for x in range(2):
                for t in range(TT):
                    last = tensor.transpose(k.ps[:, slot % 4, x * SEQ + t * P:x * SEQ + (t + 1) * P], src(t)[:, h + x, :],
                                            k.ident)
            last.then_inc(*k.att_turned.up())
            slot += 1
    pe.wait_ge(*k.att_turn_kept.next("pe", 4))
    pe_attention(pe, k, even_maps(k))


def dve_even_attention(dve, k):
    v = k.nc.vector
    dve.wait_ge(*k.att_gainT.next("dve"))
    v.tensor_copy(k.att_gain[:], k.ps[:, 0, 0:4]).then_inc(*k.dve_step.up())
    dve.wait_ge(*k.na_tableT.next("dve"))
    v.tensor_copy(k.na_table[:], k.ps[0:RPB_COLS, 1, 0:HEADS * RPB_ROWS]).then_inc(*k.na_table_kept.up())
    dve.wait_ge(*k.dve_step.now())
    for n in (0, 2):
        last = v.tensor_scalar(k.att_gain[:, n:n + 1], k.att_gain[:, n:n + 1], k.att_gain[:, n + 1:n + 2], HD ** -0.5,
                               ALU.mult, ALU.mult)
    last.then_inc(*k.att_gained.up())
    for half in range(2):
        dve.wait_ge(*k.na_toeplitz.next("dve"))
        for first in range(0, BIAS_ROUND, BIAS_PER_BANK):
            n = min(BIAS_PER_BANK, BIAS_ROUND - first)
            src = k.ps[:, first // BIAS_PER_BANK, 0:n * BIAS_COLS].rearrange("p (c h a) -> p h a c", c=n, h=HEADS)
            keys = slice(half * BIAS_ROUND + first, half * BIAS_ROUND + first + n)
            for t in range(TT):
                for r in range(2):
                    part = slice(r * GRID, (r + 1) * GRID)
                    a = GRID_ROWS - 1 - (2 * t + r)
                    window = k.na_window[part, keys].unsqueeze(1).unsqueeze(1).to_broadcast([GRID, HEADS, GRID_ROWS, n])
                    last = v.tensor_tensor(k.na_bias[part, :, t, :, keys], src[part, :, a:a + GRID_ROWS, :], window, ALU.add)
        last.then_inc(*k.na_bias_kept.up())
    dve_head_norm(dve, k, even_sources(k), k.sq)
    dve.wait_ge(*k.att_gained.now())
    slot = 0
    for first, n, src in even_sources(k):
        for h in range(0, n, 2):
            dve.wait_ge(*k.att_turned.next("dve"))
            at = first + h
            turned = k.ps[:, slot % 4, :].rearrange("p (a s) -> p a s", a=2)
            to = k.na_t[:, at:at + 2, :]
            if at < HEADS or 2 * HEADS <= at < 2 * HEADS + MEM_HEADS:
                gain = 0 if at < HEADS else 2
                ins = v.tensor_scalar(to, turned, k.att_gain[:, gain:gain + 1], None, ALU.mult)
            else:
                ins = v.tensor_copy(to, turned)
            ins.then_inc(*k.att_turn_kept.up())
            slot += 1
    dve.wait_ge(*k.even_gated.next("dve"))
    dve_attention(dve, k, even_maps(k))



def early_tile(d):
    return d


def dirs(d):
    return slice(d * HEADS, (d + 1) * HEADS)


def late(d):
    return slice((1 - d) * P, (2 - d) * P)


def pair_mask(k, n):
    return k.proj[:, n // 4, MG + n % 4 * P:MG + (n % 4 + 1) * P]


def heads_of(ap):
    return ap.rearrange("p (h e) -> p h e", h=HEADS)


def pool_delta(pool, k):
    g = k.nc.gpsimd
    d = k.dram
    pool.wait_ge(*k.at_y.next("pool", HEADS + MEM_HEADS))
    pool.dma_start(k.dn_rows[:], d["dn_conv_w_2"][0]).then_inc(*k.dn_rows_in.up(16))
    pairs = d["c_pairs"].rearrange("p (n i) -> p n i", n=LEVELS)
    for t, first, end in ((0, 0, 4), (1, 4, LEVELS)):
        to = k.proj[:, t, MG:MG + (end - first) * P].rearrange("p (n i) -> p n i", n=end - first)
        pool.dma_start(to, pairs[:, first:end, :]).then_inc(*k.dn_pairs_in.up(16))
    g.memset(k.dn_u[:, :, 0:2], 0.0)
    g.memset(k.dn_u[:, :, SEQ + 2:DN_T], 0.0).then_inc(*k.dn_pad.up())
    pool.wait_ge(*k.dn_scaled.next("pool"))
    pool.wait_ge(*k.dn_g_done.next("pool"))
    for t in range(TT):
        if t:
            pool.wait_ge(*k.dn_row.next("pool"))
        for dr, tri in ((0, k.tri), (1, k.tri_t)):
            last = g.tensor_tensor(k.dn_rhs[:, dirs(dr), :], tri.unsqueeze(1).to_broadcast([P, HEADS, P]),
                                   k.dn_g[:, t, dirs(dr)].unsqueeze(2).to_broadcast([P, HEADS, P]), ALU.mult)
        last.then_inc(*k.dn_tri_g.up())
        pool.wait_ge(*k.dn_decay.next("pool"))
        for dr, tri in ((0, k.tri), (1, k.tri_t)):
            last = g.tensor_tensor(k.dn_dec[:, dirs(dr), :], k.dn_dec[:, dirs(dr), :],
                                   tri.unsqueeze(1).to_broadcast([P, HEADS, P]), ALU.mult)
        last.then_inc(*k.dn_decay_masked.up())
    k.dn_row.next("pool")
    pool.wait_ge(*k.dn_pairs_in.next("pool", 32))
    pool.wait_ge(*k.dn_qk_kept.next("pool", 2))
    for n in reversed(range(LEVELS)):
        for t in range(TT):
            if (n, t) == (LEVELS - 1, 1):
                pool.wait_ge(*k.dn_up_kept.next("pool", 1))
            elif (n, t) == (LEVELS - 2, 0):
                pool.wait_ge(*k.dn_up_kept.next("pool", 1))
            elif (n, t) != (LEVELS - 1, 0):
                pool.wait_ge(*k.dn_m_done.next("pool", 3))
            g.tensor_tensor(k.dn_off[:], k.dn_a[:, t], pair_mask(k, n).unsqueeze(1).to_broadcast([P, DIRS, P]),
                            ALU.mult).then_inc(*k.dn_off_ready.up())


def act_delta(act, k):
    a = k.nc.scalar

    def step(ins):
        ins.then_inc(*k.act_step.up())
        act.wait_ge(*k.act_step.now())

    act.wait_ge(*k.dn_abs.next("act"))
    step(a.activation(k.dn_sp[:], k.dn_x[:], ACT.Abs))
    step(a.activation(k.dn_sp[:], k.dn_sp[:], ACT.Exp, scale=-1.0))
    a.activation(k.dn_rate[:], k.dn_rate[:], ACT.Exp)
    a.activation(k.dn_sp[:], k.dn_sp[:], ACT.Ln, bias=1.0).then_inc(*k.dn_soft.up())
    act.wait_ge(*k.dn_lnb.next("act"))
    a.activation(k.dn_beta[:], k.dn_beta[:], ACT.Exp).then_inc(*k.dn_beta_done.up())
    act.wait_ge(*k.dn_cum_kept.next("act"))
    a.activation(k.dn_ecum[:], k.dn_cum[:], ACT.Exp)
    a.activation(k.dn_tail[:], k.dn_tail[:], ACT.Exp).then_inc(*k.dn_e.up())
    act.wait_ge(*k.at_y.next("act", HEADS + MEM_HEADS))
    for g in range(DN_TILES // 2):
        act.wait_ge(*k.dn_turned.next("act"))
        a.activation(k.dn_u[:, 2 * g:2 * g + 2, 2:SEQ + 2], k.ps[:, g % 4, :].rearrange("p (a s) -> p a s", a=2),
                     ACT.Copy).then_inc(*k.dn_turn_kept.up())
    for part in range(3):
        act.wait_ge(*k.dn_tap.next("act", HEADS * DN_TAPS))
        y = k.dn_y[:, dirs(part), :]
        a.activation(y, y, ACT.Silu).then_inc(*k.dn_silu.up())
        for g in range(3 * part, 3 * part + 3):
            act.wait_ge(*k.dn_back.next("act"))
            a.activation(k.proj[:, :, DQ + g * 2 * P:DQ + (g + 1) * 2 * P],
                         k.ps[:, g % 4, :].rearrange("p (t c) -> p t c", t=TT), ACT.Copy).then_inc(*k.dn_back_kept.up())
    act.wait_ge(*k.dn_back_kept.now())
    a.activation(k.dn_sq[:], k.proj[:, :, DQ:DQ + 2 * HW], ACT.Square).then_inc(*k.dn_squared.up())
    act.wait_ge(*k.dn_summed.next("act"))
    a.activation(k.head_ss[:, :, 0:DIRS], k.head_ss[:, :, 0:DIRS], ACT.Sqrt, bias=k.eps[:, 1:2]).then_inc(*k.dn_rooted.up())
    for t in range(TT):
        act.wait_ge(*k.dn_rel.next("act"))
        a.activation(k.dn_dec[:], k.dn_dec[:], ACT.Exp).then_inc(*k.dn_decay.up())
    banks = 0
    inverse = (k.dn_inv, k.dn_inv2)
    for n in reversed(range(LEVELS)):
        for t in range(TT):
            if n < LEVELS - 1:
                for g in range(3):
                    act.wait_ge(*k.dn_m_done.next("act"))
                    a.activation(k.dn_m[:, 4 * g:4 * g + 4, :], bank_of(k, banks), ACT.Copy).then_inc(*k.dn_m_kept.up())
                    banks += 1
                banks += 3
            if n > 0:
                for g in range(3):
                    act.wait_ge(*k.dn_it_done.next("act"))
                    a.activation(inverse[t][:, 4 * g:4 * g + 4, :], bank_of(k, banks), ACT.Copy).then_inc(*k.dn_it_kept.up())
                    banks += 1
    act.wait_ge(*k.dn_s_done.next("act"))
    a.activation(k.dn_state[:], three_banks(k), ACT.Copy).then_inc(*k.dn_s_kept.up())
    act.wait_ge(*k.dn_o_kept.next("act"))
    a.activation(k.dn_a[:, :, dirs(1), :], k.dn_a[:, :, dirs(0), :], ACT.Square).then_inc(*k.dn_osq.up())
    act.wait_ge(*k.dn_oms.next("act"))
    a.activation(k.dn_ms[:], k.dn_ms[:], ACT.Sqrt, scale=1.0 / HD, bias=k.eps[:, 1:2]).then_inc(*k.dn_oroot.up())


def bank_of(k, n):
    return k.ps[:, n % 4, :].rearrange("p (a i) -> p a i", a=4)


def three_banks(k):
    return k.ps[:, 0:3, :].rearrange("p b (a i) -> p (b a) i", a=4)


def pe_delta(pe, k):
    tensor = k.nc.tensor
    pe.wait_ge(*k.dn_g_done.next("pe"))
    for t in range(TT):
        for at, n, square, g in ((0, HEADS, k.tri, dirs(0)), (HEADS, HEADS, k.tri_t, dirs(1)), (DIRS, DIRS, k.ones, slice(0, DIRS))):
            at += t * 2 * DIRS
            last = tensor.matmul(k.ps[:, 0, at:at + n], square, k.dn_g[:, t, g], start=True, stop=True)
    last.then_inc(*k.dn_cums.up())
    pe.wait_ge(*k.dn_rows_in.next("pe", 16))
    pe.wait_ge(*k.dn_cum_kept.next("pe"))
    for c in range(DN_TILES):
        last = tensor.transpose(k.ps[:, 3, c * DN_TAPS:(c + 1) * DN_TAPS], k.dn_rows[:, c * P:(c + 1) * P],
                                k.ident[0:DN_TAPS, 0:DN_TAPS])
    last.then_inc(*k.dn_wT.up())
    pe.wait_ge(*k.dn_w_kept.next("pe"))
    for g in range(DN_TILES // 2):
        if g >= 4:
            pe.wait_ge(*k.dn_turn_kept.next("pe"))
        for x in range(2):
            for t in range(TT):
                last = tensor.transpose(k.ps[:, g % 4, x * SEQ + t * P:x * SEQ + (t + 1) * P],
                                        k.proj[:, t, DQ + (2 * g + x) * P:DQ + (2 * g + x + 1) * P], k.ident)
        last.then_inc(*k.dn_turned.up())
    pe.wait_ge(*k.dn_turn_kept.next("pe", 4))
    for g in range(DN_TILES // 2):
        if g % 3 == 0:
            pe.wait_ge(*k.dn_silu.next("pe"))
        if g >= 4:
            pe.wait_ge(*k.dn_back_kept.next("pe"))
        for t in range(TT):
            for x in range(2):
                last = tensor.transpose(k.ps[:, g % 4, t * SEQ + x * P:t * SEQ + (x + 1) * P],
                                        k.dn_y[:, 2 * g + x, t * P:(t + 1) * P], k.ident)
        last.then_inc(*k.dn_back.up())
    pe.wait_ge(*k.dn_back_kept.next("pe", 4))
    pe.wait_ge(*k.dn_scaled.next("pe"))
    for g in range(HEADS):
        if g >= 4:
            pe.wait_ge(*k.dn_qkT_kept.next("pe"))
        for x in range(2):
            for t in range(TT):
                last = tensor.transpose(k.ps[:, g % 4, x * SEQ + t * P:x * SEQ + (t + 1) * P],
                                        k.proj[:, t, DQ + (2 * g + x) * P:DQ + (2 * g + x + 1) * P], k.ident)
        last.then_inc(*k.dn_qkT.up())
    pe.wait_ge(*k.dn_qkT_kept.next("pe", 4))
    for t in range(TT):
        pe.wait_ge(*k.dn_tri_g.next("pe"))
        if t:
            pe.wait_ge(*k.dn_qk_kept.next("pe"))
        for g in range(3):
            last = tensor.matmul(k.ps[:, g, :], k.ones, k.dn_rhs[:, 4 * g:4 * g + 4, :], start=True, stop=True)
        last.then_inc(*k.dn_row.up())
        pe.wait_ge(*k.dn_rel.next("pe"))
        tokens = slice(t * P, (t + 1) * P)
        for x, which in ((0, 1), (2, 0)):
            for h in range(HEADS):
                last = tensor.matmul(k.ps[:, x + h // 4, h % 4 * P:(h % 4 + 1) * P], k.dn_t[:, 1, h, tokens],
                                     k.dn_t[:, which, h, tokens], start=True, stop=True)
        last.then_inc(*k.dn_kk.up())
    pe.wait_ge(*k.dn_qk_kept.next("pe"))

    readers = [None] * 4
    banks = 0
    inverse = (k.dn_inv, k.dn_inv2)

    def group(count, kept, g, left, right, turn=False):
        nonlocal banks
        if readers[banks % 4]:
            pe.wait_ge(*readers[banks % 4])
        out = bank_of(k, banks)
        for x in range(4):
            n = 4 * g + x
            if turn:
                last = tensor.transpose(out[:, x, :], left[:, n, :], k.ident)
            else:
                last = tensor.matmul(out[:, x, :], left[:, n, :], right[:, n, :], start=True, stop=True)
        last.then_inc(*count.up())
        readers[banks % 4] = kept.next("issued")
        banks += 1

    for n in reversed(range(LEVELS)):
        for t in range(TT):
            rows = k.dn_rows_t[:, t]
            if n < LEVELS - 1:
                pe.wait_ge(*k.dn_off_ready.next("pe"))
                pe.wait_ge(*inverse_kept[t])
                for g in range(3):
                    group(k.dn_m_done, k.dn_m_kept, g, k.dn_off, inverse[t])
                for g in range(3):
                    pe.wait_ge(*k.dn_m_kept.next("pe"))
                    group(k.dn_up_done, k.dn_rows_kept, g, k.dn_m, rows)
            else:
                pe.wait_ge(*k.dn_up_kept.next("pe"))
                k.dn_off_ready.next("pe")
                inverse_kept = [None, None] if t == 0 else inverse_kept
            if n > 0:
                for g in range(3):
                    if n < LEVELS - 1:
                        pe.wait_ge(*k.dn_rows_kept.next("pe"))
                    group(k.dn_it_done, k.dn_it_kept, g, rows, None, turn=True)
                inverse_kept[t] = k.dn_it_kept.sem, k.dn_it_kept.seen["issued"]
    pe.wait_ge(*k.dn_rows_kept.next("pe", 6))

    out = three_banks(k)

    def each(left, right):
        for n in range(DIRS):
            d, h = divmod(n, HEADS)
            last = tensor.matmul(out[:, n, :], left(n, d, h), right(n, d, h), start=True, stop=True)
        return last

    each(lambda n, d, h: k.dn_rows_t[:, d, n, :],
         lambda n, d, h: k.proj[:, d, DV + h * HD:DV + (h + 1) * HD]).then_inc(*k.dn_tv.up())
    pe.wait_ge(*k.dn_vs_kept.next("pe"))
    each(lambda n, d, h: k.proj[:, d, DK + h * HD:DK + (h + 1) * HD], lambda n, d, h: k.dn_vs[:, n, :])\
        .then_inc(*k.dn_s_done.up())
    pe.wait_ge(*k.dn_s_kept.next("pe"))
    each(lambda n, d, h: k.dn_t[:, 1, h, late(d)], lambda n, d, h: k.dn_state[:, n, :]).then_inc(*k.dn_ks.up())
    pe.wait_ge(*k.dn_ks_kept.next("pe"))
    each(lambda n, d, h: k.dn_t[:, 0, h, late(d)], lambda n, d, h: k.dn_state[:, n, :]).then_inc(*k.dn_qs_done.up())
    pe.wait_ge(*k.dn_qs_kept.next("pe"))
    each(lambda n, d, h: k.dn_rows_t[:, 1 - d, n, :], lambda n, d, h: k.dn_r[:, n, :]).then_inc(*k.dn_tv2.up())
    pe.wait_ge(*k.dn_v2_kept.next("pe"))
    for t in range(TT):
        for h in range(HEADS):
            for d in range(2):
                n = d * HEADS + h
                value = k.dn_v1 if t == early_tile(d) else k.dn_v2
                last = tensor.matmul(out[:, t * HEADS + h, :], k.dn_qk[:, t, n, :], value[:, n, :], start=d == 0, stop=d == 1)
    last.then_inc(*k.dn_o.up())


def dve_delta(dve, k):
    v = k.nc.vector

    def step(ins):
        ins.then_inc(*k.dve_step.up())
        dve.wait_ge(*k.dve_step.now())

    step(v.tensor_tensor(k.dn_x[:, :, DIRS:], k.dn_x[:, :, DIRS:], k.dn_shift[:].unsqueeze(1).to_broadcast([P, TT, DIRS]),
                         ALU.add))
    v.memset(k.dn_ms[:], 0.0).then_inc(*k.dn_abs.up())
    dve.wait_ge(*k.dn_soft.next("dve"))
    step(v.scalar_tensor_tensor(k.dn_sp[:], k.dn_x[:], 0.0, k.dn_sp[:], ALU.max, ALU.add))
    v.tensor_tensor(k.dn_beta[:], k.dn_x[:, :, 0:DIRS], k.dn_sp[:, :, 0:DIRS], ALU.subtract).then_inc(*k.dn_lnb.up())
    v.scalar_tensor_tensor(k.dn_g[:], k.dn_sp[:, :, DIRS:], -1.0, k.dn_rate[:].unsqueeze(1).to_broadcast([P, TT, DIRS]),
                           ALU.mult, ALU.mult).then_inc(*k.dn_g_done.up())
    dve.wait_ge(*k.dn_cums.next("dve"))
    sums = k.ps[:, 0, 0:4 * DIRS].rearrange("p (t x n) -> p t x n", t=TT, x=2)
    v.tensor_copy(k.dn_cum[:], sums[:, :, 0, :])
    step(v.tensor_copy(k.dn_total[:], sums[:, :, 1, :]))
    v.tensor_tensor(k.dn_tail[:], k.dn_total[:], k.dn_cum[:], ALU.subtract).then_inc(*k.dn_cum_kept.up())
    dve.wait_ge(*k.dn_beta_done.next("dve"))
    dve.wait_ge(*k.dn_e.next("dve"))
    step(v.tensor_tensor(k.dn_tail[:], k.dn_tail[:], k.dn_beta[:], ALU.mult))
    dve.wait_ge(*k.dn_wT.next("dve"))
    v.tensor_copy(k.dn_w[:], k.ps[:, 3, 0:DN_TILES * DN_TAPS].rearrange("p (c x) -> p c x", c=DN_TILES))\
        .then_inc(*k.dn_w_kept.up())
    dve.wait_ge(*k.dn_w_kept.now())
    dve.wait_ge(*k.dn_pad.next("dve"))
    sem, done = k.dn_tap.now()
    for part in range(3):
        dve.wait_ge(*k.dn_turn_kept.next("dve", 3))
        for tap in range(DN_TAPS):
            for x in range(HEADS):
                c = part * HEADS + x
                u, y, w = k.dn_u[:, c, tap:tap + SEQ], k.dn_y[:, c, :], k.dn_w[:, c, tap:tap + 1]
                if tap == 0:
                    ins = v.tensor_scalar(y, u, w, None, ALU.mult)
                else:
                    dve.wait_ge(sem, done + HEADS * (DN_TAPS * part + tap - 1) + x + 1)
                    ins = v.scalar_tensor_tensor(y, u, w, y, ALU.mult, ALU.add)
                ins.then_inc(*k.dn_tap.up())
    dve.wait_ge(*k.dn_squared.next("dve"))
    for t in range(TT):
        last = v.tensor_reduce(k.head_ss[:, t, 0:DIRS], k.dn_sq[:, t, :].rearrange("p (n e) -> p n e", n=DIRS), AX_X, ALU.add)
    last.then_inc(*k.dn_summed.up())
    dve.wait_ge(*k.dn_rooted.next("dve"))
    step(v.reciprocal(k.head_ss[:, :, 0:DIRS], k.head_ss[:, :, 0:DIRS]))
    step(v.tensor_scalar(k.head_ss[:, :, 0:HEADS], k.head_ss[:, :, 0:HEADS], HD ** -0.5, None, ALU.mult))
    for t in range(TT):
        qk = k.proj[:, t, DQ:DQ + 2 * HW].rearrange("p (n e) -> p n e", n=DIRS)
        last = v.tensor_tensor(qk, qk, k.head_ss[:, t, 0:DIRS].unsqueeze(2).to_broadcast([P, DIRS, HD]), ALU.mult)
    last.then_inc(*k.dn_scaled.up())
    for g in range(HEADS):
        dve.wait_ge(*k.dn_qkT.next("dve"))
        at = 2 * g % HEADS
        v.tensor_copy(k.dn_t[:, 2 * g // HEADS, at:at + 2, :], k.ps[:, g % 4, :].rearrange("p (a s) -> p a s", a=2))\
            .then_inc(*k.dn_qkT_kept.up())
    rows = three_banks(k)
    for t in range(TT):
        dve.wait_ge(*k.dn_row.next("dve"))
        step(v.tensor_tensor(k.dn_dec[:], rows, k.dn_cum[:, t, :].unsqueeze(2).to_broadcast([P, DIRS, P]), ALU.subtract))
        v.tensor_scalar(k.dn_dec[:], k.dn_dec[:], 0.0, None, ALU.min).then_inc(*k.dn_rel.up())
        dve.wait_ge(*k.dn_decay_masked.next("dve"))
        dve.wait_ge(*k.dn_kk.next("dve"))
        for n in range(DIRS):
            h = n % HEADS
            v.scalar_tensor_tensor(k.dn_a[:, t, n, :], k.ps[:, h // 4, h % 4 * P:(h % 4 + 1) * P], k.dn_beta[:, t, n:n + 1],
                                   k.dn_dec[:, n, :], ALU.mult, ALU.mult)
        qk = k.ps[:, 2:4, :].rearrange("p b (a i) -> p (b a) i", a=4)[:, 0:HEADS, :]
        for d in range(2):
            last = v.tensor_tensor(k.dn_qk[:, t, dirs(d), :], qk, k.dn_dec[:, dirs(d), :], ALU.mult)
        last.then_inc(*k.dn_qk_kept.up())
        dve.wait_ge(*k.dn_qk_kept.now())
    banks = 0
    for n in reversed(range(LEVELS)):
        for t in range(TT):
            if n == LEVELS - 1:
                dve.wait_ge(*k.dn_off_ready.next("dve"))
                v.tensor_tensor(k.dn_rows_t[:, t], k.ident.unsqueeze(1).to_broadcast([P, DIRS, P]), k.dn_off[:],
                                ALU.subtract).then_inc(*k.dn_up_kept.up())
                dve.wait_ge(*k.dn_up_kept.now())
            else:
                banks += 3
                for g in range(3):
                    dve.wait_ge(*k.dn_up_done.next("dve"))
                    part = k.dn_rows_t[:, t, 4 * g:4 * g + 4, :]
                    v.tensor_tensor(part, part, bank_of(k, banks), ALU.subtract).then_inc(*k.dn_rows_kept.up())
                    banks += 1
            if n > 0:
                banks += 3
    out = three_banks(k)

    def by_token(to, scale, tile):
        for d in range(2):
            last = v.tensor_tensor(to[:, dirs(d), :], out[:, dirs(d), :],
                                   scale[:, tile(d), dirs(d)].unsqueeze(2).to_broadcast([P, HEADS, HD]), ALU.mult)
        return last

    dve.wait_ge(*k.dn_tv.next("dve"))
    by_token(k.dn_v1, k.dn_beta, lambda d: d)
    by_token(k.dn_vs, k.dn_tail, lambda d: d).then_inc(*k.dn_vs_kept.up())
    dve.wait_ge(*k.dn_ks.next("dve"))
    step(by_token(k.dn_r, k.dn_ecum, lambda d: 1 - d))
    for d in range(2):
        last = v.tensor_tensor(k.dn_r[:, dirs(d), :], heads_of(k.proj[:, 1 - d, DV:DV + HW]), k.dn_r[:, dirs(d), :],
                               ALU.subtract)
    last.then_inc(*k.dn_ks_kept.up())
    dve.wait_ge(*k.dn_qs_done.next("dve"))
    by_token(k.dn_qs, k.dn_ecum, lambda d: 1 - d).then_inc(*k.dn_qs_kept.up())
    dve.wait_ge(*k.dn_tv2.next("dve"))
    by_token(k.dn_v2, k.dn_beta, lambda d: 1 - d).then_inc(*k.dn_v2_kept.up())
    dve.wait_ge(*k.dn_qs_kept.now())
    dve.wait_ge(*k.dn_o.next("dve"))
    for t in range(TT):
        last = v.tensor_tensor(k.dn_a[:, t, dirs(0), :], out[:, t * HEADS:(t + 1) * HEADS, :], k.dn_qs[:, dirs(1 - t), :],
                               ALU.add)
    last.then_inc(*k.dn_o_kept.up())
    dve.wait_ge(*k.dn_osq.next("dve"))
    for t in range(TT):
        last = v.tensor_reduce(k.dn_ms[:, t, :], k.dn_a[:, t, dirs(1), :], AX_X, ALU.add)
    last.then_inc(*k.dn_oms.up())
    dve.wait_ge(*k.dn_oroot.next("dve"))
    step(v.reciprocal(k.dn_ms[:], k.dn_ms[:]))
    for t in range(TT):
        o = k.dn_a[:, t, dirs(0), :]
        step(v.tensor_tensor(o, o, k.dn_ms[:, t, :].unsqueeze(2).to_broadcast([P, HEADS, HD]), ALU.mult))
        step(v.tensor_tensor(o, o, k.dn_norm[:].unsqueeze(1).to_broadcast([P, HEADS, HD]), ALU.mult))
        gate = heads_of(k.proj[:, t, DG:DG + HW])
        ins = v.tensor_tensor(gate, gate, o, ALU.mult)
        if t == 0:
            step(ins)
    ins.then_inc(*k.turn_source.up(BLOCKS))


def even_mix_tile(k):
    def tile(kt, t):
        at = NQ + P * kt if kt < HEADS else DG + P * (kt - HEADS) if kt < 2 * HEADS else MQ + P * (kt - 2 * HEADS)
        return k.proj[:, t, at:at + P]
    return tile


ODD_ROWS = 7 * 16


def odd_sources(k):
    def heads(buffer, at, n):
        return lambda t: buffer[:, t, at:at + n * HD].rearrange("p (n d) -> p n d", n=n)
    m0 = 2 * DIFF_MAPS
    return [(0, DIFF_MAPS, heads(k.proj, OQ, DIFF_MAPS)), (DIFF_MAPS, DIFF_MAPS, heads(k.proj, OK, DIFF_MAPS)),
            (m0, MEM_HEADS, heads(k.proj, MQ, MEM_HEADS)), (m0 + MEM_HEADS, MEM_HEADS, heads(k.kv, 2 * MW, MEM_HEADS))]


def odd_mem_maps(k):
    def cols(buffer, at):
        return lambda t: buffer[:, t, at:at + HD]
    m0 = 2 * DIFF_MAPS
    return [(k.o_t[:, m0 + h, :], k.o_t[:, m0 + MEM_HEADS + h, :], None, cols(k.kv, 3 * MW + h * HD),
             cols(k.proj, MG + h * HD), cols(k.proj, MQ + h * HD)) for h in range(MEM_HEADS)]


def rotate_in_place(own, k, which, at, step):
    for t in range(TT):
        x = k.proj[:, t, at:at + DIFF_W].rearrange("p (n x s) -> p n x s", n=DIFF_MAPS, x=2)
        x1, x2 = x[:, :, 0, :], x[:, :, 1, :]
        a, b, c, d = (k.o_tables[:, which, n, t, :].unsqueeze(1).to_broadcast([P, DIFF_MAPS, HALF]) for n in range(4))
        w0, w1 = k.o_work[:, which, 0], k.o_work[:, which, 1]
        own.tensor_tensor(w0, x2, b, ALU.mult)
        step(own.tensor_tensor(w1, x1, c, ALU.mult))
        own.tensor_tensor(x1, x1, a, ALU.mult)
        step(own.tensor_tensor(x2, x2, d, ALU.mult))
        own.tensor_tensor(x1, x1, w0, ALU.subtract)
        last = own.tensor_tensor(x2, x2, w1, ALU.add)
        if t < TT - 1:
            step(last)
    return last


def pool_odd_rows(pool, k):
    d = k.dram
    rope = d["c_rope"].rearrange("(t p) (x s) -> p t x s", p=P, x=2)
    lam = d["df_lambda_2"].rearrange("a b c -> (a b c)").partition_broadcast(P).rearrange("p (a b c) -> p a b c", a=2, b=2)
    for to, src in ((k.o_rope[:], rope), (k.o_lam_rows[:], lam),
                    (k.o_gain[:, 0, :], d["df_q_norm_2"][0].partition_broadcast(P)),
                    (k.o_gain[:, 1, :], d["df_k_norm_2"][0].partition_broadcast(P)),
                    (k.o_gain[:, 2, :], d["o_mem_q_norm_2"][0].partition_broadcast(P)),
                    (k.o_gain[:, 3, :], d["o_mem_k_norm_2"][0].partition_broadcast(P)),
                    (k.o_subln[:], d["df_subln_2"][0].partition_broadcast(P))):
        pool.dma_start(to, src).then_inc(*k.o_rows_in.up(16))


def pool_odd_attention(pool, k):
    def step(ins):
        ins.then_inc(*k.pool_step.up())
        pool.wait_ge(*k.pool_step.now())

    g = k.nc.gpsimd
    pool.wait_ge(*k.o_tables_done.next("pool"))
    pool.wait_ge(*k.att_scaled.next("pool", 2))
    rotate_in_place(g, k, 1, OK, step).then_inc(*k.o_keys.up())
    pool.wait_ge(*k.o_rows_in.next("pool", ODD_ROWS))
    pool.wait_ge(*k.o_gated.next("pool"))
    for t in range(TT):
        gate = k.proj[:, t, OG:OG + DIFF_W].rearrange("p (h e) -> p h e", h=HEADS)
        last = g.tensor_tensor(gate, gate, k.o_subln[:].unsqueeze(1).to_broadcast([P, HEADS, 2 * HD]), ALU.mult)
    last.then_inc(*k.o_gate_done.up())


def act_odd_attention(act, k):
    a = k.nc.scalar
    act.wait_ge(k.evacuated, 2 * BLOCKS + k.block0["act"])
    for at, n in ((OG, DIFF_W), (MG, MW)):
        cols = k.proj[:, :, at:at + n]
        last = a.activation(cols, cols, ACT.Silu)
    last.then_inc(*k.o_gated.up())
    act_head_squares(act, k, odd_sources(k), k.o_sq)
    act.wait_ge(*k.o_lam_sums.next("act"))
    a.activation(k.lam[:, 0:2], k.lam[:, 0:2], ACT.Exp).then_inc(*k.o_lam_exp.up())
    for g in range(len(odd_turns(k))):
        act.wait_ge(*k.o_turned.next("act"))
        at = odd_turns(k)[g][0]
        a.activation(k.o_t[:, at:at + 2, :], k.ps[:, g % 4, :].rearrange("p (a s) -> p a s", a=2),
                     ACT.Copy).then_inc(*k.o_turn_kept.up())
    act.wait_ge(*k.o_keys.next("act"))
    for n in range(HEADS + 2):
        if n < HEADS:
            act.wait_ge(*k.d_max.next("act"))
            if n >= 2:
                act.wait_ge(*k.d_t.next("act free"))
            for m, to in ((0, k.att_e), (1, k.att_s)):
                for t in range(TT):
                    last = a.activation(to[:, n % 2, t, :], k.ps[:, m, t * SEQ:(t + 1) * SEQ], ACT.Exp,
                                        bias=k.att_max[:, 2 * n + m, t:t + 1],
                                        accum_out=k.att_sum[:, 2 * n + m, t:t + 1])
            last.then_inc(*k.d_e.up())
        if 1 <= n <= HEADS:
            act.wait_ge(*k.d_t.next("act"))
            if n >= 3:
                act.wait_ge(*k.d_o.next("act free"))
            a.activation(k.att_t[:, (n - 1) % 2], k.ps[:, 2, :].rearrange("p (a s) -> p a s", a=TT), ACT.Copy)\
                .then_inc(*k.d_c.up())
        if n >= 2:
            if n >= 4:
                act.wait_ge(k.d_sq.sem, k.d_sq.made - 1)
            act.wait_ge(*k.d_o.next("act"))
            for t in range(TT):
                last = a.activation(k.o_junk[:, n % 2, t, :], k.ps[:, 3, t * 2 * HD:(t + 1) * 2 * HD], ACT.Square,
                                    accum_out=k.o_ss[:, t, n - 2:n - 1])
            last.then_inc(*k.d_sq.up())
    act_attention(act, k, odd_mem_maps(k))
    act.wait_ge(*k.d_sq.now())
    a.activation(k.o_ss[:], k.o_ss[:], ACT.Sqrt, scale=1.0 / (2 * HD), bias=k.eps[:, 1:2]).then_inc(*k.o_root.up())


def odd_turns(k):
    m0 = 2 * DIFF_MAPS
    order = [*range(0, DIFF_MAPS, 2), *range(m0, m0 + 2 * MEM_HEADS, 2), *range(DIFF_MAPS, m0, 2)]
    out = []
    for at in order:
        for first, n, src in odd_sources(k):
            if first <= at < first + n:
                out.append((at, at - first, src))
    return out


def pe_odd_attention(pe, k):
    tensor = k.nc.tensor
    pe.wait_ge(*k.o_queries.next("pe"))
    for g, (at, h, src) in enumerate(odd_turns(k)):
        if at == DIFF_MAPS:
            pe.wait_ge(*k.o_keys.next("pe"))
        if g >= 4:
            pe.wait_ge(*k.o_turn_kept.next("pe"))
        for x in range(2):
            for t in range(TT):
                last = tensor.transpose(k.ps[:, g % 4, x * SEQ + t * P:x * SEQ + (t + 1) * P], src(t)[:, h + x, :], k.ident)
        last.then_inc(*k.o_turned.up())
    pe.wait_ge(*k.o_turn_kept.next("pe", 4))
    for n in range(HEADS + 2):
        if n < HEADS:
            if n >= 1:
                pe.wait_ge(*k.d_e.next("pe"))
            for m in range(2):
                q, key = k.o_t[:, 2 * n + m, :], k.o_t[:, DIFF_MAPS + 2 * n + m, :]
                for t in range(TT):
                    last = tensor.matmul(k.ps[:, m, t * SEQ:(t + 1) * SEQ], q[:, t * P:(t + 1) * P], key, start=True, stop=True)
            last.then_inc(*k.d_s.up())
        if 1 <= n <= HEADS:
            pe.wait_ge(*k.d_a.next("pe"))
            if n >= 2:
                pe.wait_ge(*k.d_c.next("pe free"))
            for t in range(TT):
                for kt in range(TT):
                    last = tensor.transpose(k.ps[:, 2, kt * SEQ + t * P:kt * SEQ + (t + 1) * P],
                                            k.att_e[:, (n - 1) % 2, t, kt * P:(kt + 1) * P], k.ident)
            last.then_inc(*k.d_t.up())
        if n >= 2:
            h = n - 2
            pe.wait_ge(*k.d_c.next("pe"))
            if h >= 1:
                pe.wait_ge(*k.d_y.next("pe"))
            for t in range(TT):
                for kt in range(TT):
                    last = tensor.matmul(k.ps[:, 3, t * 2 * HD:(t + 1) * 2 * HD], k.att_t[:, h % 2, kt, t * P:(t + 1) * P],
                                         k.proj[:, kt, OV + h * 2 * HD:OV + (h + 1) * 2 * HD], start=kt == 0, stop=kt == TT - 1)
            last.then_inc(*k.d_o.up())
    pe.wait_ge(*k.d_y.next("pe"))
    pe.wait_ge(*k.d_e.next("pe"))
    pe_attention(pe, k, odd_mem_maps(k))


def dve_odd_attention(dve, k):
    v = k.nc.vector

    def step(ins):
        ins.then_inc(*k.dve_step.up())
        dve.wait_ge(*k.dve_step.now())

    dve.wait_ge(*k.o_rows_in.next("dve", ODD_ROWS))
    step(v.tensor_scalar(k.o_gain[:, 0, :], k.o_gain[:, 0, :], HD ** -0.5, None, ALU.mult))
    v.scalar_tensor_tensor(k.o_mem_gain[:], k.o_gain[:, 2, :], HD ** -0.5, k.o_gain[:, 3, :], ALU.mult, ALU.mult)
    for which in range(2):
        for n, (x, part) in enumerate(((0, 0), (1, 1), (1, 0), (0, 1))):
            gain = k.o_gain[:, which, part * HALF:(part + 1) * HALF].unsqueeze(1).to_broadcast([P, TT, HALF])
            last = v.tensor_tensor(k.o_tables[:, which, n], k.o_rope[:, :, x, :], gain, ALU.mult)
    last.then_inc(*k.o_tables_done.up())
    pairs = k.o_lam_rows
    step(v.tensor_tensor(pairs[:, :, 0, :], pairs[:, :, 0, :], pairs[:, :, 1, :], ALU.mult))
    v.tensor_reduce(k.lam[:, 0:2], pairs[:, :, 0, :], AX_X, ALU.add).then_inc(*k.o_lam_sums.up())
    dve_head_norm(dve, k, odd_sources(k), k.o_sq)
    dve.wait_ge(*k.att_scaled.now())
    mem_q = k.proj[:, :, MQ:MQ + MW].rearrange("p t (n d) -> p t n d", n=MEM_HEADS)
    for t in range(TT):
        v.tensor_tensor(mem_q[:, t], mem_q[:, t], k.o_mem_gain[:].unsqueeze(1).to_broadcast([P, MEM_HEADS, HD]), ALU.mult)
    dve.wait_ge(*k.o_lam_sums.now())
    rotate_in_place(v, k, 0, OQ, step).then_inc(*k.o_queries.up())
    dve.wait_ge(*k.o_lam_exp.next("dve"))
    step(v.tensor_tensor(k.lam[:, 2:3], k.lam[:, 0:1], k.lam[:, 1:2], ALU.subtract))
    step(v.tensor_scalar(k.lam[:, 2:3], k.lam[:, 2:3], LAM_INIT, None, ALU.add))
    dve.wait_ge(*k.o_gate_done.next("dve"))
    for n in range(HEADS + 2):
        if n < HEADS:
            dve.wait_ge(*k.d_s.next("dve"))
            v.tensor_reduce(k.att_max[:, 2 * n:2 * n + 2, :], k.ps[:, 0:2, :].rearrange("p m (t s) -> p m t s", t=TT),
                            AX_X, ALU.max, negate=True).then_inc(*k.d_max.up())
        if 1 <= n <= HEADS:
            m = 2 * (n - 1)
            e0, e1 = k.att_e[:, (n - 1) % 2], k.att_s[:, (n - 1) % 2]
            dve.wait_ge(*k.d_e.next("dve"))
            step(v.reciprocal(k.att_sum[:, m:m + 2, :], k.att_sum[:, m:m + 2, :]))
            step(v.tensor_scalar(k.att_sum[:, m + 1, :], k.att_sum[:, m + 1, :], k.lam[:, 2:3], None, ALU.mult))
            for t in range(TT):
                last = v.tensor_scalar(e1[:, t, :], e1[:, t, :], k.att_sum[:, m + 1, t:t + 1], None, ALU.mult)
            step(last)
            for t in range(TT):
                last = v.scalar_tensor_tensor(e0[:, t, :], e0[:, t, :], k.att_sum[:, m, t:t + 1], e1[:, t, :],
                                              ALU.mult, ALU.subtract)
            last.then_inc(*k.d_a.up())
        if n >= 2:
            h = n - 2
            dve.wait_ge(*k.d_sq.next("dve"))
            cols = slice(h * 2 * HD, (h + 1) * 2 * HD)
            v.tensor_tensor(k.proj[:, :, OQ:OQ + DIFF_W][:, :, cols], k.ps[:, 3, :].rearrange("p (t e) -> p t e", t=TT),
                            k.proj[:, :, OG:OG + DIFF_W][:, :, cols], ALU.mult).then_inc(*k.d_y.up())
    dve_attention(dve, k, odd_mem_maps(k))
    dve.wait_ge(*k.o_root.next("dve"))
    step(v.reciprocal(k.o_ss[:], k.o_ss[:]))
    step(v.tensor_scalar(k.o_ss[:], k.o_ss[:], 1.0 - LAM_INIT, None, ALU.mult))
    dve.wait_ge(*k.d_y.now())
    for t in range(TT):
        y = k.proj[:, t, OQ:OQ + DIFF_W].rearrange("p (h e) -> p h e", h=HEADS)
        last = v.tensor_tensor(y, y, k.o_ss[:, t, :].unsqueeze(2).to_broadcast([P, HEADS, 2 * HD]), ALU.mult)
    last.then_inc(*k.turn_source.up(BLOCKS))


def odd_mix_tile(k):
    def tile(kt, t):
        at = OQ + P * kt if kt < DIFF_MAPS else MQ + P * (kt - DIFF_MAPS)
        return k.proj[:, t, at:at + P]
    return tile


IN_UNITS, OUT_UNITS, MEM_UNITS = D_IN // NC, D // NC, 4 * MW // NC
EVEN_UNITS = 8 * HW // NC
FIRST_SUMS = DEPTH * (OUT_UNITS + FF_GROUPS * OUT_UNITS)


def x_tile(k):
    return lambda kt, t: k.x[:, t, kt * P:(kt + 1) * P]


def rows_tile(buffer):
    return lambda kt, t: buffer[:, t, kt * P:(kt + 1) * P]


def tokens(ap):
    return ap.rearrange("(t p) d -> p t d", p=P)


def two_blocks_kernel(nc, dram, out):
    k = set_up(nc, dram, out)
    first_buffers(k)
    second_buffers(k)
    d = dram

    with nc.Block() as block:

        @block.sync
        def _(sp):
            sp.dma_start(k.square[:], d["c_square"].rearrange("p (a b) -> p a b", a=4)).then_inc(*k.consts_in.up(16))
            sp.dma_start(k.x[:], tokens(d["x"][0])).then_inc(*k.x_in.up(16))
            with nc.allow_non_contiguous_dma(reason="positions"):
                sp.dma_start(k.pos_i[:], d["positions"].rearrange("a (t p) -> p (a t)", p=P)).then_inc(*k.pos_in.up(16))
            sp.dma_start(k.inv_freq[:], d["c_inv_freq"][0].partition_broadcast(P)).then_inc(*k.pos_in.up(16))
            for l in range(DEPTH):
                sp_units(sp, k, d["w_in"][l], IN_UNITS)
                sp_units(sp, k, d["w_out"][l], OUT_UNITS)
                sp_feed_forward(sp, k, d["w_ff1"][l], d["w_ff2"][l])
            sp_units(sp, k, d["e_w_mem_kv_2"][0], MEM_UNITS // 2)
            sp_units(sp, k, d["o_w_mem_kv_2"][0], MEM_UNITS // 2)
            sp_units(sp, k, d["e_w_in_2"][0], EVEN_UNITS)
            sp_units(sp, k, d["e_w_in_2"][0], IN_UNITS - EVEN_UNITS, W_MEM)
            sp_units(sp, k, d["e_w_out_2"][0], OUT_UNITS)
            sp_units(sp, k, d["o_w_in_2"][0], IN_UNITS)
            sp_units(sp, k, d["o_w_out_2"][0], OUT_UNITS)
            for c in range(OUT_UNITS):
                sp.wait_ge(k.stats_ready, FIRST_SUMS + OUT_UNITS + c + 1)
                cols = slice(c * NC, (c + 1) * NC)
                sp.dma_start(tokens(k.out[0])[:, :, cols], k.x[:, :, cols]).then_inc(*k.stored.up(16))
            sp.wait_ge(*k.stored.now())

        @block.gpsimd
        def _(pool):
            pool.sem_inc(k.relu2_ready, 2)
            nc.gpsimd.memset(k.eps[:, 0:1], LN_EPS)
            nc.gpsimd.memset(k.eps[:, 1:2], EPS).then_inc(*k.eps_set.up())
            for l in range(DEPTH):
                if l:
                    pool.wait_ge(*k.turned.next("pool", BLOCKS))
                pool_first_rows(pool, k, l)
                pool_hgrn(pool, k)
                pool_retention_rows(pool, k, l)
                pool_retention(pool, k)
                pool.wait_ge(*k.turned.next("pool", BLOCKS if l else 2 * BLOCKS))
                pool_rows(pool, k, d["ln1_g"][l], d["ln1_b"][l])
                pool.wait_ge(*k.turned.next("pool", BLOCKS))
                pool_rows(pool, k, d["ln2_g"][l], d["ln2_b"][l])
                k.block0["pool"] += (IN_UNITS + OUT_UNITS) * BLOCKS
                pool_feed_forward(pool, k, l)
            pool.wait_ge(k.evacuated, 2 * BLOCKS + k.block0["pool"])
            pool.dma_start(k.mem[:], tokens(d["mem_2"][0])).then_inc(*k.mem_in.up(16))
            pool.wait_ge(*k.normed.next("pool", BLOCKS))
            pool_rows(pool, k, d["e_ln_g_2"][0], d["mem_norm_g_2"])
            pool.wait_ge(*k.turned.next("pool", BLOCKS))
            with nc.allow_non_contiguous_dma(reason="24 columns"):
                gates = d["e_w_in_2"][0].rearrange("(kt p) n -> p kt n", p=P)[:, :, W_GATES:W_GATES + DN_GATES]
                pool.dma_start(k.gw_raw[:], gates).then_inc(*k.gw_in.up(16))
            pool.wait_ge(*k.turned.next("pool", BLOCKS))
            pool_even_rows(pool, k)
            pool_delta(pool, k)
            pool.wait_ge(*k.turned.next("pool", BLOCKS))
            pool_rows(pool, k, d["o_ln_g_2"][0])
            pool.wait_ge(*k.turned.next("pool", BLOCKS))
            pool_odd_rows(pool, k)
            pool_odd_attention(pool, k)

        @block.scalar
        def _(act):
            for c in range(HI_SLOTS):
                act_split(act, k, 0, c)
            act_positions(act, k)
            act.wait_ge(*k.eps_set.next("act"))
            for l in range(DEPTH):
                act_turn(act, k)
                split_units(act, k, "act", act_split, IN_UNITS, act_take_proj(act, k))
                act_first_gates(act, k)
                act_conv_root(act, k)
                act_conv_silu(act, k)
                act_hgrn(act, k, l)
                act_retention(act, k)
                act_turn(act, k)
                split_units(act, k, "act", act_split, OUT_UNITS)
                act_layer_norm(act, k)
                act_turn(act, k)
                act_feed_forward(act, k, l)
                act_layer_norm(act, k)
            act.wait_ge(*k.mem_in.next("act", 16))
            act_rms(act, k, k.mem, k.mem_normed)
            act_turn(act, k)
            split_units(act, k, "act", act_split, MEM_UNITS, act_take_memory(act, k))
            act.wait_ge(*k.normed.next("act", BLOCKS))
            act_rms(act, k, k.x, k.normed_x)
            act_turn(act, k)
            act_gate_columns(act, k)
            split_units(act, k, "act", act_split, EVEN_UNITS, act_take_proj(act, k))
            split_units(act, k, "act", act_split, IN_UNITS - EVEN_UNITS, act_take_proj(act, k, MQ))
            act_even_attention(act, k)
            act_delta(act, k)
            act_turn(act, k)
            split_units(act, k, "act", act_split, OUT_UNITS)
            act.wait_ge(k.stats_ready, FIRST_SUMS + OUT_UNITS)
            act_rms(act, k, k.x, k.normed_x)
            act_turn(act, k)
            split_units(act, k, "act", act_split, IN_UNITS, act_take_proj(act, k))
            act_odd_attention(act, k)
            act_turn(act, k)
            split_units(act, k, "act", act_split, OUT_UNITS, last=True)

        @block.vector
        def _(dve):
            dve.sem_inc(k.lo_ready, BLOCKS)
            dve.sem_inc(k.evacuated, 2 * BLOCKS)
            dve.sem_inc(k.f_lo_ready, 2)
            dve.wait_ge(*k.consts_in.next("dve", 16))
            dve.wait_ge(*k.x_in.next("dve", 16))
            nc.vector.memset(k.rstd[:], 0.0).then_inc(*k.turn_source.up(BLOCKS))
            for c in range(HI_SLOTS):
                dve_split(dve, k, 0, c)
            dve_positions(dve, k)
            for l in range(DEPTH):
                dve_turn(dve, k)
                dve_scale_residual(dve, k)
                split_units(dve, k, "dve", dve_split, IN_UNITS)
                dve_conv(dve, k)
                dve_hgrn(dve, k, l)
                dve_retention(dve, k)
                dve_turn(dve, k)
                split_units(dve, k, "dve", dve_split, OUT_UNITS, dve_take_residual(dve, k))
                dve_layer_norm(dve, k, OUT_UNITS, k.turn_source)
                dve_turn(dve, k)
                dve_scale_residual(dve, k)
                dve_feed_forward(dve, k, l)
                dve_layer_norm(dve, k, FF_GROUPS * OUT_UNITS, k.turn_source if l < DEPTH - 1 else k.normed)
            dve.wait_ge(*k.row_in.next("dve", 32))
            dve_rms(dve, k, k.mem, k.mem_normed, k.shift)
            dve_turn(dve, k)
            split_units(dve, k, "dve", dve_split, MEM_UNITS)
            dve_rms(dve, k, k.x, k.normed_x, k.gain)
            dve_turn(dve, k)
            dve_gate_columns(dve, k)
            split_units(dve, k, "dve", dve_split, EVEN_UNITS)
            split_units(dve, k, "dve", dve_split, IN_UNITS - EVEN_UNITS)
            dve_even_attention(dve, k)
            dve_delta(dve, k)
            dve_turn(dve, k)
            split_units(dve, k, "dve", dve_split, OUT_UNITS, dve_take_residual(dve, k))
            dve.wait_ge(*k.row_in.next("dve", 16))
            dve_rms(dve, k, k.x, k.normed_x, k.gain)
            dve_turn(dve, k)
            split_units(dve, k, "dve", dve_split, IN_UNITS)
            dve_odd_attention(dve, k)
            dve_turn(dve, k)
            split_units(dve, k, "dve", dve_split, OUT_UNITS, dve_take_residual(dve, k), last=True)

        @block.tensor
        def _(pe):
            pe.sem_inc(k.block_done, HI_SLOTS)
            pe.sem_inc(k.f_turned, 2)
            pe.wait_ge(*k.consts_in.next("pe", 16))
            for l in range(DEPTH):
                pe_turn(pe, k, x_tile(k))
                pe_units(pe, k, IN_UNITS)
                pe_conv(pe, k)
                pe_hgrn(pe, k, l)
                pe_retention(pe, k)
                pe_turn(pe, k, first_mix_tile(k))
                pe_units(pe, k, OUT_UNITS)
                pe_turn(pe, k, x_tile(k))
                pe_feed_forward(pe, k, l)
            pe_turn(pe, k, rows_tile(k.mem_normed))
            pe_units(pe, k, MEM_UNITS)
            pe_turn(pe, k, rows_tile(k.normed_x))
            pe_gate_columns(pe, k)
            pe_units(pe, k, EVEN_UNITS)
            pe_units(pe, k, IN_UNITS - EVEN_UNITS)
            pe_even_attention(pe, k)
            pe_delta(pe, k)
            pe_turn(pe, k, even_mix_tile(k))
            pe_units(pe, k, OUT_UNITS)
            pe_turn(pe, k, rows_tile(k.normed_x))
            pe_units(pe, k, IN_UNITS)
            pe_odd_attention(pe, k)
            pe_turn(pe, k, odd_mix_tile(k))
            pe_units(pe, k, OUT_UNITS)

    for old, made in k.taken_over:
        assert old.made == made, old.sem


INPUTS = ("x", "positions", "w_in", "w_dw", "b_dw", "conv_ln_g", "conv_ln_b", "hgrn_lb", "hgrn_norm_g", "ret_gn_g", "ret_gn_b",
          "w_out", "ln1_g", "ln1_b", "w_ff1", "w_ff2", "ln2_g", "ln2_b", "mem_2", "mem_norm_g_2", "e_ln_g_2", "e_w_in_2",
          "e_w_mem_kv_2", "e_w_out_2", "na_q_norm_2", "na_k_norm_2", "na_rpb_2", "dn_conv_w_2", "dn_a_log_2", "dn_dt_bias_2",
          "dn_out_norm_2", "e_mem_q_norm_2", "e_mem_k_norm_2", "o_ln_g_2", "o_w_in_2", "o_w_mem_kv_2", "o_w_out_2",
          "df_q_norm_2", "df_k_norm_2", "df_lambda_2", "df_subln_2", "o_mem_q_norm_2", "o_mem_k_norm_2")


def kernel(**inputs):
    import concourse.bacc as bacc
    from concourse.bass_utils import run_bass_kernel_spmd

    nc = bacc.Bacc("TRN2", target_bir_lowering=False, num_devices=1)
    arrays = {name: np.ascontiguousarray(inputs[name]) for name in INPUTS}
    arrays.update(constants())
    dram = {name: nc.dram_tensor(f"in_{name}_dram", a.shape, mybir.dt.from_np(a.dtype), kind="ExternalInput").ap()
            for name, a in arrays.items()}
    out = nc.dram_tensor("out_0_dram", (1, SEQ, D), F32, kind="ExternalOutput").ap()
    two_blocks_kernel(nc, dram, out)
    result = run_bass_kernel_spmd(nc, [{f"in_{name}_dram": a for name, a in arrays.items()}], core_ids=[0])
    return result.results[0]["out_0_dram"]
```

```python
import math

import numpy as np

import concourse.bass as bass
from concourse import mybir

F32 = mybir.dt.float32
F32R = mybir.dt.float32r
I32 = mybir.dt.int32
ACT = mybir.ActivationFunctionType
ALU = mybir.AluOpType
AX_X = mybir.AxisListType.X

P = 128
SEQ = 256
TT = SEQ // P
D = 2048
KT = D // P
NC = 512
D_FF = 8192
DEPTH = 2
HEADS = 6
HD = 128
HALF = HD // 2
HW = HEADS * HD
CONV_C = 512
CONV_W = 31
D_IN = 2 * CONV_C + 8 * HW
LN_EPS = 1e-5
EPS = 1e-6
ALPHA = (2.0 * DEPTH) ** 0.25

BLOCKS = 8
KB = KT // BLOCKS
HI_SLOTS = 4


class Count:

    def __init__(self, sem, made=0):
        self.sem = sem
        self.made = self.first = made
        self.seen = {}

    def up(self, n=1):
        self.made += n
        return self.sem, n

    def now(self):
        return self.sem, self.made

    def next(self, who, n=1):
        self.seen[who] = self.seen.get(who, self.first) + n
        return self.sem, self.seen[who]


class Core:
    pass


def level_masks():
    s, t = np.arange(P)[:, None], np.arange(P)[None, :]
    out = []
    for n in range(7):
        h = 64 >> n
        out.append((s // (2 * h) == t // (2 * h)) & (s % (2 * h) < h) & (t % (2 * h) >= h))
    return np.stack(out, 1).astype(np.float32)


def retention_mask():
    s, t = np.arange(P)[:, None], np.arange(SEQ)[None, :]
    log_gamma = np.log1p(-(2.0 ** (-5.0 - np.arange(HEADS))))
    m = np.where(t >= s, np.exp(log_gamma[:, None, None] * np.maximum(t - s, 0)), 0.0) * HD ** -0.5
    return m.transpose(1, 0, 2).astype(np.float32)


def constants():
    f32 = np.float32
    eye = np.eye(P, dtype=f32)
    tri = np.triu(np.ones((P, P), f32))
    lev = level_masks()
    inv = (f32(10000.0) ** (-np.arange(HALF, dtype=f32) / f32(HALF))).astype(f32)
    inv2 = (f32(10000.0) ** (-np.arange(0, HD, 2, dtype=f32) / f32(HD))).astype(f32)
    ang = np.arange(SEQ, dtype=f32)[:, None] * inv2[None, :]
    rope = np.stack([np.cos(ang), np.sin(ang)], 1).astype(f32)
    j, v = np.arange(31)[:, None], np.arange(63 + P)[None, :]
    band = ((63 - v + 15) % 64 == j).astype(f32)
    c, k = np.arange(64)[:, None], np.arange(64)[None, :]
    c0 = np.clip(c - 8, 0, 48)
    window = np.where((k >= c0) & (k < c0 + 16), 0.0, -1e30).astype(f32)
    return {
        "c_square": np.concatenate([eye, tri, np.ascontiguousarray(tri.T), np.ones((P, P), f32)], 1),
        "c_levels": np.ascontiguousarray(lev.reshape(P, 7 * P)),
        "c_retention": np.ascontiguousarray(retention_mask().reshape(P, HEADS * SEQ)),
        "c_inv_freq": inv.reshape(1, HALF),
        "c_rope": rope.reshape(SEQ, HD),
        "c_band": band,
        "c_window": np.concatenate([window, window], 0),
        "c_pairs": np.ascontiguousarray((lev + lev.transpose(2, 1, 0)).reshape(P, 7 * P)),
    }


def set_up(nc, dram, out):
    k = Core()
    k.nc, k.dram, k.out = nc, dram, out
    k.at = {}

    def sb(name, address, shape, dtype=F32):
        size = 4 * int(np.prod(shape[1:]))
        return nc.alloc_sbuf_tensor_at("sb_" + name, shape, dtype, offset=base + address)

    def small(name, shape, dtype=F32):
        at = k.small
        k.small += (4 * int(np.prod(shape[1:])) + 31) // 32 * 32
        assert k.small <= k.small_end, name
        return sb(name, at, shape, dtype)

    k.sb, k.sb_small = sb, small
    K = 1024
    base = k.base = 33 * 512
    k.raw = sb("raw", 0, [P, BLOCKS, KB, NC])
    k.w_hi = sb("w_hi", 32 * K, [P, HI_SLOTS, KB, NC], F32R)
    k.w_lo = sb("w_lo", 48 * K, [P, HI_SLOTS, KB, NC], F32R)
    k.x = sb("x", 64 * K, [P, TT, D])
    k.a_hi = sb("a_hi", 80 * K, [P, KT, SEQ], F32R)
    k.a_lo = sb("a_lo", 96 * K, [P, KT, SEQ], F32R)
    k.scratch = 80 * K
    k.p0 = 112 * K
    k.proj = sb("proj", k.p0, [P, TT, D_IN])
    k.f_hi = sb("f_hi", k.p0, [P, KT, SEQ], F32R)
    k.f_lo = sb("f_lo", k.p0 + 16 * K, [P, KT, SEQ], F32R)
    k.relu = sb("relu", k.p0 + 32 * K, [P, 2, TT, NC])
    k.relu2 = sb("relu2", k.p0 + 40 * K, [P, 2, TT, NC])
    t0 = 168 * K
    k.square = sb("square", t0, [P, 4, P])
    k.ident, k.tri, k.tri_t, k.ones = (k.square[:, n, :] for n in range(4))
    k.small, k.small_end = t0 + 2 * K, t0 + 4 * K
    k.stats = small("stats", [P, TT, D // NC, 6])
    k.mv = small("mv", [P, TT, 2])
    k.rstd = small("rstd", [P, TT])
    k.eps = small("eps", [P, 2])
    k.warm = small("warm", [P, 1])
    k.mixer_small = k.small
    k.cos = sb("cos", t0 + 4 * K, [P, TT, HALF])
    k.sin = sb("sin", t0 + 4 * K + 512, [P, TT, HALF])
    k.inv_freq = sb("inv_freq", t0 + 33 * K, [P, HALF])
    k.turns = sb("turns", t0 + 33 * K + 256, [P, TT, HALF])
    k.pos_i = sb("pos_i", t0 + 33 * K + 768, [P, TT], I32)
    k.pos_f = sb("pos_f", t0 + 33 * K + 800, [P, TT])
    k.gain = sb("gain", t0 + 5 * K, [P, D])
    k.shift = sb("shift", t0 + 13 * K, [P, D])
    k.t1 = t0 + 5 * K
    k.t2 = t0 + 21 * K

    k.ps_unit = nc.alloc_psum_tensor("ps_unit", [P, 2, TT, NC], F32)
    k.ps = nc.alloc_psum_tensor("ps_mix", [P, 4, NC], F32)

    def count(*names):
        return (Count(nc.alloc_semaphore(name)) for name in names)

    def later(made, *earlier):
        for old in earlier:
            k.taken_over.append((old, made))
        return (Count(old.sem, made) for old in earlier)

    k.count, k.later, k.taken_over = count, later, []
    k.raw_ready = [nc.alloc_semaphore(f"raw_ready{j}") for j in range(BLOCKS)]
    k.hi_ready = nc.alloc_semaphore("hi_ready")
    k.lo_ready = nc.alloc_semaphore("lo_ready")
    k.block_done = nc.alloc_semaphore("block_done")
    k.evacuated = nc.alloc_semaphore("evacuated")
    k.block0 = dict.fromkeys(("sp", "act", "dve", "pe", "pool"), 0)
    k.relu2_ready = nc.alloc_semaphore("relu2_ready")
    k.f_turned = nc.alloc_semaphore("f_turned")
    k.f_lo_ready = nc.alloc_semaphore("f_lo_ready")
    k.f_hi_ready = nc.alloc_semaphore("f_hi_ready")
    k.stats_ready = nc.alloc_semaphore("stats_ready")
    k.stats_units = 0
    k.consts_in, k.x_in, k.row_in, k.eps_set, k.turn_source = count("consts_in", "x_in", "row_in", "eps_set", "turn_source")
    k.turned, k.turn_hi, k.turn_lo, k.pos_in, k.angles = count("turned", "turn_hi", "turn_lo", "pos_in", "angles")
    k.rotary, k.aggregated, k.root, k.normed, k.dve_step = count("rotary", "aggregated", "root", "normed", "dve_step")
    k.act_step, k.pool_step, k.stored = count("act_step", "pool_step", "stored")
    return k



def sp_units(sp, k, weights, units, column=0):
    first = k.block0["sp"]
    k.block0["sp"] += units * BLOCKS
    with sp.Fori(0, units // 2) as i:
        for s in range(2):
            sp_unit(sp, k, weights, 0, i * (2 * BLOCKS) + first, s, i * (2 * NC) + (column + s * NC))


def sp_unit(sp, k, weights, row, b0, s, column):
    w = weights[row:row + D, :].rearrange("(kt p) n -> p kt n", p=P)
    for j in range(BLOCKS):
        sp.wait_ge(k.lo_ready, b0 + (s * BLOCKS + j + 1))
        sp.dma_start(k.raw[:, j], w[:, KB * j:KB * (j + 1), bass.ds(column, NC)]).then_inc(k.raw_ready[j], 16)


def act_split(act, k, b0, c):
    j, slot = c % BLOCKS, c % HI_SLOTS
    act.wait_ge(k.raw_ready[j], b0 * 2 + 16 * (c // BLOCKS + 1))
    act.wait_ge(k.block_done, b0 + (c + 1))
    k.nc.scalar.activation(k.w_hi[:, slot], k.raw[:, j], ACT.Copy).then_inc(k.hi_ready, 1)


def dve_split(dve, k, b0, c):
    j, slot = c % BLOCKS, c % HI_SLOTS
    dve.wait_ge(k.hi_ready, b0 + (c + 1))
    k.nc.vector.tensor_tensor(k.w_lo[:, slot], k.raw[:, j], k.w_hi[:, slot].bitcast(F32),
                              ALU.subtract).then_inc(k.lo_ready, 1)


def pe_block(pe, k, b0, c, hi, lo):
    s, j, slot = c // BLOCKS % 2, c % BLOCKS, c % HI_SLOTS
    if j == 0:
        pe.wait_ge(k.evacuated, b0 + (c + BLOCKS))
    pe.wait_ge(k.lo_ready, b0 + (BLOCKS + c + 1))
    for n in range(KB):
        kt = KB * j + n
        for t in range(TT):
            tokens = slice(t * P, (t + 1) * P)
            acc = k.ps_unit[:, s, t, :]
            w_hi, w_lo = k.w_hi[:, slot, n, :], k.w_lo[:, slot, n, :]
            k.nc.tensor.matmul(acc, hi[:, kt, tokens], w_hi, start=kt == 0, stop=False)
            k.nc.tensor.matmul(acc, hi[:, kt, tokens], w_lo, start=False, stop=False)
            last = k.nc.tensor.matmul(acc, lo[:, kt, tokens], w_hi, start=False, stop=kt == KT - 1)
    last.then_inc(k.block_done, 1)


def pe_units(pe, k, units, tile=None):
    first = k.block0["pe"]
    k.block0["pe"] += units * BLOCKS
    pairs = units // 2
    if tile:
        pe_turn_start(pe, k, tile)
        for c in range(2 * BLOCKS):
            if c < BLOCKS:
                pe_turn_step(pe, k, tile, c)
            pe_block(pe, k, first, c, k.a_hi, k.a_lo)
        first += 2 * BLOCKS
        pairs -= 1
    if pairs:
        with pe.Fori(0, pairs) as i:
            for c in range(2 * BLOCKS):
                pe_block(pe, k, i * (2 * BLOCKS) + first, c, k.a_hi, k.a_lo)


def split_units(eng, k, who, split, units, take=None, last=False):
    first = k.block0[who]
    k.block0[who] += units * BLOCKS
    pairs = units // 2

    def pair(b0, i, ending):
        for s in range(2):
            for c in range(HI_SLOTS, HI_SLOTS + BLOCKS):
                if take and c == HI_SLOTS + BLOCKS - 1:
                    take(b0, s, i)
                if not (ending and s == 1 and c >= BLOCKS):
                    split(eng, k, b0, s * BLOCKS + c)

    loops = pairs - 1 if last else pairs
    if loops:
        with eng.Fori(0, loops) as i:
            pair(i * (2 * BLOCKS) + first, i, False)
    if last:
        pair(first + loops * 2 * BLOCKS, loops, True)


def no_blocks(n):
    pass


class Meanwhile:

    def __init__(self, eng, k, who, block, units, take=None):
        self.eng, self.k, self.block, self.take = eng, k, block, take
        self.ahead = 0 if who == "pe" else HI_SLOTS
        self.first = k.block0[who]
        k.block0[who] += units * BLOCKS
        self.done, self.blocks = 0, units * BLOCKS

    def __call__(self, n):
        for _ in range(n):
            c = self.done
            assert c < self.blocks
            if self.ahead:
                self.block(self.eng, self.k, self.first, c + self.ahead)
            else:
                self.block(self.eng, self.k, self.first, c, self.k.a_hi, self.k.a_lo)
            self.done += 1
            unit = c // BLOCKS
            if self.take and self.done % BLOCKS == 0:
                self.take(self.first + unit // 2 * 2 * BLOCKS, unit % 2, unit // 2)

    def rest(self):
        self(self.blocks - self.done)

    def evacuated(self, units):
        return self.k.evacuated, 2 * BLOCKS + self.first + units * BLOCKS


def wait_unit(eng, k, b0, s):
    eng.wait_ge(k.block_done, b0 + (HI_SLOTS + (s + 1) * BLOCKS))


def act_take_proj(act, k, column=0):
    def take(b0, s, i):
        wait_unit(act, k, b0, s)
        k.nc.scalar.activation(k.proj[:, :, bass.ds(i * (2 * NC) + (column + s * NC), NC)], k.ps_unit[:, s],
                               ACT.Copy).then_inc(k.evacuated, BLOCKS)
    return take


def dve_take_residual(dve, k):
    def take(b0, s, i):
        residual(dve, k, b0, s, i * 2 + s)
    return take


def residual(dve, k, b0, u, chunk):
    wait_unit(dve, k, b0, u)
    cols = bass.ds(chunk * NC, NC)
    k.nc.vector.tensor_tensor(k.x[:, :, cols], k.x[:, :, cols], k.ps_unit[:, u % 2],
                              ALU.add).then_inc(k.evacuated, BLOCKS)
    dve.wait_ge(k.evacuated, b0 + (u + 3) * BLOCKS)
    for t in range(TT):
        last = k.nc.vector.bn_stats(k.stats[:, t, bass.ds(chunk, 1), :].rearrange("p c s -> p (c s)"), k.x[:, t, cols])
    last.then_inc(k.stats_ready, 1)


def pe_turn_bank(pe, k, tile, g):
    pe.wait_ge(*k.turn_source.next("pe"))
    if g >= 4:
        pe.wait_ge(*k.turn_lo.next("pe bank"))
    bank = k.ps[:, g % 4, :].rearrange("p (a s) -> p a s", a=KB)
    for n in range(KB):
        for t in range(TT):
            last = k.nc.tensor.transpose(bank[:, n, t * P:(t + 1) * P], tile(KB * g + n, t), k.ident)
    last.then_inc(*k.turned.up())


def pe_turn_start(pe, k, tile):
    for g in range(4):
        pe_turn_bank(pe, k, tile, g)


def pe_turn_step(pe, k, tile, j):
    for g in ((), (4,), (5,), (6, 7))[j] if j < 4 else ():
        pe_turn_bank(pe, k, tile, g)
    pe.wait_ge(*k.turn_lo.next("pe"))
    if j == BLOCKS - 1:
        k.turn_lo.next("pe bank", 4)


def pe_turn_end(pe, k):
    pe.wait_ge(*k.turn_lo.next("pe", BLOCKS))
    k.turn_lo.next("pe bank", 4)


def act_turn_bank(act, k, g):
    act.wait_ge(*k.turned.next("act"))
    k.nc.scalar.activation(k.a_hi[:, KB * g:KB * (g + 1), :],
                           k.ps[:, g % 4, :].rearrange("p (a s) -> p a s", a=KB), ACT.Copy).then_inc(*k.turn_hi.up())


def act_turn(act, k):
    for g in range(BLOCKS):
        act_turn_bank(act, k, g)


def dve_turn_bank(dve, k, g):
    dve.wait_ge(*k.turn_hi.next("dve"))
    part = slice(KB * g, KB * (g + 1))
    k.nc.vector.tensor_tensor(k.a_lo[:, part, :], k.ps[:, g % 4, :].rearrange("p (a s) -> p a s", a=KB),
                              k.a_hi[:, part, :].bitcast(F32), ALU.subtract).then_inc(*k.turn_lo.up())


def dve_turn_behind(dve, k):
    def after(chunk):
        banks = range(2 * chunk - 2, 2 * chunk) if chunk else ()
        for g in (*banks, *((6, 7) if chunk == D // NC - 1 else ())):
            dve_turn_bank(dve, k, g)
    return after


def dve_turn(dve, k):
    for g in range(BLOCKS):
        dve_turn_bank(dve, k, g)


def pool_rows(pool, k, *rows):
    for row, to in zip(rows, (k.gain, k.shift)):
        pool.dma_start(to[:], row.partition_broadcast(P)).then_inc(*k.row_in.up(16))


def no_step(chunk):
    pass


def dve_layer_norm(dve, k, units, done, run=no_blocks, after=no_step):
    v = k.nc.vector
    k.stats_units += units
    dve.wait_ge(k.stats_ready, k.stats_units)
    for t in range(TT):
        last = v.bn_aggr(k.mv[:, t, :], k.stats[:, t].rearrange("p c s -> p (c s)"))
    last.then_inc(*k.aggregated.up())
    run(2)
    dve.wait_ge(*k.root.next("dve"))
    v.reciprocal(k.rstd[:], k.rstd[:]).then_inc(*k.dve_step.up())
    dve.wait_ge(*k.row_in.next("dve", 32))
    dve.wait_ge(*k.dve_step.now())
    for c in range(D // NC):
        cols = slice(c * NC, (c + 1) * NC)
        for t in range(TT):
            last = v.scalar_tensor_tensor(k.x[:, t, cols], k.x[:, t, cols], k.mv[:, t, 0:1], k.gain[:, cols],
                                          ALU.subtract, ALU.mult)
        last.then_inc(*k.dve_step.up())
        run(1)
        dve.wait_ge(*k.dve_step.now())
        for t in range(TT):
            last = v.scalar_tensor_tensor(k.x[:, t, cols], k.x[:, t, cols], k.rstd[:, t:t + 1], k.shift[:, cols],
                                          ALU.mult, ALU.add)
        last.then_inc(*done.up(2))
        run(1)
        after(c)


def act_sqrt_table(k):
    k.nc.scalar.activation(k.warm[:], k.eps[:, 0:1], ACT.Sqrt)


def act_layer_norm(act, k):
    act_sqrt_table(k)
    act.wait_ge(*k.aggregated.next("act"))
    k.nc.scalar.activation(k.rstd[:], k.mv[:, :, 1], ACT.Sqrt, bias=k.eps[:, 0:1]).then_inc(*k.root.up())


def dve_scale_residual(dve, k):
    dve.wait_ge(*k.turn_lo.now())
    k.nc.vector.tensor_scalar(k.x[:], k.x[:], ALPHA, None, ALU.mult).then_inc(*k.dve_step.up())
    dve.wait_ge(*k.dve_step.now())


FF_GROUPS = D_FF // D
FF_UNITS = 2 * (D // NC)


def sp_feed_forward(sp, k, w1, w2):
    first = k.block0["sp"]
    k.block0["sp"] += FF_GROUPS * FF_UNITS * BLOCKS
    w2_groups = w2.rearrange("(q kt p) n -> p q kt n", kt=KT, p=P)
    w1_rows = w1.rearrange("(kt p) n -> p kt n", p=P)
    with sp.Fori(0, FF_GROUPS) as q:
        b0 = q * (FF_UNITS * BLOCKS) + first
        for u in range(FF_UNITS):
            for j in range(BLOCKS):
                rows = slice(KB * j, KB * (j + 1))
                if u < 4:
                    src = w1_rows[:, rows, bass.ds(q * D + u * NC, NC)]
                else:
                    src = w2_groups[:, bass.ds(q, 1), rows, (u - 4) * NC:(u - 3) * NC].rearrange("p q kt n -> p (q kt) n")
                sp.wait_ge(k.lo_ready, b0 + (u * BLOCKS + j + 1))
                sp.dma_start(k.raw[:, j], src).then_inc(k.raw_ready[j], 16)


def pe_feed_forward(pe, k, layer, tile, between=None):
    first = k.block0["pe"]
    k.block0["pe"] += FF_GROUPS * FF_UNITS * BLOCKS
    done = layer * FF_GROUPS * 4

    def turn(n, u):
        pe.wait_ge(k.relu2_ready, n + (u + 3))
        pe.wait_ge(k.f_lo_ready, n + (u + 1))
        for kt in range(4):
            bank = k.ps[:, 2 * (u % 2) + kt // 2, :].rearrange("p (a s) -> p a s", a=2)
            for t in range(TT):
                last = k.nc.tensor.transpose(bank[:, kt % 2, t * P:(t + 1) * P],
                                             k.relu2[:, u % 2, t, kt * P:(kt + 1) * P], k.ident)
        last.then_inc(k.f_turned, 1)

    def group(q, g0, between=None):
        b0 = q * (FF_UNITS * BLOCKS) + (first + g0 * FF_UNITS * BLOCKS)
        n = q * 4 + (done + g0 * 4)
        for u in range(FF_UNITS):
            hi, lo = (k.a_hi, k.a_lo) if u < 4 else (k.f_hi, k.f_lo)
            for j in range(BLOCKS):
                if u == 4 and j == 0:
                    pe.wait_ge(k.f_lo_ready, n + 5)
                if j == 4 and 1 <= u <= 4:
                    turn(n, u - 1)
                if u == 4 and j == 6:
                    pe.wait_ge(k.f_lo_ready, n + 6)
                if between:
                    between(u, j)
                pe_block(pe, k, b0, u * BLOCKS + j, hi, lo)

    def turn_step(u, j):
        if u == 0:
            pe_turn_step(pe, k, tile, j)

    pe_turn_start(pe, k, tile)
    group(0, 0, turn_step)
    with pe.Fori(0, FF_GROUPS - (2 if between else 1)) as q:
        group(q, 1)
    if between:
        group(0, FF_GROUPS - 1, between)


def turned_unit(k, u):
    return k.ps[:, 2 * (u % 2):2 * (u % 2) + 2, :].rearrange("p b (a s) -> p (b a) s", a=2)


def act_feed_forward(act, k, layer, between=None):
    first = k.block0["act"]
    k.block0["act"] += FF_GROUPS * FF_UNITS * BLOCKS
    done = layer * FF_GROUPS * 4
    def group(q, between=None):
        b0 = q * (FF_UNITS * BLOCKS) + first
        n = q * 4 + done
        for u in range(FF_UNITS):
            for j in range(4, 8):
                act_split(act, k, b0, u * BLOCKS + j)
                if between:
                    between(u, j - 4)
            if 1 <= u <= 4:
                act.wait_ge(k.f_turned, n + (u + 2))
                k.nc.scalar.activation(k.f_hi[:, 4 * (u - 1):4 * u, :], turned_unit(k, u - 1),
                                       ACT.Copy).then_inc(k.f_hi_ready, 1)
            for j in range(8, 12):
                act_split(act, k, b0, u * BLOCKS + j)
                if between:
                    between(u, j - 4)
            if u < 4:
                wait_unit(act, k, b0, u)
                act.wait_ge(k.relu2_ready, n + (u + 1))
                k.nc.scalar.activation(k.relu[:, u % 2], k.ps_unit[:, u % 2], ACT.Relu).then_inc(k.evacuated, BLOCKS)

    with act.Fori(0, FF_GROUPS - 1 if between else FF_GROUPS) as q:
        group(q)
    if between:
        group(FF_GROUPS - 1, between)


def pool_feed_forward(pool, k, layer):
    first = k.block0["pool"]
    k.block0["pool"] += FF_GROUPS * FF_UNITS * BLOCKS
    done = layer * FF_GROUPS * 4
    with pool.Fori(0, FF_GROUPS) as q:
        b0 = q * (FF_UNITS * BLOCKS) + first
        n = q * 4 + done
        for u in range(4):
            pool.wait_ge(k.evacuated, b0 + (u + 3) * BLOCKS)
            pool.wait_ge(k.f_turned, n + (u + 1))
            k.nc.gpsimd.tensor_tensor(k.relu2[:, u % 2], k.relu[:, u % 2], k.relu[:, u % 2],
                                      ALU.mult).then_inc(k.relu2_ready, 1)


def dve_feed_forward(dve, k, layer, between=None):
    first = k.block0["dve"]
    k.block0["dve"] += FF_GROUPS * FF_UNITS * BLOCKS
    done = layer * FF_GROUPS * 4
    def group(q, between=None):
        b0 = q * (FF_UNITS * BLOCKS) + first
        n = q * 4 + done
        for u in range(FF_UNITS):
            for j in range(4, 8):
                dve_split(dve, k, b0, u * BLOCKS + j)
                if between:
                    between(u, j - 4)
            if 1 <= u <= 4:
                dve.wait_ge(k.f_hi_ready, n + u)
                part = slice(4 * (u - 1), 4 * u)
                k.nc.vector.tensor_tensor(k.f_lo[:, part, :], turned_unit(k, u - 1), k.f_hi[:, part, :].bitcast(F32),
                                          ALU.subtract).then_inc(k.f_lo_ready, 1)
            for j in range(8, 12):
                if u >= 4 and j == 11:
                    residual(dve, k, b0, u, u - 4)
                dve_split(dve, k, b0, u * BLOCKS + j)
                if between:
                    between(u, j - 4)

    with dve.Fori(0, FF_GROUPS - 1 if between else FF_GROUPS) as q:
        group(q)
    if between:
        group(FF_GROUPS - 1, between)


CA, CG = 0, CONV_C
HQ, HF, HI, HG = (2 * CONV_C + n * HW for n in range(4))
RQ, RK, RV, RG = (2 * CONV_C + (4 + n) * HW for n in range(4))
LEVELS = 7
LOG_LB_MAX = math.log(1 - 1e-6)
LOG_1M_LB_MIN = math.log(1e-6)
CONV_T = CONV_W - 1 + SEQ
DVE_CONV = CONV_C // P - 1
LATE = 4


def first_mix_tile(k):
    def tile(kt, t):
        at = P * kt if kt < 4 else HQ + P * (kt - 4) if kt < 10 else RQ + P * (kt - 10)
        return k.proj[:, t, at:at + P]
    return tile


def first_buffers(k):
    K = 1024
    w, t1, t2 = k.scratch, k.t1, k.t2
    k.conv_rows = k.sb("conv_rows", t1, [CONV_W + 1, CONV_C])
    k.conv_gain = k.sb("conv_gain", t1 + 2 * K, [P, CONV_C])
    k.conv_shift = k.sb("conv_shift", t1 + 4 * K, [P, CONV_C])
    k.conv_u = k.sb("conv_u", t1 + 6 * K, [P, CONV_C // P, CONV_T])
    k.conv_y = k.sb("conv_y", t1 + 11 * K, [P, CONV_C // P, SEQ])
    k.conv_work = k.sb("conv_work", t1, [P, 2, SEQ])
    k.conv_w = k.sb("conv_w", t1 + 15 * K, [P, CONV_C // P, CONV_W + 1])
    n = HEADS * SEQ
    k.h_cum = k.sb("h_cum", t1, [P, n])
    k.h_d0 = k.sb("h_d0", t1 + 6 * K, [P, n])
    k.h_s = k.sb("h_s", t2, [P, 3 * HEADS, P])
    k.h_lf = k.sb("h_lf", t2, [P, n])
    k.h_lb_rows = k.sb("h_lb_rows", t2 + 6 * K, [DEPTH, HW])
    k.h_gain = k.sb("h_gain", t2 + 9 * K, [P, HW])
    k.h_d1 = k.sb("h_d1", t2 + 12 * K, [P, n])
    k.h_k, k.h_q = k.proj[:, :, HF:HF + HW], k.proj[:, :, HQ:HQ + HW]
    k.h_lb = k.sb_small("h_lb", [P, HEADS, DEPTH])
    k.h_log = k.sb_small("h_log", [P, 4, HEADS])
    k.h_ms = k.sb_small("h_ms", [P, TT * HEADS])
    k.conv_stats = k.sb_small("conv_stats", [P, TT, 6])
    k.conv_mv = k.sb_small("conv_mv", [P, TT, 2])
    k.conv_rstd = k.sb_small("conv_rstd", [P, TT])
    k.mem = k.sb("mem", t2, [P, TT, D])
    k.mem_gain = k.sb("mem_gain", k.p0 + 48 * K, [P, D])
    k.mem_stats = k.sb_small("mem_stats", [P, TT, D // NC, 6])
    k.mem_mv = k.sb_small("mem_mv", [P, TT, 2])
    k.mem_root = k.sb_small("mem_root", [P, TT])
    k.r_s = k.sb("r_s", t2, [P, HEADS, 3 * P])
    k.r_mask = k.sb("r_mask", t2 + 9 * K, [P, HEADS, SEQ])
    k.r_gain = k.sb("r_gain", t2 + 15 * K, [P, HW])
    k.r_shift = k.sb("r_shift", t1, [P, HW])
    k.r_work = k.sb("r_work", t1 + 12 * K, [P, 2, HEADS, HALF])
    k.r_stats = k.sb_small("r_stats", [P, TT * HEADS, 6])
    k.r_mv = k.sb_small("r_mv", [P, TT * HEADS, 2])
    k.r_rstd = k.sb_small("r_rstd", [P, TT * HEADS])
    count = k.count
    k.conv_pool, = count("conv_pool")
    k.conv_pad, k.conv_gate, k.h_gate, k.h_qsilu, k.r_gate = count("conv_pad", "conv_gate", "h_gate", "h_qsilu", "r_gate")
    k.conv_weights, k.conv_gated, k.conv_turned, k.conv_back, k.conv_var = \
        count("conv_weights", "conv_gated", "conv_turned", "conv_back", "conv_var")
    k.conv_root, k.conv_linear, k.conv_done, k.h_fT, k.h_f_read = \
        count("conv_root", "conv_linear", "conv_done", "h_fT", "h_f_read")
    k.h_kx, k.h_key, k.h_qT, k.h_query, k.h_cumulated = count("h_kx", "h_key", "h_qT", "h_query", "h_cumulated")
    k.h_o, k.h_square, k.h_msq, k.h_root, k.h_gated = count("h_o", "h_square", "h_msq", "h_root", "h_gated")
    k.r_roped, k.r_rope_free, k.r_qT, k.r_q, k.r_kT = count("r_roped", "r_rope_free", "r_qT", "r_q", "r_kT")
    k.r_k, k.r_o, k.r_var, k.r_root, k.r_key_roped = count("r_k", "r_o", "r_var", "r_root", "r_key_roped")
    k.conv_tap, k.h_rel, k.h_decay, k.h_factors, k.h_scores = count("conv_tap", "h_rel", "h_decay", "h_factors", "h_scores")
    k.h_score_kept, k.r_scores, k.r_kept, k.conv_rows_in, k.conv_norm_in = \
        count("h_score_kept", "r_scores", "r_kept", "conv_rows_in", "conv_norm_in")
    k.h_gain_in, k.h_mask_in, k.r_rows_in, k.h_lb_in, k.h_softplus = \
        count("h_gain_in", "h_mask_in", "r_rows_in", "h_lb_in", "h_softplus")
    k.h_softplus2, k.h_delta, k.h_lb_log, k.h_lbT = count("h_softplus2", "h_delta", "h_lb_log", "h_lbT")


def head_view(ap):
    return ap.rearrange("p (h s) -> p h s", h=HEADS)


def in_halves(buffer):
    return buffer[:].rearrange("p (x n) -> p x n", x=2)


def tile_of(halves, n):
    x, n = divmod(n, HEADS)
    return halves[:, x, n * P:(n + 1) * P]


def head_of(halves, h):
    x, h = divmod(h, HEADS // 2)
    return halves[:, x, h * SEQ:(h + 1) * SEQ]


def level_mask(k, n):
    return k.proj[:, n // 4, CG + n % 4 * P:CG + (n % 4 + 1) * P]


def dve_positions(dve, k):
    v = k.nc.vector

    def step(ins):
        ins.then_inc(*k.dve_step.up())
        dve.wait_ge(*k.dve_step.now())

    dve.wait_ge(k.pos_in.sem, 32)
    step(v.tensor_copy(k.pos_f[:], k.pos_i[:]))
    for t in range(TT):
        last = v.tensor_scalar(k.cos[:, t, :], k.inv_freq[:], k.pos_f[:, t:t + 1], None, ALU.mult)
    step(last)
    near = 1.5 * 2.0 ** 23
    step(v.tensor_scalar(k.turns[:], k.cos[:], 1 / (2 * math.pi), None, ALU.mult))
    step(v.tensor_scalar(k.turns[:], k.turns[:], near, None, ALU.add))
    step(v.tensor_scalar(k.turns[:], k.turns[:], near, None, ALU.subtract))
    first, second = 6.28125, 2029 / 2.0 ** 20
    for part in (first, second, 2 * math.pi - first - second):
        step(v.scalar_tensor_tensor(k.cos[:], k.turns[:], -part, k.cos[:], ALU.mult, ALU.add))
    pi = 3.1415925
    step(v.tensor_scalar(k.sin[:], k.cos[:], pi, -pi, ALU.min, ALU.max))
    step(v.tensor_scalar(k.cos[:], k.cos[:], math.pi / 2, None, ALU.add))
    step(v.tensor_scalar(k.turns[:], k.cos[:], math.pi, -2 * math.pi, ALU.is_gt, ALU.mult))
    step(v.tensor_tensor(k.cos[:], k.cos[:], k.turns[:], ALU.add))
    v.tensor_scalar(k.cos[:], k.cos[:], pi, -pi, ALU.min, ALU.max).then_inc(*k.angles.up())


def act_positions(act, k):
    act.wait_ge(*k.angles.next("act"))
    k.nc.scalar.activation(k.sin[:], k.sin[:], ACT.Sin)
    k.nc.scalar.activation(k.cos[:], k.cos[:], ACT.Sin).then_inc(*k.rotary.up())


def pool_first_rows(pool, k, l):
    d = k.dram
    with k.nc.allow_non_contiguous_dma(reason="short rows"):
        pool.dma_start(k.conv_rows[0:CONV_W, :], d["w_dw"][l]).then_inc(*k.conv_rows_in.up(16))
        pool.dma_start(k.conv_rows[CONV_W:CONV_W + 1, :], d["b_dw"][l:l + 1, :]).then_inc(*k.conv_rows_in.up(16))
        pool.dma_start(k.conv_gain[:], d["conv_ln_g"][l].partition_broadcast(P)).then_inc(*k.conv_norm_in.up(16))
        pool.dma_start(k.conv_shift[:], d["conv_ln_b"][l].partition_broadcast(P)).then_inc(*k.conv_norm_in.up(16))
        pool.dma_start(k.h_gain[:], d["hgrn_norm_g"][l].partition_broadcast(P)).then_inc(*k.h_gain_in.up(16))
        if l:
            pool.dma_start(k.h_lb_rows[:], d["hgrn_lb"]).then_inc(*k.h_lb_in.up(16))
    k.nc.gpsimd.memset(k.conv_u[:, :, 0:CONV_W - 1], 0.0).then_inc(*k.conv_pad.up())
    pool.wait_ge(*k.conv_gated.next("pool"))
    masks = d["c_levels"].rearrange("p (n t) -> p n t", n=LEVELS)
    for t, first, end in ((0, 0, 4), (1, 4, LEVELS)):
        to = k.proj[:, t, CG:CG + (end - first) * P].rearrange("p (n i) -> p n i", n=end - first)
        pool.dma_start(to, masks[:, first:end, :]).then_inc(*k.h_mask_in.up(16))



def act_conv(act, k, l, run):
    a = k.nc.scalar
    act.wait_ge(*run.evacuated(0))
    cg = k.proj[:, :, CG:CG + CONV_C]
    a.activation(cg, cg, ACT.Sigmoid).then_inc(*k.conv_gate.up())
    run(28)
    act_hgrn_gates(act, k, l, run)
    upto(run, 40 + LATE * l)
    act.wait_ge(*k.conv_var.next("act"))
    a.activation(k.conv_rstd[:], k.conv_mv[:, :, 1], ACT.Sqrt, bias=k.eps[:, 0:1]).then_inc(*k.conv_root.up())
    run(2)
    act.wait_ge(*k.conv_linear.next("act"))
    ca = k.proj[:, :, CA:CA + CONV_C]
    a.activation(ca, ca, ACT.Silu).then_inc(*k.conv_done.up())


def pool_conv(pool, k):
    g = k.nc.gpsimd

    def step(ins):
        ins.then_inc(*k.pool_step.up())
        pool.wait_ge(*k.pool_step.now())

    def weight(n):
        return k.conv_w[:, DVE_CONV, n:n + 1].to_broadcast([P, SEQ])

    y = k.conv_y[:, DVE_CONV, :]
    pool.wait_ge(*k.conv_tap.next("pool"))
    k.conv_tap.next("pool", DVE_CONV * CONV_W - 1)
    step(g.tensor_tensor(y, k.conv_u[:, DVE_CONV, 0:SEQ], weight(0), ALU.mult))
    g.tensor_tensor(k.conv_work[:, 1, :], k.conv_u[:, DVE_CONV, 1:1 + SEQ], weight(1), ALU.mult)
    step(g.tensor_tensor(y, y, weight(CONV_W), ALU.add))
    for tap in range(1, CONV_W):
        if tap + 1 < CONV_W:
            g.tensor_tensor(k.conv_work[:, (tap + 1) % 2, :], k.conv_u[:, DVE_CONV, tap + 1:tap + 1 + SEQ], weight(tap + 1),
                            ALU.mult)
        last = g.tensor_tensor(y, y, k.conv_work[:, tap % 2, :], ALU.add)
        if tap + 1 < CONV_W:
            step(last)
    last.then_inc(*k.conv_pool.up())


def pe_conv(pe, k, l, run):
    run(4)
    pe.wait_ge(*k.conv_rows_in.next("pe", 32))
    for c in range(4):
        last = k.nc.tensor.transpose(k.ps[:, 0, c * 32:(c + 1) * 32], k.conv_rows[:, c * P:(c + 1) * P],
                                     k.ident[0:CONV_W + 1, 0:CONV_W + 1])
    last.then_inc(*k.conv_weights.up())
    pe.wait_ge(*k.conv_gated.next("pe"))
    for c in range(4):
        for t in range(TT):
            last = k.nc.tensor.transpose(k.ps[:, 1 + c // 2, (c % 2) * SEQ + t * P:(c % 2) * SEQ + (t + 1) * P],
                                         k.proj[:, t, CA + c * P:CA + (c + 1) * P], k.ident)
    last.then_inc(*k.conv_turned.up())
    run(22)
    pe.wait_ge(*k.conv_tap.next("pe", 1))
    pe_hgrn_gates(pe, k, l, run)
    upto(run, 38 + LATE * l)
    pe.wait_ge(*k.h_kx.next("pe"))
    pe.wait_ge(*k.conv_tap.next("pe", DVE_CONV * CONV_W - 1))
    pe.wait_ge(*k.conv_pool.next("pe"))
    for t in range(TT):
        for c in range(4):
            last = k.nc.tensor.transpose(k.ps[:, 1 + t, c * P:(c + 1) * P], k.conv_y[:, c, t * P:(t + 1) * P], k.ident)
    last.then_inc(*k.conv_back.up())


def dve_conv(dve, k, l, run):
    v = k.nc.vector
    ca = k.proj[:, :, CA:CA + CONV_C]
    dve.wait_ge(*k.conv_gate.next("dve"))
    v.tensor_tensor(ca, ca, k.proj[:, :, CG:CG + CONV_C], ALU.mult).then_inc(*k.conv_gated.up())
    run(5)
    dve.wait_ge(*k.conv_weights.next("dve"))
    v.tensor_copy(k.conv_w[:], k.ps[:, 0, 0:P].rearrange("p (c k) -> p c k", c=4)).then_inc(*k.dve_step.up())
    dve.wait_ge(*k.conv_turned.next("dve"))
    v.tensor_copy(k.conv_u[:, :, CONV_W - 1:CONV_T],
                  k.ps[:, 1:3, :].rearrange("p b (a s) -> p (b a) s", a=2)).then_inc(*k.dve_step.up())
    dve.wait_ge(*k.conv_pad.next("dve"))
    dve.wait_ge(*k.dve_step.now())
    sem, done = k.conv_tap.now()
    for tap in range(CONV_W):
        for c in range(DVE_CONV):
            u, y = k.conv_u[:, c, tap:tap + SEQ], k.conv_y[:, c, :]
            if tap == 0:
                ins = v.tensor_scalar(y, u, k.conv_w[:, c, 0:1], k.conv_w[:, c, CONV_W:CONV_W + 1], ALU.mult, ALU.add)
            else:
                dve.wait_ge(sem, done + DVE_CONV * (tap - 1) + c + 1)
                ins = v.scalar_tensor_tensor(y, u, k.conv_w[:, c, tap:tap + 1], y, ALU.mult, ALU.add)
            ins.then_inc(*k.conv_tap.up())
        run(1)
        dve_hgrn_gates(dve, k, l, tap)
    run(3 + LATE * l)
    dve.wait_ge(*k.conv_back.next("dve"))
    for t in range(TT):
        v.bn_stats(k.conv_stats[:, t, :], k.ps[:, 1 + t, :]).then_inc(*k.dve_step.up())
    dve.wait_ge(*k.dve_step.now())
    for t in range(TT):
        last = v.bn_aggr(k.conv_mv[:, t, :], k.conv_stats[:, t, :])
    last.then_inc(*k.conv_var.up())
    dve.wait_ge(*k.conv_norm_in.next("dve", 32))
    dve.wait_ge(*k.conv_var.now())
    for t in range(TT):
        v.scalar_tensor_tensor(k.proj[:, t, CA:CA + CONV_C], k.ps[:, 1 + t, :], k.conv_mv[:, t, 0:1], k.conv_gain[:],
                               ALU.subtract, ALU.mult).then_inc(*k.dve_step.up())
    run(2)
    dve.wait_ge(*k.conv_root.next("dve"))
    v.reciprocal(k.conv_rstd[:], k.conv_rstd[:]).then_inc(*k.dve_step.up())
    dve.wait_ge(*k.dve_step.now())
    for t in range(TT):
        y = k.proj[:, t, CA:CA + CONV_C]
        last = v.scalar_tensor_tensor(y, y, k.conv_rstd[:, t:t + 1], k.conv_shift[:], ALU.mult, ALU.add)
    last.then_inc(*k.conv_linear.up())



def hgrn_turn(k, at):
    for h in range(HEADS):
        for t in range(TT):
            last = k.nc.tensor.transpose(k.ps[:, h // 2, (h % 2) * SEQ + t * P:(h % 2) * SEQ + (t + 1) * P],
                                         k.proj[:, t, at + h * P:at + (h + 1) * P], k.ident)
    return last


def pe_hgrn_gates(pe, k, l, run):
    if l:
        pe.wait_ge(*k.h_lb_in.next("pe", 16))
        for h in range(HEADS):
            last = k.nc.tensor.transpose(k.ps[:, 3, h * DEPTH:(h + 1) * DEPTH], k.h_lb_rows[:, h * P:(h + 1) * P],
                                         k.ident[0:DEPTH, 0:DEPTH])
        last.then_inc(*k.h_lbT.up())
    pe.wait_ge(*run.evacuated(3))
    hgrn_turn(k, HF).then_inc(*k.h_fT.up())


def pe_hgrn(pe, k, l, run):
    tensor = k.nc.tensor
    upto(run, 43 + LATE * l)
    pe.wait_ge(*k.conv_linear.next("pe"))
    pe.wait_ge(*k.h_qsilu.next("pe"))
    hgrn_turn(k, HQ).then_inc(*k.h_qT.up())
    run(3)

    pe.wait_ge(*k.h_query.next("pe"))
    pe.wait_ge(*k.h_key.next("pe"))
    scores = k.ps[:, 0:3, :].rearrange("p b (a t) -> p (b a) t", a=4)
    for level in range(-1, LEVELS + 1):
        if level < 0:
            left, right = k.h_k, k.h_q
        else:
            run(3)
            left = right = in_halves((k.h_d0, k.h_d1)[level % 2])
            pe.wait_ge(*k.h_factors.next("pe"))
            pe.wait_ge(*k.h_score_kept.next("pe"))
        for n in range(HEADS if level == LEVELS else 2 * HEADS):
            s, t = (2 * n, 2 * n + 1) if level == LEVELS else (n, n)
            last = tensor.matmul(scores[:, n, :], tile_of(left, s), tile_of(right, t), start=True, stop=True)
        last.then_inc(*k.h_scores.up())
    run(2)
    pe.wait_ge(*k.h_score_kept.next("pe"))
    pe.wait_ge(*run.evacuated(5))
    for t in range(TT):
        for h in range(HEADS):
            o = scores[:, t * HEADS + h, :]
            v = slice(HI + h * HD, HI + (h + 1) * HD)
            last = tensor.matmul(o, k.h_s[:, TT * h + t, :], k.proj[:, t, v], start=True, stop=t == 0)
            if t:
                last = tensor.matmul(o, k.h_s[:, TT * HEADS + h, :], k.proj[:, 0, v], start=False, stop=True)
    last.then_inc(*k.h_o.up())


def act_hgrn_gates(act, k, l, run):
    a = k.nc.scalar

    def step(ins):
        ins.then_inc(*k.act_step.up())
        act.wait_ge(*k.act_step.now())

    act.wait_ge(*k.h_f_read.next("act"))
    step(a.activation(k.h_d1[:].rearrange("p (b s) -> p b s", b=3), k.ps[:, 0:3, :], ACT.Abs))
    run(1)
    step(a.activation(k.h_d1[:], k.h_d1[:], ACT.Exp, scale=-1.0))
    a.activation(k.h_d1[:], k.h_d1[:], ACT.Ln, bias=1.0).then_inc(*k.h_softplus.up())
    if l:
        act.wait_ge(*k.h_lb_log.next("act"))
        step(a.activation(k.h_log[:, 3, :], k.h_log[:, 2, :], ACT.Abs))
        step(a.activation(k.h_log[:, 3, :], k.h_log[:, 3, :], ACT.Exp, scale=-1.0))
        a.activation(k.h_log[:, 3, :], k.h_log[:, 3, :], ACT.Ln, bias=1.0).then_inc(*k.h_softplus.up())
    upto(run, 34)
    act.wait_ge(*k.h_kx.next("act"))
    if l == 0:
        a.activation(k.h_k, k.h_k, ACT.Exp).then_inc(*k.h_key.up())
    else:
        act.wait_ge(*k.h_delta.next("act"))
        for h in range(HEADS):
            last = a.activation(head_of(k.h_k, h), head_of(k.h_k, h), ACT.Exp, bias=k.h_log[:, 1, h:h + 1])
        last.then_inc(*k.h_key.up())
        run(1)
        step(a.activation(k.h_d1[:], k.h_lf[:], ACT.Abs))
        run(1)
        step(a.activation(k.h_d1[:], k.h_d1[:], ACT.Exp, scale=-1.0))
        a.activation(k.h_d1[:], k.h_d1[:], ACT.Ln, bias=1.0).then_inc(*k.h_softplus2.up())


def act_hgrn(act, k, l, run):
    a = k.nc.scalar
    act.wait_ge(*run.evacuated(2))
    a.activation(k.h_q, k.h_q, ACT.Silu).then_inc(*k.h_qsilu.up())
    upto(run, 43 + LATE * l)
    for level in range(LEVELS + 1):
        run(3)
        d = (k.h_d0, k.h_d1)[level % 2]
        act.wait_ge(*k.h_rel.next("act"))
        a.activation(d[:], d[:], ACT.Exp).then_inc(*k.h_decay.up())
    run(2)
    act.wait_ge(*run.evacuated(6))
    hg = k.proj[:, :, HG:HG + HW]
    a.activation(hg, hg, ACT.Sigmoid).then_inc(*k.h_gate.up())
    run(4)
    act.wait_ge(*k.h_o.next("act"))
    a.activation(k.h_d0[:].rearrange("p (b s) -> p b s", b=3), k.ps[:, 0:3, :], ACT.Square).then_inc(*k.h_square.up())
    run(2)
    act.wait_ge(*k.h_msq.next("act"))
    a.activation(k.h_ms[:], k.h_ms[:], ACT.Sqrt, scale=1.0 / HD, bias=k.eps[:, 0:1]).then_inc(*k.h_root.up())


def pool_hgrn(pool, k):
    g = k.nc.gpsimd
    pool.wait_ge(*k.h_cumulated.next("pool"))
    for level in range(LEVELS + 1):
        half = 128 if level == LEVELS else 64 >> level
        blocks = HEADS * SEQ // (2 * half)
        if level >= 2:
            pool.wait_ge(*k.h_scores.next("pool", 2 if level == 2 else 1))
        c = k.h_cum[:].rearrange("p (b x s) -> p b x s", b=blocks, x=2)
        d = (k.h_d0, k.h_d1)[level % 2][:].rearrange("p (b x s) -> p b x s", b=blocks, x=2)
        middle = c[:, :, 0, half - 1:half].to_broadcast([P, blocks, half])
        g.tensor_tensor(d[:, :, 0, :], middle, c[:, :, 0, :], ALU.subtract)
        if level == LEVELS:
            last = g.tensor_copy(d[:, :, 1, :], c[:, :, 1, :])
        else:
            last = g.tensor_tensor(d[:, :, 1, :], c[:, :, 1, :], middle, ALU.subtract)
        last.then_inc(*k.h_rel.up())
    k.h_scores.next("pool", 2)


def pool_hgrn_gate(pool, k):
    g = k.nc.gpsimd
    hg = k.proj[:, :, HG:HG + HW]
    pool.wait_ge(*k.h_gain_in.next("pool", 16))
    pool.wait_ge(*k.h_gate.next("pool"))
    g.tensor_tensor(hg, hg, k.h_gain[:].unsqueeze(1).to_broadcast([P, TT, HW]), ALU.mult).then_inc(*k.h_gated.up())


def dve_hgrn_gates(dve, k, l, tap):
    v = k.nc.vector

    def step(ins):
        ins.then_inc(*k.dve_step.up())
        dve.wait_ge(*k.dve_step.now())

    f = k.ps[:, 0:3, :].rearrange("p b s -> p (b s)")
    log_lb, log_1m, delta, work = (k.h_log[:, n, :] for n in range(4))
    if tap == 22:
        dve.wait_ge(*k.h_fT.next("dve"))
        v.tensor_scalar(k.h_lf[:], f, 0.0, None, ALU.min)
        v.tensor_scalar(k.h_k, f.rearrange("p (x n) -> p x n", x=2), 0.0, None, ALU.max).then_inc(*k.h_f_read.up())
        if l:
            dve.wait_ge(*k.h_lbT.next("dve"))
            step(v.tensor_copy(k.h_lb[:], k.ps[:, 3, 0:HEADS * DEPTH].rearrange("p (h n) -> p h n", h=HEADS)))
            v.tensor_tensor(delta, k.h_lb[:, :, 1], k.h_lb[:, :, 0], ALU.subtract).then_inc(*k.h_lb_log.up())
    elif tap == 26:
        dve.wait_ge(*k.h_f_read.now())
        dve.wait_ge(*k.h_softplus.next("dve"))
        step(v.tensor_tensor(k.h_lf[:], k.h_lf[:], k.h_d1[:], ALU.subtract))
    elif tap == 27:
        v.scalar_tensor_tensor(k.h_k, k.h_k, -1.0, in_halves(k.h_d1), ALU.mult, ALU.subtract).then_inc(*k.h_kx.up())
        if l:
            dve.wait_ge(*k.h_softplus.next("dve"))
            v.scalar_tensor_tensor(log_lb, delta, 0.0, work, ALU.min, ALU.subtract)
            step(v.tensor_scalar(log_1m, delta, 0.0, -1.0, ALU.max, ALU.mult))
            step(v.tensor_tensor(log_1m, log_1m, work, ALU.subtract))
            v.tensor_scalar(log_lb, log_lb, LOG_LB_MAX, None, ALU.min)
            step(v.tensor_scalar(log_1m, log_1m, LOG_1M_LB_MIN, None, ALU.max))
            step(v.tensor_tensor(delta, log_1m, log_lb, ALU.subtract))
            for h in range(HEADS):
                last = v.tensor_scalar(head_view(k.h_lf[:])[:, h, :], head_view(k.h_lf[:])[:, h, :], delta[:, h:h + 1], None,
                                       ALU.add)
            last.then_inc(*k.h_delta.up())


def dve_hgrn(dve, k, l, run):
    v = k.nc.vector

    def step(ins):
        ins.then_inc(*k.dve_step.up())
        dve.wait_ge(*k.dve_step.now())

    f = k.ps[:, 0:3, :].rearrange("p b s -> p (b s)")
    dve.wait_ge(*k.conv_linear.now())
    if l:
        log_lb = k.h_log[:, 0, :]
        dve.wait_ge(*k.h_softplus2.next("dve"))
        step(v.tensor_scalar(k.h_lf[:], k.h_lf[:], 0.0, None, ALU.max))
        for h in range(HEADS):
            last = v.scalar_tensor_tensor(head_view(k.h_lf[:])[:, h, :], head_view(k.h_d1[:])[:, h, :],
                                          log_lb[:, h:h + 1], head_view(k.h_lf[:])[:, h, :], ALU.add, ALU.add)
        step(last)
    dve.wait_ge(*k.h_kx.now())
    v.memset(k.h_d0[:], 1.0).then_inc(*k.dve_step.up())
    dve.wait_ge(*k.dve_step.now())
    step(v.memset(k.h_d0[:].rearrange("p (n s) -> p n s", s=P)[:, :, 0:1], 0.0))
    v.tensor_tensor_scan(k.h_cum[:], k.h_d0[:], k.h_lf[:], 0.0, ALU.mult, ALU.add).then_inc(*k.h_cumulated.up())
    upto(run, 44 + LATE * l)
    dve.wait_ge(*k.h_qT.next("dve"))
    v.tensor_copy(k.h_q, f.rearrange("p (x n) -> p x n", x=2)).then_inc(*k.h_query.up())
    dve.wait_ge(*k.h_query.now())
    dve.wait_ge(*k.h_key.next("dve"))
    dve.wait_ge(*k.h_mask_in.next("dve", 32))

    scores = k.ps[:, 0:3, :].rearrange("p b (a t) -> p (b a) t", a=4)
    dve.wait_ge(*k.h_cumulated.now())

    def factors(level):
        half = 128 if level == LEVELS else 64 >> level
        d, q, key = (x.rearrange("p y (b x s) -> p y b x s", x=2, s=half)
                     for x in (in_halves((k.h_d0, k.h_d1)[level % 2]), k.h_q, k.h_k))
        dve.wait_ge(*k.h_decay.next("dve"))
        v.tensor_tensor(d[:, :, :, 0, :], d[:, :, :, 0, :], key[:, :, :, 0, :], ALU.mult)
        v.tensor_tensor(d[:, :, :, 1, :], d[:, :, :, 1, :], q[:, :, :, 1, :], ALU.mult).then_inc(*k.h_factors.up())

    def keep(level):
        dve.wait_ge(*k.h_scores.next("dve"))
        kept = k.h_s[:, 0:2 * HEADS, :]
        if level < 0:
            ins = v.tensor_tensor(kept, scores, k.ident.unsqueeze(1).to_broadcast([P, 2 * HEADS, P]), ALU.mult)
        elif level == LEVELS:
            ins = v.tensor_copy(k.h_s[:, 2 * HEADS:, :], scores[:, 0:HEADS, :])
        else:
            mask = level_mask(k, level).unsqueeze(1).to_broadcast([P, 2 * HEADS, P])
            ins = v.copy_predicated(kept, mask.bitcast(I32), scores)
        ins.then_inc(*k.h_score_kept.up())
        dve.wait_ge(*k.h_score_kept.now())

    for level in range(-1, LEVELS):
        run(3)
        factors(level + 1)
        keep(level)
    run(3)
    keep(LEVELS)
    run(3)
    dve.wait_ge(*k.h_square.next("dve"))
    v.tensor_reduce(k.h_ms[:], k.h_d0[:].rearrange("p (n e) -> p n e", e=HD), AX_X, ALU.add).then_inc(*k.h_msq.up())
    dve.wait_ge(*k.h_gated.next("dve"))
    y = k.proj[:, :, HQ:HQ + HW]
    step(v.tensor_tensor(y, k.ps[:, 0:3, :].rearrange("p b s -> p (b s)").rearrange("p (t n) -> p t n", t=TT),
                         k.proj[:, :, HG:HG + HW], ALU.mult))
    run(3)
    dve.wait_ge(*k.h_root.next("dve"))
    step(v.reciprocal(k.h_ms[:], k.h_ms[:]))
    for t in range(TT):
        yt = head_view(k.proj[:, t, HQ:HQ + HW])
        last = v.tensor_tensor(yt, yt, k.h_ms[:, t * HEADS:(t + 1) * HEADS].unsqueeze(2).to_broadcast([P, HEADS, HD]),
                               ALU.mult)
    step(last)


def pairs_at(buffer, at):
    return lambda p: buffer[:, :, at + p * 2 * HD:at + (p + 1) * 2 * HD]


def turned_head(buffer, at, n):
    return buffer[:, n % 2, at + n // 2 * SEQ:at + (n // 2 + 1) * SEQ]


def upto(run, n):
    run(max(min(n, run.blocks) - run.done, 0))


def pool_rotate(pool, k, at):
    g = k.nc.gpsimd

    def step(ins):
        ins.then_inc(*k.pool_step.up())
        pool.wait_ge(*k.pool_step.now())

    for t in range(TT):
        x = k.proj[:, t, at:at + HW].rearrange("p (h x s) -> p h x s", h=HEADS, x=2)
        x1, x2 = x[:, :, 0, :], x[:, :, 1, :]
        cos, sin = (a[:, t, :].unsqueeze(1).to_broadcast([P, HEADS, HALF]) for a in (k.cos, k.sin))
        w0, w1 = k.r_work[:, 0], k.r_work[:, 1]
        g.tensor_tensor(w0, x2, sin, ALU.mult)
        step(g.tensor_tensor(w1, x1, sin, ALU.mult))
        g.tensor_tensor(x1, x1, cos, ALU.mult)
        step(g.tensor_tensor(x2, x2, cos, ALU.mult))
        g.tensor_tensor(x1, x1, w0, ALU.subtract)
        last = g.tensor_tensor(x2, x2, w1, ALU.add)
        step(last)


def pool_retention(pool, k, l):
    d = k.dram
    pool_hgrn_gate(pool, k)
    pool.wait_ge(k.rotary.sem, 1)
    pool.wait_ge(k.evacuated, 2 * BLOCKS + k.block0["pool"] + RV // NC * BLOCKS)
    pool_rotate(pool, k, RQ)
    pool.sem_inc(*k.r_roped.up())
    pool_rotate(pool, k, RK)
    pool.sem_inc(*k.r_key_roped.up())
    pool.wait_ge(*k.r_rope_free.next("pool"))
    pool.dma_start(k.r_mask[:], d["c_retention"].rearrange("p (h t) -> p h t", h=HEADS)).then_inc(*k.r_rows_in.up(16))
    pool.dma_start(k.r_gain[:], d["ret_gn_g"][l].partition_broadcast(P)).then_inc(*k.r_rows_in.up(16))
    pool.dma_start(k.r_shift[:], d["ret_gn_b"][l].partition_broadcast(P)).then_inc(*k.r_rows_in.up(16))


def pe_retention(pe, k, l, run):
    tensor = k.nc.tensor

    def turn(at, bank):
        for p in range(HEADS // 2):
            for x in range(2):
                for t in range(TT):
                    last = tensor.transpose(k.ps[:, (bank + p) % 4, x * SEQ + t * P:x * SEQ + (t + 1) * P],
                                            pairs_at(k.proj, at)(p)[:, t, x * HD:(x + 1) * HD], k.ident)
        return last

    upto(run, 78 + LATE * l)
    pe.wait_ge(*k.r_rope_free.next("pe"))
    pe.wait_ge(*k.r_roped.next("pe"))
    turn(RQ, 0).then_inc(*k.r_qT.up())
    upto(run, 82 + LATE * l)
    pe.wait_ge(*k.r_key_roped.next("pe"))
    pe.wait_ge(*k.r_q.next("pe"))
    turn(RK, 3).then_inc(*k.r_kT.up())
    upto(run, 84 + LATE * l)
    pe.wait_ge(*k.r_k.next("pe"))
    for h in range(HEADS):
        if h == 4:
            upto(run, 86 + LATE * l)
        if h >= 4:
            pe.wait_ge(*k.r_kept.next("pe"))
        q, key = turned_head(k.proj, RQ, h), turned_head(k.proj, RK, h)
        tensor.matmul(k.ps[:, h % 4, 0:SEQ], key[:, 0:P], q, start=True, stop=True)
        tensor.matmul(k.ps[:, h % 4, SEQ:3 * P], key[:, P:SEQ], q[:, P:SEQ], start=True, stop=True)\
            .then_inc(*k.r_scores.up())
    upto(run, 88 + LATE * l)
    pe.wait_ge(*k.r_kept.next("pe", 4))
    pe.wait_ge(*run.evacuated((RG - HQ + NC - 1) // NC))
    o = k.ps[:, 0:3, :].rearrange("p b (a e) -> p (b a) e", a=4)
    for t in range(TT):
        for h in range(HEADS):
            v = slice(RV + h * HD, RV + (h + 1) * HD)
            last = tensor.matmul(o[:, t * HEADS + h, :], k.r_s[:, h, t * P:(t + 1) * P], k.proj[:, 0, v],
                                 start=True, stop=t == 0)
            if t:
                last = tensor.matmul(o[:, t * HEADS + h, :], k.r_s[:, h, SEQ:3 * P], k.proj[:, 1, v],
                                     start=False, stop=True)
    last.then_inc(*k.r_o.up())
    run.rest()


def act_retention(act, k, l, run):
    a = k.nc.scalar

    def keep(at, bank):
        for p in range(HEADS // 2):
            last = a.activation(pairs_at(k.proj, at)(p), k.ps[:, (bank + p) % 4, :].rearrange("p (a s) -> p a s", a=2), ACT.Copy)
        return last

    upto(run, 79 + LATE * l)
    act.wait_ge(*k.r_qT.next("act"))
    keep(RQ, 0).then_inc(*k.r_q.up())
    upto(run, 83 + LATE * l)
    act.wait_ge(*k.r_kT.next("act"))
    keep(RK, 3).then_inc(*k.r_k.up())
    upto(run, 91 + LATE * l)
    act.wait_ge(*k.r_var.next("act"))
    a.activation(k.r_rstd[:], k.r_mv[:, :, 1], ACT.Sqrt, bias=k.eps[:, 0:1]).then_inc(*k.r_root.up())
    run.rest()
    rg = k.proj[:, :, RG:RG + HW]
    act.wait_ge(*run.evacuated(run.blocks // BLOCKS))
    a.activation(rg, rg, ACT.Silu).then_inc(*k.r_gate.up())


def dve_retention(dve, k, l, run):
    v = k.nc.vector

    def step(ins):
        ins.then_inc(*k.dve_step.up())
        dve.wait_ge(*k.dve_step.now())

    v.memset(k.r_rstd[:], 0.0).then_inc(*k.r_rope_free.up())
    upto(run, 85 + LATE * l)
    dve.wait_ge(*k.r_rows_in.next("dve", 48))
    for h in range(HEADS):
        if h == 4:
            upto(run, 87 + LATE * l)
        dve.wait_ge(*k.r_scores.next("dve"))
        v.tensor_tensor(k.r_s[:, h, 0:SEQ], k.ps[:, h % 4, 0:SEQ], k.r_mask[:, h, :], ALU.mult)
        v.tensor_tensor(k.r_s[:, h, SEQ:3 * P], k.ps[:, h % 4, SEQ:3 * P], k.r_mask[:, h, 0:P], ALU.mult)\
            .then_inc(*k.r_kept.up())
    upto(run, 89 + LATE * l)
    dve.wait_ge(*k.r_o.next("dve"))
    o = k.ps[:, 0:3, :].rearrange("p b (a e) -> p (b a) e", a=4)
    for n in range(TT * HEADS):
        last = v.bn_stats(k.r_stats[:, n, :], o[:, n, :])
    step(last)
    for n in range(TT * HEADS):
        last = v.bn_aggr(k.r_mv[:, n, :], k.r_stats[:, n, :])
    last.then_inc(*k.r_var.up())
    upto(run, 92 + LATE * l)
    dve.wait_ge(*k.r_root.next("dve"))
    step(v.reciprocal(k.r_rstd[:], k.r_rstd[:]))
    for t in range(TT):
        for h in range(HEADS):
            n = t * HEADS + h
            last = v.tensor_scalar(k.proj[:, t, RQ + h * HD:RQ + (h + 1) * HD], o[:, n, :], k.r_mv[:, n, 0:1],
                                   k.r_rstd[:, n:n + 1], ALU.subtract, ALU.mult)
    step(last)
    dve.wait_ge(*k.conv_done.next("dve"))
    dve.sem_inc(*k.turn_source.up(BLOCKS - HEADS // 2))
    y = k.proj[:, :, RQ:RQ + HW]
    step(v.tensor_tensor(y, y, k.r_gain[:].unsqueeze(1).to_broadcast([P, TT, HW]), ALU.mult))
    upto(run, 94 + LATE * l)
    step(v.tensor_tensor(y, y, k.r_shift[:].unsqueeze(1).to_broadcast([P, TT, HW]), ALU.add))
    run.rest()
    dve.wait_ge(*k.r_gate.next("dve"))
    for p in range(HEADS // 2):
        y, gate = pairs_at(k.proj, RQ)(p), pairs_at(k.proj, RG)(p)
        v.tensor_tensor(y, y, gate, ALU.mult).then_inc(*k.turn_source.up())


GRID = 64
GRID_ROWS = SEQ // GRID
RPB_ROWS, RPB_COLS = 15, 31
DELTAS = 2 * GRID_ROWS - 1
BIAS_COLS = HEADS * DELTAS
BIAS_PER_BANK = NC // BIAS_COLS
BIAS_ROUND = GRID // 2
MEM_HEADS = 4
MW = MEM_HEADS * HD
DN_TAPS = 5
DN_C = 3 * HW
DN_TILES = DN_C // P
DN_GATES = 4 * HEADS
DIRS = 2 * HEADS
DN_T = SEQ + DN_TAPS - 1
DIFF_MAPS = 2 * HEADS
DIFF_W = DIFF_MAPS * HD
LAM_INIT = 0.8 - 0.6 * math.exp(-0.3)
NQ, NK, NV, NG = (n * HW for n in range(4))
DQ, DK, DV, DG = (4 * HW + n * HW for n in range(4))
MQ, MG = 8 * HW, 8 * HW + MW
W_GATES, W_MEM = 8 * HW, 8 * HW + DN_GATES
OQ, OK, OV, OG = (n * DIFF_W for n in range(4))


def second_buffers(k):
    K = 1024
    w, t1 = k.scratch, k.t1
    end = (229368 - k.base) // 32 * 32
    k.kv = k.sb("kv", end - 16 * K, [P, TT, 4 * MW])
    free = end - 16 * K - t1
    k.normed_x = k.sb("normed_x", k.p0, [P, TT, D])
    k.gw_raw = k.sb("gw_raw", t1 + 8 * K, [P, KT, DN_GATES])
    k.gw_hi = k.sb("gw_hi", t1 + 10 * K, [P, KT, DN_GATES], F32R)
    k.gw_lo = k.sb("gw_lo", t1 + 12 * K, [P, KT, DN_GATES], F32R)
    k.small = k.mixer_small
    k.small_end = t1
    small = k.sb_small
    k.ss = small("ss", [P, TT, 2])
    k.head_ss = small("head_ss", [P, TT, 32])
    k.att_gain = small("att_gain", [P, 4])
    k.att_max = small("att_max", [P, 16, TT])
    k.att_sum = small("att_sum", [P, 16, TT])
    k.lam = small("lam", [P, 4])
    after_common = k.small
    k.dn_x = small("dn_x", [P, TT, DN_GATES])
    k.dn_sp = small("dn_sp", [P, TT, DN_GATES])
    k.dn_beta = small("dn_beta", [P, TT, DIRS])
    k.dn_g = small("dn_g", [P, TT, DIRS])
    k.dn_cum = small("dn_cum", [P, TT, DIRS])
    k.dn_total = small("dn_total", [P, TT, DIRS])
    k.dn_tail = small("dn_tail", [P, TT, DIRS])
    k.dn_ecum = small("dn_ecum", [P, TT, DIRS])
    k.dn_rate = small("dn_rate", [P, DIRS])
    k.dn_shift = small("dn_shift", [P, DIRS])
    k.dn_w = small("dn_w", [P, DN_TILES, DN_TAPS])
    k.dn_norm = small("dn_norm", [P, HD])
    k.dn_ms = small("dn_ms", [P, TT, HEADS])
    k.small = after_common
    k.o_subln = small("o_subln", [P, 2 * HD])
    k.o_mem_gain = small("o_mem_gain", [P, HD])
    k.o_ss = small("o_ss", [P, TT, HEADS])
    k.dn_u = k.sb("dn_u", t1, [P, HEADS, DN_T])
    k.dn_y = k.sb("dn_y", t1 + 6656, [P, HEADS, SEQ])
    k.dn_rows = k.sb("dn_rows", t1 + 6656, [DN_TAPS, DN_C])
    k.dn_sq = k.sb("dn_sq", t1, [P, TT, 2 * HW])
    k.na_bias = k.sb("na_bias", t1, [P, HEADS, TT, GRID_ROWS, GRID])
    k.e_junk = k.sb("e_junk", t1 + 12 * K, [P, 2 * 4, HD])
    r = t1 + 16 * K
    k.na_rows = k.sb("na_rows", r, [HEADS * RPB_ROWS, RPB_COLS])
    k.na_band = k.sb("na_band", r + 128, [RPB_COLS, GRID - 1 + P])
    k.na_window = k.sb("na_window", r + 896, [P, GRID])
    k.na_table = k.sb("na_table", r + 1152, [RPB_COLS, HEADS * RPB_ROWS])
    k.gain_rows = k.sb("gain_rows", r + 1536, [4, HD])
    k.na_t = k.sb("na_t", w, [P, 20, SEQ])
    k.e_att = [k.sb(f"e_att_{n}", w + (20 + 4 * i) * K, [P, 2, TT, SEQ]) for i, n in enumerate("set")]
    k.o_att = [k.sb(f"o_att_{n}", t1 + 4 * i * K, [P, 2, TT, SEQ]) for i, n in enumerate("set")]
    k.att_s, k.att_e, k.att_t = k.o_att
    m = 6 * K
    k.dn_t = k.sb("dn_t", w, [P, 2, HEADS, SEQ])
    k.dn_rows_t = k.sb("dn_rows_t", w + 2 * m, [P, TT, DIRS, P])
    k.dn_inv = k.sb("dn_inv", w + 4 * m, [P, DIRS, P])
    k.dn_inv2 = k.sb("dn_inv2", t1 + 2 * m, [P, DIRS, P])
    k.dn_m = k.sb("dn_m", t1, [P, DIRS, P])
    k.dn_off = k.sb("dn_off", t1 + m, [P, DIRS, P])
    k.dn_dec = [k.sb(f"dn_dec_{t}", at, [P, DIRS, P]) for t, at in enumerate((t1, w + 4 * m))]
    k.dn_outside = k.sb("dn_outside", w + 5 * m, [P, 2, P])
    k.dn_rhs = [k.sb(f"dn_rhs_{t}", at, [P, DIRS, P]) for t, at in enumerate((t1 + 2 * m, t1 + m))]
    k.dn_a = k.proj[:, :, NK:NK + 2 * HW].rearrange("p t (n i) -> p t n i", n=DIRS)
    k.dn_qk = k.proj[:, :, NG:NG + 2 * HW].rearrange("p t (n i) -> p t n i", n=DIRS)
    k.dn_v1 = k.sb("dn_v1", w + 4 * m, [P, DIRS, P])
    k.dn_vs = k.sb("dn_vs", t1, [P, DIRS, P])
    k.dn_state = k.sb("dn_state", t1 + m, [P, DIRS, P])
    k.dn_r = k.sb("dn_r", t1 + 2 * m, [P, DIRS, P])
    k.dn_qs = k.sb("dn_qs", t1, [P, DIRS, P])
    k.dn_v2 = k.sb("dn_v2", t1 + 2 * m, [P, DIRS, P])
    k.o_tables = k.sb("o_tables", t1, [P, 2, 4, TT, HALF])
    k.o_work = k.sb("o_work", t1 + 4 * K, [P, 2, 2, DIFF_MAPS, HALF])
    k.o_lam_rows = k.sb("o_lam_rows", t1 + 4 * K, [P, 2, 2, HD])
    k.o_gain = k.sb("o_gain", t1 + 10 * K, [P, 4, HD])
    k.o_rope = k.sb("o_rope", t1 + 16 * K, [P, TT, 2, HALF])
    k.o_junk = k.sb("o_junk", t1 + 12 * K, [P, 2, TT, 2 * HD])
    k.o_junk_heads = k.o_junk[:].rearrange("p x t (a e) -> p (x t a) e", a=2)
    assert free >= 3 * m
    count, later = k.count, k.later
    k.mem_in, k.gw_in, k.even_rows_in, k.dn_pairs_in = \
        count("mem_in", "gw_in", "even_rows_in", "dn_pairs_in")
    k.o_rows_in, k.dn_tv, k.dn_vs_kept, k.dn_s_done, k.dn_s_kept = \
        count("o_rows_in", "dn_tv", "dn_vs_kept", "dn_s_done", "dn_s_kept")
    k.dn_ks, k.dn_ks_kept, k.dn_qs_done, k.dn_qs_kept, k.dn_tv2 = \
        count("dn_ks", "dn_ks_kept", "dn_qs_done", "dn_qs_kept", "dn_tv2")
    k.dn_v2_kept, k.dn_o, k.dn_o_kept, k.dn_osq, k.dn_oms = count("dn_v2_kept", "dn_o", "dn_o_kept", "dn_osq", "dn_oms")
    k.dn_oroot, = count("dn_oroot")
    k.square_sum, k.rms_root, k.gw_hi_ready, k.gw_lo_ready, k.gates_done = \
        later(DEPTH, k.conv_pad, k.conv_gate, k.h_gate, k.h_qsilu, k.r_gate)
    k.gates_kept, k.even_gated = later(DEPTH, k.conv_weights, k.conv_gated)
    k.att_scaled, k.att_gainT, k.att_gained, k.na_tableT, k.na_table_kept = \
        later(DEPTH, k.conv_root, k.conv_linear, k.conv_done, k.h_fT, k.h_f_read)
    k.na_toeplitz, k.na_bias_kept, k.att_turned, k.att_turn_kept, k.at_s = \
        later(DEPTH, k.h_kx, k.h_key, k.h_qT, k.h_query, k.h_cumulated)
    k.at_max, k.at_e, k.at_t, k.at_c, k.at_o = later(DEPTH, k.h_o, k.h_square, k.h_msq, k.h_root, k.h_gated)
    k.at_y, k.dn_wT, k.dn_w_kept, k.dn_turned, k.dn_turn_kept = \
        later(DEPTH, k.r_roped, k.r_rope_free, k.r_qT, k.r_q, k.r_kT)
    k.dn_tap, k.dn_silu, k.dn_squared = later(DEPTH, k.r_k, k.r_o, k.r_var)
    k.dn_summed, = later(DEPTH * DVE_CONV * CONV_W, k.conv_tap)
    k.dn_rooted, k.dn_scaled, k.dn_qkT = later(DEPTH * (LEVELS + 1), k.h_rel, k.h_decay, k.h_factors)
    k.dn_qkT_kept, k.dn_abs = later(DEPTH * (LEVELS + 2), k.h_scores, k.h_score_kept)
    k.dn_soft, k.dn_lnb = later(DEPTH * HEADS, k.r_scores, k.r_kept)
    k.dn_beta_done, k.dn_g_done, k.dn_cums, k.dn_cum_kept, k.dn_tri_g = \
        count("dn_beta_done", "dn_g_done", "dn_cums", "dn_cum_kept", "dn_tri_g")
    k.dn_row, k.dn_rel, k.dn_decay, k.dn_gate_gained, k.dn_kk = \
        count("dn_row", "dn_rel", "dn_decay", "dn_gate_gained", "dn_kk")
    k.dn_qk_kept, k.dn_off_ready, k.dn_m_done, k.dn_m_kept, k.dn_up_done = \
        count("dn_qk_kept", "dn_off_ready", "dn_m_done", "dn_m_kept", "dn_up_done")
    k.dn_up_kept, k.dn_rows_kept, k.dn_pad, k.dn_it_done, k.dn_it_kept = \
        count("dn_up_kept", "dn_rows_kept", "dn_pad", "dn_it_done", "dn_it_kept")
    k.dn_e, = count("dn_e")
    k.o_tables_done, k.o_lam_sums, k.o_lam_exp, k.o_queries, k.o_keys = \
        later(1, k.dn_tv, k.dn_oms, k.dn_s_done, k.dn_s_kept, k.dn_ks)
    k.o_gate_done, k.o_turned, k.o_turn_kept, k.d_s = \
        later(1, k.dn_ks_kept, k.dn_qs_done, k.dn_qs_kept, k.dn_tv2)
    k.d_max, k.d_e, k.d_a = later(2, k.dn_o, k.dn_vs_kept, k.dn_osq)
    k.d_t, = later(2, k.dn_o_kept)
    k.d_c, = later(1, k.dn_oroot)
    k.d_o, k.d_sq, k.d_y, k.o_root = count("d_o", "d_sq", "d_y", "o_root")
    k.o_scaled, k.heads_rooted = count("o_scaled", "heads_rooted")
    return free


def act_rms(act, k, src, junk):
    for t in range(TT):
        last = k.nc.scalar.activation(junk[:, t, :], src[:, t, :], ACT.Square, accum_out=k.ss[:, t, 0:1])
    last.then_inc(*k.square_sum.up())
    act.wait_ge(*k.square_sum.now())
    k.nc.scalar.activation(k.ss[:, :, 1], k.ss[:, :, 0], ACT.Sqrt, scale=1.0 / D, bias=k.eps[:, 1:2])\
        .then_inc(*k.rms_root.up())


def dve_mean_square(dve, k, units):
    v = k.nc.vector
    k.stats_units += units
    dve.wait_ge(k.stats_ready, k.stats_units)
    for t in range(TT):
        last = v.bn_aggr(k.mv[:, t, :], k.stats[:, t].rearrange("p c s -> p (c s)"))
    last.then_inc(*k.dve_step.up())
    dve.wait_ge(*k.dve_step.now())
    v.tensor_tensor(k.ss[:, :, 0], k.mv[:, :, 0], k.mv[:, :, 0], ALU.mult).then_inc(*k.dve_step.up())
    dve.wait_ge(*k.dve_step.now())
    v.tensor_tensor(k.ss[:, :, 0], k.ss[:, :, 0], k.mv[:, :, 1], ALU.add).then_inc(*k.aggregated.up())


def act_root_mean_square(act, k):
    act_sqrt_table(k)
    act.wait_ge(*k.aggregated.next("act"))
    k.nc.scalar.activation(k.ss[:, :, 1], k.ss[:, :, 0], ACT.Sqrt, bias=k.eps[:, 1:2]).then_inc(*k.rms_root.up())


def dve_rms(dve, k, src, dst, gain, run=no_blocks, after=no_step):
    v = k.nc.vector
    dve.wait_ge(*k.rms_root.next("dve"))
    v.reciprocal(k.ss[:, :, 1], k.ss[:, :, 1]).then_inc(*k.dve_step.up())
    dve.wait_ge(*k.dve_step.now())
    for c in range(D // NC):
        cols = slice(c * NC, (c + 1) * NC)
        for t in range(TT):
            last = v.scalar_tensor_tensor(dst[:, t, cols], src[:, t, cols], k.ss[:, t, 1:2], gain[:, cols],
                                          ALU.mult, ALU.mult)
        last.then_inc(*k.turn_source.up(2))
        run(1)
        after(c)


def dve_memory(dve, k):
    v = k.nc.vector

    def step(ins):
        ins.then_inc(*k.dve_step.up())
        dve.wait_ge(*k.dve_step.now())

    def between(u, j):
        c, t = divmod(j, TT)
        cols = slice(c * NC, (c + 1) * NC)
        if u == 1:
            if j == 0:
                dve.wait_ge(*k.mem_in.next("dve", 32))
            ins = v.bn_stats(k.mem_stats[:, t, c, :], k.mem[:, t, cols])
            if j == BLOCKS - 1:
                step(ins)
        elif (u, j) == (2, 0):
            for t in range(TT):
                last = v.bn_aggr(k.mem_mv[:, t, :], k.mem_stats[:, t].rearrange("p c s -> p (c s)"))
            step(last)
            step(v.tensor_tensor(k.mem_root[:], k.mem_mv[:, :, 0], k.mem_mv[:, :, 0], ALU.mult))
            v.tensor_tensor(k.mem_root[:], k.mem_root[:], k.mem_mv[:, :, 1], ALU.add).then_inc(*k.aggregated.up())
        elif (u, j) == (3, 4):
            dve.wait_ge(*k.root.next("dve"))
            step(v.reciprocal(k.mem_root[:], k.mem_root[:]))
        elif u == 4:
            ins = v.scalar_tensor_tensor(k.mem[:, t, cols], k.mem[:, t, cols], k.mem_root[:, t:t + 1], k.mem_gain[:, cols],
                                         ALU.mult, ALU.mult)
            if t == TT - 1:
                ins.then_inc(*k.turn_source.up(2))
        elif u == 5:
            dve_turn_bank(dve, k, j)
    return between


def act_memory(act, k):
    def between(u, j):
        if (u, j) == (3, 2):
            act.wait_ge(*k.aggregated.next("act"))
            k.nc.scalar.activation(k.mem_root[:], k.mem_root[:], ACT.Sqrt, bias=k.eps[:, 1:2]).then_inc(*k.root.up())
        elif u == 5:
            act_turn_bank(act, k, j)
    return between


def pe_memory(pe, k):
    def tile(kt, t):
        return k.mem[:, t, kt * P:(kt + 1) * P]

    def between(u, j):
        if u == 5:
            pe_turn_bank(pe, k, tile, j)
    return between


def pe_gate_columns(pe, k):
    pe.wait_ge(*k.gw_lo_ready.next("pe"))
    for t in range(TT):
        tokens = slice(t * P, (t + 1) * P)
        out = k.ps[:, t, 0:DN_GATES]
        for kt in range(KT):
            k.nc.tensor.matmul(out, k.a_hi[:, kt, tokens], k.gw_hi[:, kt, :], start=kt == 0, stop=False)
            k.nc.tensor.matmul(out, k.a_hi[:, kt, tokens], k.gw_lo[:, kt, :], start=False, stop=False)
            last = k.nc.tensor.matmul(out, k.a_lo[:, kt, tokens], k.gw_hi[:, kt, :], start=False, stop=kt == KT - 1)
    last.then_inc(*k.gates_done.up())


def act_gate_split(act, k):
    act.wait_ge(*k.gw_in.next("act", 16))
    k.nc.scalar.activation(k.gw_hi[:], k.gw_raw[:], ACT.Copy).then_inc(*k.gw_hi_ready.up())


def dve_gate_split(dve, k):
    dve.wait_ge(*k.gw_hi_ready.next("dve"))
    k.nc.vector.tensor_tensor(k.gw_lo[:], k.gw_raw[:], k.gw_hi[:].bitcast(F32), ALU.subtract)\
        .then_inc(*k.gw_lo_ready.up())


def dve_gate_columns(dve, k):
    dve.wait_ge(*k.gates_done.next("dve"))
    k.nc.vector.tensor_copy(k.dn_x[:], k.ps[:, 0:TT, 0:DN_GATES]).then_inc(*k.gates_kept.up())


def act_take_columns(act, k, columns):
    def take(b0, s, i):
        wait_unit(act, k, b0, s)
        at = columns[2 * i + s]
        k.nc.scalar.activation(k.proj[:, :, at:at + NC], k.ps_unit[:, s], ACT.Copy).then_inc(k.evacuated, BLOCKS)
    return take


def act_take_memory(act, k):
    def take(b0, s, i):
        wait_unit(act, k, b0, s)
        k.nc.scalar.activation(k.kv[:, :, bass.ds(i * (2 * NC) + s * NC, NC)], k.ps_unit[:, s],
                               ACT.Copy).then_inc(k.evacuated, BLOCKS)
    return take


def pe_attention(pe, k, maps, arrays, run=no_blocks, apart=0):
    tensor = k.nc.tensor
    _, att_e, att_t = arrays

    def turn(n):
        pe.wait_ge(*k.at_e.next("pe"))
        if n >= 1:
            pe.wait_ge(*k.at_c.next("pe free"))
        for t in range(TT):
            for kt in range(TT):
                last = tensor.transpose(k.ps[:, 2, kt * SEQ + t * P:kt * SEQ + (t + 1) * P],
                                        att_e[:, n % 2, t, kt * P:(kt + 1) * P], k.ident)
        last.then_inc(*k.at_t.up())

    def weigh(n):
        pe.wait_ge(*k.at_c.next("pe"))
        if n >= 1:
            pe.wait_ge(*k.at_y.next("pe"))
        value = maps[n][3]
        for t in range(TT):
            for kt in range(TT):
                last = tensor.matmul(k.ps[:, 3, t * HD:(t + 1) * HD], att_t[:, n % 2, kt, t * P:(t + 1) * P], value(kt),
                                     start=kt == 0, stop=kt == TT - 1)
        last.then_inc(*k.at_o.up())

    for n in range(len(maps) + 2):
        run(apart)
        if n < len(maps):
            if n >= 2:
                pe.wait_ge(*k.at_e.next("pe free"))
            q, key = maps[n][0], maps[n][1]
            for t in range(TT):
                last = tensor.matmul(k.ps[:, n % 2, t * SEQ:(t + 1) * SEQ], q[:, t * P:(t + 1) * P], key,
                                     start=True, stop=True)
            last.then_inc(*k.at_s.up())
        if 1 <= n <= len(maps):
            turn(n - 1)
        if n >= 2:
            weigh(n - 2)
    pe.wait_ge(*k.at_y.next("pe"))
    k.at_c.next("pe free")
    k.at_e.next("pe free", 2)


def act_attention(act, k, maps, arrays, run=no_blocks, apart=0):
    a = k.nc.scalar
    att_s, att_e, att_t = arrays

    def copy(n):
        act.wait_ge(*k.at_t.next("act"))
        if n >= 2:
            act.wait_ge(*k.at_o.next("act"))
        a.activation(att_t[:, n % 2], k.ps[:, 2, :].rearrange("p (a s) -> p a s", a=TT), ACT.Copy)\
            .then_inc(*k.at_c.up())

    for n, (_, _, bias, *_) in enumerate(maps):
        run(apart)
        act.wait_ge(*k.at_max.next("act"))
        scores = att_s[:, n % 2] if bias is not None else k.ps[:, n % 2, :].rearrange("p (a s) -> p a s", a=TT)
        if n >= 2:
            act.wait_ge(*k.at_t.next("act free"))
        for t in range(TT):
            last = a.activation(att_e[:, n % 2, t, :], scores[:, t, :], ACT.Exp, bias=k.att_max[:, n, t:t + 1],
                                accum_out=k.att_sum[:, n, t:t + 1])
        last.then_inc(*k.at_e.up())
        if n >= 1:
            copy(n - 1)
    run(apart)
    copy(len(maps) - 1)
    run(apart)
    k.at_t.next("act free", 2)
    k.at_o.next("act", 2)


def dve_attention(dve, k, maps, arrays, run=no_blocks, apart=0):
    v = k.nc.vector
    att_s, _, _ = arrays

    def output(n):
        _, _, _, _, gate, out = maps[n]
        dve.wait_ge(*k.at_e.next("dve"))
        v.reciprocal(k.att_sum[:, n, :], k.att_sum[:, n, :]).then_inc(*k.dve_step.up())
        dve.wait_ge(*k.at_o.next("dve"))
        dve.wait_ge(*k.dve_step.now())
        for t in range(TT):
            last = v.scalar_tensor_tensor(out(t), k.ps[:, 3, t * HD:(t + 1) * HD], k.att_sum[:, n, t:t + 1], gate(t),
                                          ALU.mult, ALU.mult)
        last.then_inc(*k.at_y.up())

    for n in range(len(maps) + 2):
        run(apart)
        if n < len(maps):
            bias = maps[n][2]
            dve.wait_ge(*k.at_s.next("dve"))
            scores = k.ps[:, n % 2, :].rearrange("p (a s) -> p a s", a=TT)
            if bias is not None:
                v.tensor_tensor(att_s[:, n % 2], scores, bias, ALU.add).then_inc(*k.dve_step.up())
                scores = att_s[:, n % 2]
                dve.wait_ge(*k.dve_step.now())
            v.tensor_reduce(k.att_max[:, n, :], scores, AX_X, ALU.max, negate=True).then_inc(*k.at_max.up())
        if n >= 2:
            output(n - 2)


def even_maps(k):
    def cols(buffer, at):
        return lambda t: buffer[:, t, at:at + HD]

    maps = [(k.na_t[:, h, :], k.na_t[:, HEADS + h, :], k.na_bias[:, h].rearrange("p t r c -> p t (r c)"),
             cols(k.proj, NV + h * HD), cols(k.proj, NG + h * HD), cols(k.proj, NQ + h * HD)) for h in range(HEADS)]
    m0 = 2 * HEADS
    return maps + [(k.na_t[:, m0 + h, :], k.na_t[:, m0 + MEM_HEADS + h, :], None,
                    cols(k.kv, MW + h * HD), cols(k.proj, MG + h * HD), cols(k.proj, MQ + h * HD))
                   for h in range(MEM_HEADS)]


def pool_even_rows(pool, k):
    d = k.dram
    pool.wait_ge(*k.gates_done.next("pool"))
    for to, src in ((k.na_rows[:], d["na_rpb_2"][0].rearrange("h a b -> (h a) b")), (k.na_band[:], d["c_band"]),
                    (k.na_window[:], d["c_window"]), (k.gain_rows[0:1, :], d["na_q_norm_2"]),
                    (k.gain_rows[1:2, :], d["na_k_norm_2"]), (k.gain_rows[2:3, :], d["e_mem_q_norm_2"]),
                    (k.gain_rows[3:4, :], d["e_mem_k_norm_2"]),
                    (k.dn_rate[:], d["dn_a_log_2"].rearrange("a b c -> (a b c)").partition_broadcast(P)),
                    (k.dn_shift[:], d["dn_dt_bias_2"].rearrange("a b c -> (a b c)").partition_broadcast(P)),
                    (k.dn_norm[:], d["dn_out_norm_2"][0].partition_broadcast(P)), (k.dn_rows[:], d["dn_conv_w_2"][0])):
        pool.dma_start(to, src).then_inc(*k.even_rows_in.up(16))


EVEN_ROWS = 11 * 16


def even_sources(k):
    def heads(buffer, at, n):
        return lambda t: buffer[:, t, at:at + n * HD].rearrange("p (n d) -> p n d", n=n)
    return [(0, 2 * HEADS, heads(k.proj, NQ, 2 * HEADS)), (2 * HEADS, MEM_HEADS, heads(k.proj, MQ, MEM_HEADS)),
            (2 * HEADS + MEM_HEADS, MEM_HEADS, heads(k.kv, 0, MEM_HEADS))]


THIRD = 13
E_Q, E_MQ, E_MK = 0, 2 * HEADS, 2 * HEADS + MEM_HEADS


def act_squares(act, k, run, buffer, at, n, first, junk):
    for h in range(0, n, 4):
        for t in range(TT):
            act.wait_ge(k.act_step.sem, k.act_step.made - 1)
            for x in range(4):
                head = buffer[:, t, at + (h + x) * HD:at + (h + x + 1) * HD]
                last = k.nc.scalar.activation(junk[:, 4 * t + x, :], head, ACT.Square,
                                              accum_out=k.head_ss[:, t, first + h + x:first + h + x + 1])
            last.then_inc(*k.act_step.up())
            run(1)


def act_root(act, k, first, n):
    act.wait_ge(*k.act_step.now())
    part = k.head_ss[:, :, first:first + n]
    k.nc.scalar.activation(part, part, ACT.Sqrt, scale=1.0 / HD, bias=k.eps[:, 1:2]).then_inc(*k.heads_rooted.up())


def dve_divide(dve, k, first, n):
    dve.wait_ge(*k.heads_rooted.next("dve"))
    part = k.head_ss[:, :, first:first + n]
    k.nc.vector.reciprocal(part, part).then_inc(*k.dve_step.up())
    dve.wait_ge(*k.dve_step.now())


def scale_heads(k, buffer, at, n, first, t):
    heads = buffer[:, t, at:at + n * HD].rearrange("p (n d) -> p n d", n=n)
    return k.nc.vector.tensor_tensor(heads, heads, k.head_ss[:, t, first:first + n].unsqueeze(2).to_broadcast([P, n, HD]),
                                     ALU.mult)


def act_even_inputs(act, k, run):
    a = k.nc.scalar

    def step(ins):
        ins.then_inc(*k.act_step.up())
        act.wait_ge(*k.act_step.now())

    act.wait_ge(*run.evacuated(0))
    dg = k.proj[:, :, DG:DG + HW]
    a.activation(dg, dg, ACT.Silu)
    run(2)
    act.wait_ge(*k.dn_abs.next("act"))
    step(a.activation(k.dn_sp[:], k.dn_x[:], ACT.Abs))
    step(a.activation(k.dn_sp[:], k.dn_sp[:], ACT.Exp, scale=-1.0))
    a.activation(k.dn_rate[:], k.dn_rate[:], ACT.Exp)
    a.activation(k.dn_sp[:], k.dn_sp[:], ACT.Ln, bias=1.0).then_inc(*k.dn_soft.up())
    run(2)
    act.wait_ge(*k.dn_lnb.next("act"))
    a.activation(k.dn_beta[:], k.dn_beta[:], ACT.Exp).then_inc(*k.dn_beta_done.up())
    run(1)

    def keep(group, to):
        act.wait_ge(*k.dn_turned.next("act"))
        a.activation(to, k.ps[:, group % 4, :].rearrange("p (a s) -> p a s", a=2), ACT.Copy).then_inc(*k.dn_turn_kept.up())

    for part in range(3):
        run(5 + THIRD * part - run.done)
        for g in range(3):
            keep(6 * part + g, k.dn_u[:, 2 * g:2 * g + 2, 2:SEQ + 2])
        run(14 + THIRD * part - run.done)
        act.wait_ge(*k.dn_tap.next("act", HEADS * DN_TAPS))
        a.activation(k.dn_y[:], k.dn_y[:], ACT.Silu).then_inc(*k.dn_silu.up())
        if part == 1:
            act.wait_ge(*run.evacuated(2))
            mg = k.proj[:, :, MG:MG + MW]
            a.activation(mg, mg, ACT.Silu)
        if part == 0:
            act.wait_ge(*k.dn_cum_kept.next("act"))
            a.activation(k.dn_ecum[:], k.dn_cum[:], ACT.Exp)
            a.activation(k.dn_tail[:], k.dn_tail[:], ACT.Exp).then_inc(*k.dn_e.up())
        run(16 + THIRD * part - run.done)
        for g in range(3):
            keep(6 * part + 3 + g, k.proj[:, :, DQ + (3 * part + g) * 2 * P:DQ + (3 * part + g + 1) * 2 * P])
    run(1)
    act.wait_ge(*k.dn_turn_kept.now())
    for t in range(TT):
        last = a.activation(k.dn_sq[:, t, :], k.proj[:, t, DQ:DQ + 2 * HW], ACT.Square)
    last.then_inc(*k.dn_squared.up())
    run(3)
    act.wait_ge(*k.dn_summed.next("act"))
    a.activation(k.head_ss[:, :, 0:DIRS], k.head_ss[:, :, 0:DIRS], ACT.Sqrt, bias=k.eps[:, 1:2]).then_inc(*k.dn_rooted.up())
    run(2)
    act.wait_ge(*run.evacuated(5))
    act.wait_ge(*k.dn_scaled.next("act"))
    act_squares(act, k, run, k.proj, MQ, MEM_HEADS, E_MQ, k.e_junk)
    act_squares(act, k, run, k.kv, 0, MEM_HEADS, E_MK, k.e_junk)
    act_squares(act, k, run, k.proj, NQ, 2 * HEADS, E_Q, k.e_junk)
    act_root(act, k, E_Q, 2 * HEADS + 2 * MEM_HEADS)
    act.wait_ge(*run.evacuated(7))
    ng = k.proj[:, :, NG:NG + HW]
    a.activation(ng, ng, ACT.Silu).then_inc(*k.even_gated.up())
    run.rest()


def pe_even_inputs(pe, k, run):
    tensor = k.nc.tensor
    run(3)
    pe.wait_ge(*k.even_rows_in.next("pe", EVEN_ROWS))
    pe.wait_ge(*k.gates_kept.next("pe"))
    for c in range(DN_TILES):
        last = tensor.transpose(k.ps[:, 3, c * DN_TAPS:(c + 1) * DN_TAPS], k.dn_rows[:, c * P:(c + 1) * P],
                                k.ident[0:DN_TAPS, 0:DN_TAPS])
    last.then_inc(*k.dn_wT.up())
    pe.wait_ge(*run.evacuated(0))
    run(1)
    groups = 0

    def turn(tile):
        nonlocal groups
        if groups >= 4:
            pe.wait_ge(*k.dn_turn_kept.next("pe"))
        for x in range(2):
            for y in range(2):
                last = tensor.transpose(k.ps[:, groups % 4, x * SEQ + y * P:x * SEQ + (y + 1) * P], tile(x, y), k.ident)
        last.then_inc(*k.dn_turned.up())
        groups += 1

    for part in range(3):
        run(4 + THIRD * part - run.done)
        for g in range(3):
            at = DQ + (6 * part + 2 * g) * P
            turn(lambda x, t: k.proj[:, t, at + x * P:at + (x + 1) * P])
        if part == 0:
            run(2)
            pe.wait_ge(*k.dn_g_done.next("pe"))
            pe.wait_ge(*k.dn_w_kept.next("pe"))
            for t in range(TT):
                for at, n, square, gates in ((0, HEADS, k.tri, dirs(0)), (HEADS, HEADS, k.tri_t, dirs(1)),
                                             (DIRS, DIRS, k.ones, slice(0, DIRS))):
                    at += t * 2 * DIRS
                    last = tensor.matmul(k.ps[:, 3, at:at + n], square, k.dn_g[:, t, gates], start=True, stop=True)
            last.then_inc(*k.dn_cums.up())
        run(15 + THIRD * part - run.done)
        pe.wait_ge(*k.dn_silu.next("pe"))
        if part == 0:
            pe.wait_ge(*k.dn_cum_kept.next("pe"))
        for g in range(3):
            turn(lambda t, x: k.dn_y[:, 2 * g + x, t * P:(t + 1) * P])
    run(51 - run.done)
    pe.wait_ge(*k.dn_turn_kept.next("pe", 4))
    tensor.transpose(k.ps[:, 0, 0:4], k.gain_rows[:], k.ident[0:4, 0:4]).then_inc(*k.att_gainT.up())
    tensor.transpose(k.ps[0:RPB_COLS, 1, 0:HEADS * RPB_ROWS], k.na_rows[:],
                     k.ident[0:HEADS * RPB_ROWS, 0:HEADS * RPB_ROWS]).then_inc(*k.na_tableT.up())
    run(2)
    pe.wait_ge(*k.na_table_kept.next("pe"))
    table = k.na_table[:].rearrange("j (h a) -> j h a", h=HEADS)[:, :, RPB_ROWS // 2 - (GRID_ROWS - 1):
                                                                  RPB_ROWS // 2 + GRID_ROWS]
    for half in range(2):
        if half:
            run(5)
            pe.wait_ge(*k.na_bias_kept.next("pe"))
        for n in range(BIAS_ROUND):
            first = GRID - 1 - (half * BIAS_ROUND + n)
            pick = k.na_band[:, first:first + P]
            at = n % BIAS_PER_BANK * BIAS_COLS
            last = tensor.matmul(k.ps[:, n // BIAS_PER_BANK, at:at + BIAS_COLS], pick, table, start=True, stop=True)
        last.then_inc(*k.na_toeplitz.up())
    run.rest()
    pe.wait_ge(*k.na_bias_kept.next("pe"))


def dve_even_inputs(dve, k, run):
    v = k.nc.vector

    def step(ins):
        ins.then_inc(*k.dve_step.up())
        dve.wait_ge(*k.dve_step.now())

    run(1)
    dve.wait_ge(*k.even_rows_in.next("dve", EVEN_ROWS))
    dve.wait_ge(*k.gates_kept.now())
    step(v.tensor_tensor(k.dn_x[:, :, DIRS:], k.dn_x[:, :, DIRS:], k.dn_shift[:].unsqueeze(1).to_broadcast([P, TT, DIRS]),
                         ALU.add))
    v.memset(k.dn_ms[:], 0.0).then_inc(*k.dn_abs.up())
    run(2)
    dve.wait_ge(*k.dn_soft.next("dve"))
    step(v.scalar_tensor_tensor(k.dn_sp[:], k.dn_x[:], 0.0, k.dn_sp[:], ALU.max, ALU.add))
    v.tensor_tensor(k.dn_beta[:], k.dn_x[:, :, 0:DIRS], k.dn_sp[:, :, 0:DIRS], ALU.subtract).then_inc(*k.dn_lnb.up())
    v.scalar_tensor_tensor(k.dn_g[:], k.dn_sp[:, :, DIRS:], -1.0, k.dn_rate[:].unsqueeze(1).to_broadcast([P, TT, DIRS]),
                           ALU.mult, ALU.mult).then_inc(*k.dn_g_done.up())
    run(1)
    dve.wait_ge(*k.dn_wT.next("dve"))
    v.tensor_copy(k.dn_w[:], k.ps[:, 3, 0:DN_TILES * DN_TAPS].rearrange("p (c x) -> p c x", c=DN_TILES))\
        .then_inc(*k.dn_w_kept.up())
    dve.wait_ge(*k.dn_w_kept.now())
    dve.wait_ge(*k.dn_pad.next("dve"))
    sem, done = k.dn_tap.now()
    for part in range(3):
        run(6 + THIRD * part - run.done)
        dve.wait_ge(*k.dn_turn_kept.next("dve", 6 if part else 3))
        for tap in range(DN_TAPS):
            for x in range(HEADS):
                c, n = part * HEADS + x, tap * HEADS + x
                u, y, w = k.dn_u[:, x, tap:tap + SEQ], k.dn_y[:, x, :], k.dn_w[:, c, tap:tap + 1]
                if tap == 0:
                    ins = v.tensor_scalar(y, u, w, None, ALU.mult)
                else:
                    dve.wait_ge(sem, done + HEADS * (DN_TAPS * part + tap - 1) + x + 1)
                    ins = v.scalar_tensor_tensor(y, u, w, y, ALU.mult, ALU.add)
                ins.then_inc(*k.dn_tap.up())
                if n % 4 == 3:
                    run(1)
        if part == 0:
            dve.wait_ge(*k.dn_cums.next("dve"))
            sums = k.ps[:, 3, 0:4 * DIRS].rearrange("p (t x n) -> p t x n", t=TT, x=2)
            v.tensor_copy(k.dn_cum[:], sums[:, :, 0, :])
            step(v.tensor_copy(k.dn_total[:], sums[:, :, 1, :]))
            v.tensor_tensor(k.dn_tail[:], k.dn_total[:], k.dn_cum[:], ALU.subtract).then_inc(*k.dn_cum_kept.up())
    run(45 - run.done)
    dve.wait_ge(*k.dn_beta_done.next("dve"))
    dve.wait_ge(*k.dn_e.next("dve"))
    v.tensor_tensor(k.dn_tail[:], k.dn_tail[:], k.dn_beta[:], ALU.mult)
    dve.wait_ge(*k.dn_squared.next("dve"))
    for t in range(TT):
        last = v.tensor_reduce(k.head_ss[:, t, 0:DIRS], k.dn_sq[:, t, :].rearrange("p (n e) -> p n e", n=DIRS), AX_X, ALU.add)
    last.then_inc(*k.dn_summed.up())
    run(47 - run.done)
    dve.wait_ge(*k.dn_rooted.next("dve"))
    step(v.reciprocal(k.head_ss[:, :, 0:DIRS], k.head_ss[:, :, 0:DIRS]))
    step(v.tensor_scalar(k.head_ss[:, :, 0:HEADS], k.head_ss[:, :, 0:HEADS], HD ** -0.5, None, ALU.mult))
    for t in range(TT):
        last = scale_heads(k, k.proj, DQ, DIRS, 0, t)
    last.then_inc(*k.dn_scaled.up())
    run(52 - run.done)
    dve.wait_ge(*k.att_gainT.next("dve"))
    v.tensor_copy(k.att_gain[:], k.ps[:, 0, 0:4]).then_inc(*k.dve_step.up())
    dve.wait_ge(*k.na_tableT.next("dve"))
    v.tensor_copy(k.na_table[:], k.ps[0:RPB_COLS, 1, 0:HEADS * RPB_ROWS]).then_inc(*k.na_table_kept.up())
    dve.wait_ge(*k.dve_step.now())
    for n in (0, 2):
        last = v.tensor_scalar(k.att_gain[:, n:n + 1], k.att_gain[:, n:n + 1], k.att_gain[:, n + 1:n + 2], HD ** -0.5,
                               ALU.mult, ALU.mult)
    last.then_inc(*k.att_gained.up())
    run(1)
    dve.wait_ge(*k.dn_scaled.now())
    for half in range(2):
        run(1)
        dve.wait_ge(*k.na_toeplitz.next("dve"))
        for first in range(0, BIAS_ROUND, BIAS_PER_BANK):
            n = min(BIAS_PER_BANK, BIAS_ROUND - first)
            src = k.ps[:, first // BIAS_PER_BANK, 0:n * BIAS_COLS].rearrange("p (c h a) -> p h a c", c=n, h=HEADS)
            keys = slice(half * BIAS_ROUND + first, half * BIAS_ROUND + first + n)
            for t in range(TT):
                for r in range(2):
                    part = slice(r * GRID, (r + 1) * GRID)
                    a = GRID_ROWS - 1 - (2 * t + r)
                    window = k.na_window[part, keys].unsqueeze(1).unsqueeze(1).to_broadcast([GRID, HEADS, GRID_ROWS, n])
                    last = v.tensor_tensor(k.na_bias[part, :, t, :, keys], src[part, :, a:a + GRID_ROWS, :], window, ALU.add)
            run(1)
        last.then_inc(*k.na_bias_kept.up())
    run(max(61 - run.done, 0))
    dve_divide(dve, k, E_Q, 2 * HEADS + 2 * MEM_HEADS)
    for t in range(TT):
        scale_heads(k, k.proj, NQ, 2 * HEADS, E_Q, t)
        scale_heads(k, k.kv, 0, MEM_HEADS, E_MK, t)
        last = scale_heads(k, k.proj, MQ, MEM_HEADS, E_MQ, t)
        if t == 0:
            run(1)
    last.then_inc(*k.att_scaled.up())
    run.rest()


def act_even_attention(act, k):
    act_attention(act, k, even_maps(k), k.e_att)


def pe_even_attention(pe, k):
    pe.wait_ge(*k.att_scaled.next("pe"))
    slot = 0
    for first, n, src in even_sources(k):
        for h in range(0, n, 2):
            if slot >= 4:
                pe.wait_ge(*k.att_turn_kept.next("pe"))
            for x in range(2):
                for t in range(TT):
                    last = k.nc.tensor.transpose(k.ps[:, slot % 4, x * SEQ + t * P:x * SEQ + (t + 1) * P], src(t)[:, h + x, :],
                                                 k.ident)
            last.then_inc(*k.att_turned.up())
            slot += 1
    pe.wait_ge(*k.att_turn_kept.next("pe", 4))
    pe_attention(pe, k, even_maps(k), k.e_att)


def dve_even_attention(dve, k):
    v = k.nc.vector
    dve.wait_ge(*k.att_gained.now())
    slot = 0
    for first, n, src in even_sources(k):
        for h in range(0, n, 2):
            dve.wait_ge(*k.att_turned.next("dve"))
            at = first + h
            turned = k.ps[:, slot % 4, :].rearrange("p (a s) -> p a s", a=2)
            to = k.na_t[:, at:at + 2, :]
            if at < HEADS or 2 * HEADS <= at < 2 * HEADS + MEM_HEADS:
                gain = 0 if at < HEADS else 2
                ins = v.tensor_scalar(to, turned, k.att_gain[:, gain:gain + 1], None, ALU.mult)
            else:
                ins = v.tensor_copy(to, turned)
            ins.then_inc(*k.att_turn_kept.up())
            slot += 1
    dve.wait_ge(*k.even_gated.next("dve"))
    dve_attention(dve, k, even_maps(k), k.e_att)



def early_tile(d):
    return d


def dirs(d):
    return slice(d * HEADS, (d + 1) * HEADS)


def late(d):
    return slice((1 - d) * P, (2 - d) * P)


def pair_mask(k, n):
    return k.proj[:, n // 4, MG + n % 4 * P:MG + (n % 4 + 1) * P]


def first_off(k, t):
    return k.dn_m if t else k.dn_off


def heads_of(ap):
    return ap.rearrange("p (h e) -> p h e", h=HEADS)


def pool_delta(pool, k):
    g = k.nc.gpsimd
    d = k.dram
    g.memset(k.dn_u[:, :, 0:2], 0.0)
    g.memset(k.dn_u[:, :, SEQ + 2:DN_T], 0.0).then_inc(*k.dn_pad.up())
    pool.wait_ge(*k.dn_g_done.next("pool"))
    pool.wait_ge(*k.att_scaled.next("pool"))

    def grown(t):
        for dr, tri in ((0, k.tri), (1, k.tri_t)):
            last = g.tensor_tensor(k.dn_rhs[t][:, dirs(dr), :], tri.unsqueeze(1).to_broadcast([P, HEADS, P]),
                                   k.dn_g[:, t, dirs(dr)].unsqueeze(2).to_broadcast([P, HEADS, P]), ALU.mult)
        last.then_inc(*k.dn_tri_g.up())

    grown(0)
    pool.wait_ge(*k.at_y.next("pool", HEADS + MEM_HEADS))
    grown(1)
    pairs = d["c_pairs"].rearrange("p (n i) -> p n i", n=LEVELS)
    for t, first, end in ((0, 0, 4), (1, 4, LEVELS)):
        to = k.proj[:, t, MG:MG + (end - first) * P].rearrange("p (n i) -> p n i", n=end - first)
        pool.dma_start(to, pairs[:, first:end, :]).then_inc(*k.dn_pairs_in.up(16))
    for t in range(TT):
        gate = heads_of(k.proj[:, t, DG:DG + HW])
        last = g.tensor_tensor(gate, gate, k.dn_norm[:].unsqueeze(1).to_broadcast([P, HEADS, HD]), ALU.mult)
    last.then_inc(*k.dn_gate_gained.up())
    pool.wait_ge(*k.dn_row.next("pool", TT))
    pool.wait_ge(*k.dn_pairs_in.next("pool", 32))
    for n in reversed(range(LEVELS)):
        for t in range(TT):
            off = first_off(k, t) if n == LEVELS - 1 else k.dn_off
            if n == LEVELS - 1:
                pool.wait_ge(*k.dn_qk_kept.next("pool"))
            elif (n, t) == (LEVELS - 2, 0):
                pool.wait_ge(*k.dn_up_kept.next("pool"))
            else:
                pool.wait_ge(*k.dn_m_done.next("pool", 3))
            g.tensor_tensor(off[:], k.dn_a[:, t], pair_mask(k, n).unsqueeze(1).to_broadcast([P, DIRS, P]),
                            ALU.mult).then_inc(*k.dn_off_ready.up())


def act_delta(act, k):
    a = k.nc.scalar
    for t in range(TT):
        act.wait_ge(*k.dn_rel.next("act"))
        a.activation(k.dn_dec[t][:], k.dn_dec[t][:], ACT.Exp).then_inc(*k.dn_decay.up())
    banks = 0
    inverse = (k.dn_inv, k.dn_inv2)
    for n in reversed(range(LEVELS)):
        for t in range(TT):
            if n < LEVELS - 1:
                for g in range(3):
                    act.wait_ge(*k.dn_m_done.next("act"))
                    a.activation(k.dn_m[:, 4 * g:4 * g + 4, :], bank_of(k, banks), ACT.Copy).then_inc(*k.dn_m_kept.up())
                    banks += 1
                banks += 3
            if n > 0:
                for g in range(3):
                    act.wait_ge(*k.dn_it_done.next("act"))
                    a.activation(inverse[t][:, 4 * g:4 * g + 4, :], bank_of(k, banks), ACT.Copy).then_inc(*k.dn_it_kept.up())
                    banks += 1
    act.wait_ge(*k.dn_s_done.next("act"))
    a.activation(k.dn_state[:], three_unit_banks(k), ACT.Copy).then_inc(*k.dn_s_kept.up())
    for t in range(TT):
        act.wait_ge(*k.dn_o_kept.next("act"))
        a.activation(k.dn_a[:, t, dirs(1), :], k.dn_a[:, t, dirs(0), :], ACT.Square).then_inc(*k.dn_osq.up())
    act.wait_ge(*k.dn_oms.next("act"))
    a.activation(k.dn_ms[:], k.dn_ms[:], ACT.Sqrt, scale=1.0 / HD, bias=k.eps[:, 1:2]).then_inc(*k.dn_oroot.up())


def key_products(k, t):
    return k.ps if t else unit_banks(k)


def three_unit_banks(k):
    return unit_banks(k)[:, 0:3, :].rearrange("p b (a i) -> p (b a) i", a=4)


def outputs(k, t):
    return three_unit_banks(k) if t else three_banks(k)


def bank_of(k, n):
    return k.ps[:, n % 4, :].rearrange("p (a i) -> p a i", a=4)


def unit_banks(k):
    return k.ps_unit[:].rearrange("p s t n -> p (s t) n")


def three_banks(k):
    return k.ps[:, 0:3, :].rearrange("p b (a i) -> p (b a) i", a=4)


def pe_delta(pe, k):
    tensor = k.nc.tensor
    for g in range(HEADS):
        if g >= 4:
            pe.wait_ge(*k.dn_qkT_kept.next("pe"))
        for x in range(2):
            for t in range(TT):
                last = tensor.transpose(k.ps[:, g % 4, x * SEQ + t * P:x * SEQ + (t + 1) * P],
                                        k.proj[:, t, DQ + (2 * g + x) * P:DQ + (2 * g + x + 1) * P], k.ident)
        last.then_inc(*k.dn_qkT.up())
    pe.wait_ge(*k.dn_qkT_kept.next("pe", 4))
    for t in range(TT):
        pe.wait_ge(*k.dn_tri_g.next("pe"))
        if t:
            pe.wait_ge(*k.dn_rel.next("pe"))
        for g in range(3):
            last = tensor.matmul(k.ps[:, g, :], k.ones, k.dn_rhs[t][:, 4 * g:4 * g + 4, :], start=True, stop=True)
        last.then_inc(*k.dn_row.up())
        if t:
            pe.wait_ge(*k.dn_rel.next("pe"))
        tokens = slice(t * P, (t + 1) * P)
        for x, which in ((0, 1), (2, 0)):
            for h in range(HEADS):
                last = tensor.matmul(key_products(k, t)[:, x + h // 4, h % 4 * P:(h % 4 + 1) * P], k.dn_t[:, 1, h, tokens],
                                     k.dn_t[:, which, h, tokens], start=True, stop=True)
        last.then_inc(*k.dn_kk.up())
    pe.wait_ge(*k.dn_qk_kept.next("pe", TT))

    readers = [None] * 4
    banks = 0
    inverse = (k.dn_inv, k.dn_inv2)

    def group(count, kept, g, left, right, turn=False):
        nonlocal banks
        if readers[banks % 4]:
            pe.wait_ge(*readers[banks % 4])
        out = bank_of(k, banks)
        for x in range(4):
            n = 4 * g + x
            if turn:
                last = tensor.transpose(out[:, x, :], left[:, n, :], k.ident)
            else:
                last = tensor.matmul(out[:, x, :], left[:, n, :], right[:, n, :], start=True, stop=True)
        last.then_inc(*count.up())
        readers[banks % 4] = kept.next("issued")
        banks += 1

    for n in reversed(range(LEVELS)):
        for t in range(TT):
            rows = k.dn_rows_t[:, t]
            if n < LEVELS - 1:
                pe.wait_ge(*k.dn_off_ready.next("pe"))
                pe.wait_ge(*inverse_kept[t])
                for g in range(3):
                    group(k.dn_m_done, k.dn_m_kept, g, k.dn_off, inverse[t])
                for g in range(3):
                    pe.wait_ge(*k.dn_m_kept.next("pe"))
                    group(k.dn_up_done, k.dn_rows_kept, g, k.dn_m, rows)
            else:
                pe.wait_ge(*k.dn_up_kept.next("pe"))
                k.dn_off_ready.next("pe")
                inverse_kept = [None, None] if t == 0 else inverse_kept
            if n > 0:
                for g in range(3):
                    if n < LEVELS - 1:
                        pe.wait_ge(*k.dn_rows_kept.next("pe"))
                    group(k.dn_it_done, k.dn_it_kept, g, rows, None, turn=True)
                inverse_kept[t] = k.dn_it_kept.sem, k.dn_it_kept.seen["issued"]
    pe.wait_ge(*k.dn_rows_kept.next("pe", 6))

    out = three_banks(k)

    def each(left, right, out=out):
        for n in range(DIRS):
            d, h = divmod(n, HEADS)
            last = tensor.matmul(out[:, n, :], left(n, d, h), right(n, d, h), start=True, stop=True)
        return last

    each(lambda n, d, h: k.dn_rows_t[:, d, n, :],
         lambda n, d, h: k.proj[:, d, DV + h * HD:DV + (h + 1) * HD]).then_inc(*k.dn_tv.up())
    pe.wait_ge(*k.dn_vs_kept.next("pe"))
    each(lambda n, d, h: k.proj[:, d, DK + h * HD:DK + (h + 1) * HD], lambda n, d, h: k.dn_vs[:, n, :],
         three_unit_banks(k)).then_inc(*k.dn_s_done.up())
    pe.wait_ge(*k.dn_s_kept.next("pe"))
    pe.wait_ge(*k.dn_vs_kept.next("pe"))
    each(lambda n, d, h: k.dn_t[:, 1, h, late(d)], lambda n, d, h: k.dn_state[:, n, :]).then_inc(*k.dn_ks.up())
    each(lambda n, d, h: k.dn_t[:, 0, h, late(d)], lambda n, d, h: k.dn_state[:, n, :], three_unit_banks(k))\
        .then_inc(*k.dn_qs_done.up())
    pe.wait_ge(*k.dn_ks_kept.next("pe"))
    each(lambda n, d, h: k.dn_rows_t[:, 1 - d, n, :], lambda n, d, h: k.dn_r[:, n, :]).then_inc(*k.dn_tv2.up())
    pe.wait_ge(*k.dn_qs_kept.next("pe"))
    pe.wait_ge(*k.dn_v2_kept.next("pe"))
    for t in range(TT):
        for h in range(HEADS):
            for d in range(2):
                n = d * HEADS + h
                value = k.dn_v1 if t == early_tile(d) else k.dn_v2
                last = tensor.matmul(outputs(k, t)[:, h, :], k.dn_qk[:, t, n, :], value[:, n, :], start=d == 0, stop=d == 1)
        last.then_inc(*k.dn_o.up())


def dve_delta(dve, k):
    v = k.nc.vector

    def step(ins):
        ins.then_inc(*k.dve_step.up())
        dve.wait_ge(*k.dve_step.now())

    for d, tri in ((0, k.tri), (1, k.tri_t)):
        last = v.tensor_scalar(k.dn_outside[:, d, :], tri, -1.0, 1e30, ALU.add, ALU.mult)
    step(last)
    for g in range(HEADS):
        dve.wait_ge(*k.dn_qkT.next("dve"))
        at = 2 * g % HEADS
        v.tensor_copy(k.dn_t[:, 2 * g // HEADS, at:at + 2, :], k.ps[:, g % 4, :].rearrange("p (a s) -> p a s", a=2))\
            .then_inc(*k.dn_qkT_kept.up())
    rows = three_banks(k)
    for t in range(TT):
        dve.wait_ge(*k.dn_row.next("dve"))
        for n in range(DIRS):
            last = v.scalar_tensor_tensor(k.dn_dec[t][:, n, :], rows[:, n, :], k.dn_cum[:, t, n:n + 1],
                                          k.dn_outside[:, n // HEADS, :], ALU.subtract, ALU.add)
        last.then_inc(*k.dn_rel.up())
    for t in range(TT):
        dve.wait_ge(*k.dn_decay.next("dve"))
        dve.wait_ge(*k.dn_kk.next("dve"))
        for n in range(DIRS):
            h = n % HEADS
            v.scalar_tensor_tensor(k.dn_a[:, t, n, :], key_products(k, t)[:, h // 4, h % 4 * P:(h % 4 + 1) * P],
                                   k.dn_beta[:, t, n:n + 1], k.dn_dec[t][:, n, :], ALU.mult, ALU.mult)
        qk = key_products(k, t)[:, 2:4, :].rearrange("p b (a i) -> p (b a) i", a=4)[:, 0:HEADS, :]
        for d in range(2):
            last = v.tensor_tensor(k.dn_qk[:, t, dirs(d), :], qk, k.dn_dec[t][:, dirs(d), :], ALU.mult)
        last.then_inc(*k.dn_qk_kept.up())
        dve.wait_ge(*k.dn_qk_kept.now())
    banks = 0
    for n in reversed(range(LEVELS)):
        for t in range(TT):
            if n == LEVELS - 1:
                dve.wait_ge(*k.dn_off_ready.next("dve"))
                v.tensor_tensor(k.dn_rows_t[:, t], k.ident.unsqueeze(1).to_broadcast([P, DIRS, P]), first_off(k, t)[:],
                                ALU.subtract).then_inc(*k.dn_up_kept.up())
                dve.wait_ge(*k.dn_up_kept.now())
            else:
                banks += 3
                for g in range(3):
                    dve.wait_ge(*k.dn_up_done.next("dve"))
                    part = k.dn_rows_t[:, t, 4 * g:4 * g + 4, :]
                    v.tensor_tensor(part, part, bank_of(k, banks), ALU.subtract).then_inc(*k.dn_rows_kept.up())
                    banks += 1
            if n > 0:
                banks += 3
    out = three_banks(k)

    def by_token(to, scale, tile, out=out):
        for d in range(2):
            last = v.tensor_tensor(to[:, dirs(d), :], out[:, dirs(d), :],
                                   scale[:, tile(d), dirs(d)].unsqueeze(2).to_broadcast([P, HEADS, HD]), ALU.mult)
        return last

    minus_beta = k.dn_g
    step(v.tensor_scalar(minus_beta[:], k.dn_beta[:], -1.0, None, ALU.mult))
    dve.wait_ge(*k.dn_tv.next("dve"))
    by_token(k.dn_vs, k.dn_tail, lambda d: d).then_inc(*k.dn_vs_kept.up())
    by_token(k.dn_v1, k.dn_beta, lambda d: d).then_inc(*k.dn_vs_kept.up())
    dve.wait_ge(*k.dn_ks.next("dve"))
    for n in range(DIRS):
        d, h = divmod(n, HEADS)
        last = v.scalar_tensor_tensor(k.dn_r[:, n, :], out[:, n, :], k.dn_ecum[:, 1 - d, n:n + 1],
                                      k.proj[:, 1 - d, DV + h * HD:DV + (h + 1) * HD], ALU.mult, ALU.subtract)
    last.then_inc(*k.dn_ks_kept.up())
    dve.wait_ge(*k.dn_qs_done.next("dve"))
    by_token(k.dn_qs, k.dn_ecum, lambda d: 1 - d, three_unit_banks(k)).then_inc(*k.dn_qs_kept.up())
    dve.wait_ge(*k.dn_tv2.next("dve"))
    by_token(k.dn_v2, minus_beta, lambda d: 1 - d).then_inc(*k.dn_v2_kept.up())
    dve.wait_ge(*k.dn_qs_kept.now())
    for t in range(TT):
        dve.wait_ge(*k.dn_o.next("dve"))
        v.tensor_tensor(k.dn_a[:, t, dirs(0), :], outputs(k, t)[:, 0:HEADS, :], k.dn_qs[:, dirs(1 - t), :],
                        ALU.add).then_inc(*k.dn_o_kept.up())
    for t in range(TT):
        dve.wait_ge(*k.dn_osq.next("dve"))
        last = v.tensor_reduce(k.dn_ms[:, t, :], k.dn_a[:, t, dirs(1), :], AX_X, ALU.add)
    last.then_inc(*k.dn_oms.up())
    dve.wait_ge(*k.dn_oroot.next("dve"))
    step(v.reciprocal(k.dn_ms[:], k.dn_ms[:]))
    dve.wait_ge(*k.dn_gate_gained.next("dve"))
    for t in range(TT):
        gate = heads_of(k.proj[:, t, DG:DG + HW])
        for h in range(HEADS):
            ins = v.scalar_tensor_tensor(gate[:, h, :], k.dn_a[:, t, h, :], k.dn_ms[:, t, h:h + 1], gate[:, h, :],
                                         ALU.mult, ALU.mult)
    ins.then_inc(*k.turn_source.up(BLOCKS))


def even_mix_tile(k):
    def tile(kt, t):
        at = NQ + P * kt if kt < HEADS else DG + P * (kt - HEADS) if kt < 2 * HEADS else MQ + P * (kt - 2 * HEADS)
        return k.proj[:, t, at:at + P]
    return tile


ODD_ROWS = 7 * 16
SS_Q, SS_K, SS_MQ, SS_MK = 0, DIFF_MAPS, 2 * DIFF_MAPS, 2 * DIFF_MAPS + MEM_HEADS


def odd_mem_maps(k):
    def cols(buffer, at):
        return lambda t: buffer[:, t, at:at + HD]
    return [(turned_head(k.proj, MQ, h), turned_head(k.kv, 2 * MW, h), None, cols(k.kv, 3 * MW + h * HD),
             cols(k.proj, MG + h * HD), cols(k.proj, MG + h * HD)) for h in range(MEM_HEADS)]


def pool_odd_rows(pool, k):
    d = k.dram
    rope = d["c_rope"].rearrange("(t p) (x s) -> p t x s", p=P, x=2)
    lam = d["df_lambda_2"].rearrange("a b c -> (a b c)").partition_broadcast(P).rearrange("p (a b c) -> p a b c", a=2, b=2)
    for to, src in ((k.o_rope[:], rope), (k.o_lam_rows[:], lam),
                    (k.o_gain[:, 0, :], d["df_q_norm_2"][0].partition_broadcast(P)),
                    (k.o_gain[:, 1, :], d["df_k_norm_2"][0].partition_broadcast(P)),
                    (k.o_gain[:, 2, :], d["o_mem_q_norm_2"][0].partition_broadcast(P)),
                    (k.o_gain[:, 3, :], d["o_mem_k_norm_2"][0].partition_broadcast(P)),
                    (k.o_subln[:], d["df_subln_2"][0].partition_broadcast(P))):
        pool.dma_start(to, src).then_inc(*k.o_rows_in.up(16))


def rotate_in_place(own, k, which, at, step, tiles=range(TT), run=no_blocks):
    for t in tiles:
        x = k.proj[:, t, at:at + DIFF_W].rearrange("p (n x s) -> p n x s", n=DIFF_MAPS, x=2)
        x1, x2 = x[:, :, 0, :], x[:, :, 1, :]
        a, b, c, d = (k.o_tables[:, which, n, t, :].unsqueeze(1).to_broadcast([P, DIFF_MAPS, HALF]) for n in range(4))
        w0, w1 = k.o_work[:, t, 0], k.o_work[:, t, 1]
        own.tensor_tensor(w0, x2, b, ALU.mult)
        step(own.tensor_tensor(w1, x1, c, ALU.mult))
        run(1)
        own.tensor_tensor(x1, x1, a, ALU.mult)
        step(own.tensor_tensor(x2, x2, d, ALU.mult))
        run(1)
        own.tensor_tensor(x1, x1, w0, ALU.subtract)
        last = own.tensor_tensor(x2, x2, w1, ALU.add)
        if t != tiles[-1]:
            step(last)
            run(1)
    return last


def pool_odd_attention(pool, k):
    def step(ins):
        ins.then_inc(*k.pool_step.up())
        pool.wait_ge(*k.pool_step.now())

    pool.wait_ge(*k.o_tables_done.next("pool"))
    pool.wait_ge(*k.o_scaled.next("pool"))
    rotate_in_place(k.nc.gpsimd, k, 1, OK, step, tiles=(1,)).then_inc(*k.o_keys.up())


def act_keep_turned(act, k, run, pairs, n):
    for p in range(n):
        act.wait_ge(*k.o_turned.next("act"))
        bank = (k.o_turn_kept.made - k.o_turn_kept.first) % 4
        k.nc.scalar.activation(pairs(p), k.ps[:, bank, :].rearrange("p (a s) -> p a s", a=2), ACT.Copy)\
            .then_inc(*k.o_turn_kept.up())
        run(p % 2)


def act_odd_attention(act, k, run):
    a = k.nc.scalar
    run(2)
    act.wait_ge(*run.evacuated(0))
    act_squares(act, k, run, k.proj, MQ, MEM_HEADS, SS_MQ, k.o_junk_heads)
    act_squares(act, k, run, k.kv, 2 * MW, MEM_HEADS, SS_MK, k.o_junk_heads)
    act_root(act, k, SS_MQ, 2 * MEM_HEADS)
    mg = k.proj[:, :, MG:MG + MW]
    a.activation(mg, mg, ACT.Silu).then_inc(*k.o_gate_done.up())
    act.wait_ge(*k.o_lam_sums.next("act"))
    a.activation(k.lam[:, 0:2], k.lam[:, 0:2], ACT.Exp).then_inc(*k.o_lam_exp.up())
    run(13 - run.done)
    act_keep_turned(act, k, run, pairs_at(k.proj, MQ), 2)
    act_keep_turned(act, k, run, pairs_at(k.kv, 2 * MW), 2)
    act_attention(act, k, odd_mem_maps(k), k.o_att, run, 2)
    run(max(28 - run.done, 0))
    act.wait_ge(*run.evacuated(3))
    act_squares(act, k, run, k.proj, OQ, DIFF_MAPS, SS_Q, k.o_junk_heads)
    act_root(act, k, SS_Q, DIFF_MAPS)
    run(46 - run.done)
    act_keep_turned(act, k, run, pairs_at(k.proj, OQ), HEADS)
    run(50 - run.done)
    act.wait_ge(*run.evacuated(6))
    act_squares(act, k, run, k.proj, OK, DIFF_MAPS, SS_K, k.o_junk_heads)
    act_root(act, k, SS_K, DIFF_MAPS)
    run(68 - run.done)
    act_keep_turned(act, k, run, pairs_at(k.proj, OK), HEADS)
    run(72 - run.done)
    act.wait_ge(*k.o_keys.next("act", 2))
    for n in range(HEADS + 2):
        run(3)
        if n < HEADS:
            act.wait_ge(*k.d_max.next("act"))
            if n >= 2:
                act.wait_ge(*k.d_t.next("act free"))
            for m, to in ((0, k.att_e), (1, k.att_s)):
                for t in range(TT):
                    last = a.activation(to[:, n % 2, t, :], k.ps[:, m, t * SEQ:(t + 1) * SEQ], ACT.Exp,
                                        bias=k.att_max[:, 2 * n + m, t:t + 1],
                                        accum_out=k.att_sum[:, 2 * n + m, t:t + 1])
            last.then_inc(*k.d_e.up())
        if 1 <= n <= HEADS:
            act.wait_ge(*k.d_t.next("act"))
            if n >= 3:
                act.wait_ge(*k.d_o.next("act free"))
            a.activation(k.att_t[:, (n - 1) % 2], k.ps[:, 2, :].rearrange("p (a s) -> p a s", a=TT), ACT.Copy)\
                .then_inc(*k.d_c.up())
        if n >= 2:
            if n >= 4:
                act.wait_ge(k.d_sq.sem, k.d_sq.made - 1)
            act.wait_ge(*k.d_o.next("act"))
            for t in range(TT):
                last = a.activation(k.o_junk[:, n % 2, t, :], k.ps[:, 3, t * 2 * HD:(t + 1) * 2 * HD], ACT.Square,
                                    accum_out=k.o_ss[:, t, n - 2:n - 1])
            last.then_inc(*k.d_sq.up())
    act.wait_ge(*k.d_sq.now())
    a.activation(k.o_ss[:], k.o_ss[:], ACT.Sqrt, scale=1.0 / (2 * HD), bias=k.eps[:, 1:2]).then_inc(*k.o_root.up())
    run.rest()
    act.wait_ge(*run.evacuated(12))
    for h in range(0, HEADS, 2):
        cols = k.proj[:, :, OG + h * 2 * HD:OG + (h + 2) * 2 * HD]
        a.activation(cols, cols, ACT.Silu).then_inc(*k.o_gate_done.up())


def pe_turn_pairs(pe, k, run, pairs, n):
    for p in range(n):
        g = k.o_turned.made - k.o_turned.first
        if g >= 4:
            pe.wait_ge(*k.o_turn_kept.next("pe"))
        for x in range(2):
            for t in range(TT):
                last = k.nc.tensor.transpose(k.ps[:, g % 4, x * SEQ + t * P:x * SEQ + (t + 1) * P],
                                             pairs(p)[:, t, x * HD:(x + 1) * HD], k.ident)
        last.then_inc(*k.o_turned.up())
        run(p % 2)


def pe_odd_attention(pe, k, run):
    tensor = k.nc.tensor
    run(12)
    pe.wait_ge(*k.o_queries.next("pe"))
    pe_turn_pairs(pe, k, run, pairs_at(k.proj, MQ), 2)
    pe_turn_pairs(pe, k, run, pairs_at(k.kv, 2 * MW), 2)
    pe.wait_ge(k.o_turn_kept.sem, k.o_turn_kept.first + MEM_HEADS)
    pe_attention(pe, k, odd_mem_maps(k), k.o_att, run, 2)
    run(45 - run.done)
    pe.wait_ge(*k.o_queries.next("pe"))
    pe_turn_pairs(pe, k, run, pairs_at(k.proj, OQ), HEADS)
    run(67 - run.done)
    pe.wait_ge(*k.o_keys.next("pe", 2))
    pe_turn_pairs(pe, k, run, pairs_at(k.proj, OK), HEADS)
    pe.wait_ge(*k.o_turn_kept.next("pe", 4))
    run(71 - run.done)
    for n in range(HEADS + 2):
        run(3)
        if n < HEADS:
            if n >= 1:
                pe.wait_ge(*k.d_e.next("pe"))
            for m in range(2):
                q, key = turned_head(k.proj, OQ, 2 * n + m), turned_head(k.proj, OK, 2 * n + m)
                for t in range(TT):
                    last = tensor.matmul(k.ps[:, m, t * SEQ:(t + 1) * SEQ], q[:, t * P:(t + 1) * P], key, start=True, stop=True)
            last.then_inc(*k.d_s.up())
        if 1 <= n <= HEADS:
            pe.wait_ge(*k.d_a.next("pe"))
            if n >= 2:
                pe.wait_ge(*k.d_c.next("pe free"))
            for t in range(TT):
                for kt in range(TT):
                    last = tensor.transpose(k.ps[:, 2, kt * SEQ + t * P:kt * SEQ + (t + 1) * P],
                                            k.att_e[:, (n - 1) % 2, t, kt * P:(kt + 1) * P], k.ident)
            last.then_inc(*k.d_t.up())
        if n >= 2:
            h = n - 2
            if h == 0:
                pe.wait_ge(*run.evacuated(9))
            pe.wait_ge(*k.d_c.next("pe"))
            if h >= 1:
                pe.wait_ge(*k.d_y.next("pe"))
            for t in range(TT):
                for kt in range(TT):
                    last = tensor.matmul(k.ps[:, 3, t * 2 * HD:(t + 1) * 2 * HD], k.att_t[:, h % 2, kt, t * P:(t + 1) * P],
                                         k.proj[:, kt, OV + h * 2 * HD:OV + (h + 1) * 2 * HD], start=kt == 0, stop=kt == TT - 1)
            last.then_inc(*k.d_o.up())
    run.rest()
    pe.wait_ge(*k.d_y.next("pe"))
    pe.wait_ge(*k.d_e.next("pe"))


def dve_odd_attention(dve, k, run):
    v = k.nc.vector

    def step(ins):
        ins.then_inc(*k.dve_step.up())
        dve.wait_ge(*k.dve_step.now())

    run(1)
    dve.wait_ge(*k.o_rows_in.next("dve", ODD_ROWS))
    step(v.tensor_scalar(k.o_gain[:, 0, :], k.o_gain[:, 0, :], HD ** -0.5, None, ALU.mult))
    v.scalar_tensor_tensor(k.o_mem_gain[:], k.o_gain[:, 2, :], HD ** -0.5, k.o_gain[:, 3, :], ALU.mult, ALU.mult)
    for which in range(2):
        for n, (x, part) in enumerate(((0, 0), (1, 1), (1, 0), (0, 1))):
            gain = k.o_gain[:, which, part * HALF:(part + 1) * HALF].unsqueeze(1).to_broadcast([P, TT, HALF])
            last = v.tensor_tensor(k.o_tables[:, which, n], k.o_rope[:, :, x, :], gain, ALU.mult)
    last.then_inc(*k.o_tables_done.up())
    run(2)
    pairs = k.o_lam_rows
    step(v.tensor_tensor(pairs[:, :, 0, :], pairs[:, :, 0, :], pairs[:, :, 1, :], ALU.mult))
    v.tensor_reduce(k.lam[:, 0:2], pairs[:, :, 0, :], AX_X, ALU.add).then_inc(*k.o_lam_sums.up())
    run(5)
    dve_divide(dve, k, SS_MQ, 2 * MEM_HEADS)
    for t in range(TT):
        scale_heads(k, k.kv, 2 * MW, MEM_HEADS, SS_MK, t)
        last = scale_heads(k, k.proj, MQ, MEM_HEADS, SS_MQ, t)
    step(last)
    for t in range(TT):
        mem_q = k.proj[:, t, MQ:MQ + MW].rearrange("p (n d) -> p n d", n=MEM_HEADS)
        last = v.tensor_tensor(mem_q, mem_q, k.o_mem_gain[:].unsqueeze(1).to_broadcast([P, MEM_HEADS, HD]), ALU.mult)
    last.then_inc(*k.o_queries.up())
    dve.wait_ge(*k.o_lam_exp.next("dve"))
    step(v.tensor_tensor(k.lam[:, 2:3], k.lam[:, 0:1], k.lam[:, 1:2], ALU.subtract))
    step(v.tensor_scalar(k.lam[:, 2:3], k.lam[:, 2:3], LAM_INIT, None, ALU.add))
    dve.wait_ge(*k.o_gate_done.next("dve"))
    run(14 - run.done)
    dve_attention(dve, k, odd_mem_maps(k), k.o_att, run, 2)
    run(35 - run.done)
    dve_divide(dve, k, SS_Q, DIFF_MAPS)
    for t in range(TT):
        step(scale_heads(k, k.proj, OQ, DIFF_MAPS, SS_Q, t))
        run(1)
    rotate_in_place(v, k, 0, OQ, step, run=run).then_inc(*k.o_queries.up())
    run(57 - run.done)
    dve_divide(dve, k, SS_K, DIFF_MAPS)
    scale_heads(k, k.proj, OK, DIFF_MAPS, SS_K, 1).then_inc(*k.o_scaled.up())
    step(scale_heads(k, k.proj, OK, DIFF_MAPS, SS_K, 0))
    run(2)
    rotate_in_place(v, k, 1, OK, step, tiles=(0,), run=run).then_inc(*k.o_keys.up())
    run(71 - run.done)
    for n in range(HEADS + 2):
        run(2)
        if 1 <= n <= HEADS:
            m = 2 * (n - 1)
            e0, e1 = k.att_e[:, (n - 1) % 2], k.att_s[:, (n - 1) % 2]
            dve.wait_ge(*k.d_e.next("dve"))
            step(v.reciprocal(k.att_sum[:, m:m + 2, :], k.att_sum[:, m:m + 2, :]))
            step(v.tensor_scalar(k.att_sum[:, m + 1, :], k.att_sum[:, m + 1, :], k.lam[:, 2:3], None, ALU.mult))
            for t in range(TT):
                last = v.tensor_scalar(e1[:, t, :], e1[:, t, :], k.att_sum[:, m + 1, t:t + 1], None, ALU.mult)
            step(last)
            for t in range(TT):
                last = v.scalar_tensor_tensor(e0[:, t, :], e0[:, t, :], k.att_sum[:, m, t:t + 1], e1[:, t, :],
                                              ALU.mult, ALU.subtract)
            last.then_inc(*k.d_a.up())
        run(1)
        if n < HEADS:
            dve.wait_ge(*k.d_s.next("dve"))
            v.tensor_reduce(k.att_max[:, 2 * n:2 * n + 2, :], k.ps[:, 0:2, :].rearrange("p m (t s) -> p m t s", t=TT),
                            AX_X, ALU.max, negate=True).then_inc(*k.d_max.up())
        if n >= 2:
            h = n - 2
            dve.wait_ge(*k.d_sq.next("dve"))
            v.tensor_tensor(k.proj[:, :, OV + h * 2 * HD:OV + (h + 1) * 2 * HD], k.ps[:, 3, :].rearrange("p (t e) -> p t e", t=TT),
                            k.o_subln[:].unsqueeze(1).to_broadcast([P, TT, 2 * HD]), ALU.mult).then_inc(*k.d_y.up())
    dve.wait_ge(*k.o_root.next("dve"))
    step(v.reciprocal(k.o_ss[:], k.o_ss[:]))
    step(v.tensor_scalar(k.o_ss[:], k.o_ss[:], 1.0 - LAM_INIT, None, ALU.mult))
    run.rest()
    dve.wait_ge(*k.d_y.now())
    for h in range(HEADS):
        if h % 2 == 0:
            dve.wait_ge(*k.o_gate_done.next("dve"))
        cols = slice(h * 2 * HD, (h + 1) * 2 * HD)
        for t in range(TT):
            y, gate = k.proj[:, t, OV:OV + DIFF_W][:, cols], k.proj[:, t, OG:OG + DIFF_W][:, cols]
            last = v.scalar_tensor_tensor(y, y, k.o_ss[:, t, h:h + 1], gate, ALU.mult, ALU.mult)
        last.then_inc(*k.turn_source.up(1 + (BLOCKS - HEADS) * (h == HEADS - 1)))


def odd_mix_tile(k):
    def tile(kt, t):
        at = OV + P * kt if kt < DIFF_MAPS else MG + P * (kt - DIFF_MAPS)
        return k.proj[:, t, at:at + P]
    return tile


CONV_UNITS = 2 * CONV_C // NC
IN_UNITS, OUT_UNITS, MEM_UNITS = D_IN // NC, D // NC, 4 * MW // NC
ODD_UNITS = 4 * DIFF_W // NC
DELTA_UNITS = 4 * HW // NC
FIRST_SUMS = DEPTH * (OUT_UNITS + FF_GROUPS * OUT_UNITS)


EVEN_COLUMNS = [MQ, MG, 0, NC, 2 * NC, 5 * NC, 4 * NC, 3 * NC]


def x_tile(k):
    return lambda kt, t: k.x[:, t, kt * P:(kt + 1) * P]


def rows_tile(buffer):
    return lambda kt, t: buffer[:, t, kt * P:(kt + 1) * P]


def tokens(ap):
    return ap.rearrange("(t p) d -> p t d", p=P)


def two_blocks_kernel(nc, dram, out):
    k = set_up(nc, dram, out)
    first_buffers(k)
    second_buffers(k)
    d = dram

    with nc.Block() as block:

        @block.sync
        def _(sp):
            sp.dma_start(k.square[:], d["c_square"].rearrange("p (a b) -> p a b", a=4)).then_inc(*k.consts_in.up(16))
            sp.dma_start(k.x[:], tokens(d["x"][0])).then_inc(*k.x_in.up(16))
            for l in range(DEPTH):
                sp_units(sp, k, d["w_in"][l], IN_UNITS)
                sp_units(sp, k, d["w_out"][l], OUT_UNITS)
                sp_feed_forward(sp, k, d["w_ff1"][l], d["w_ff2"][l])
            sp_units(sp, k, d["e_w_mem_kv_2"][0], MEM_UNITS // 2)
            sp_units(sp, k, d["o_w_mem_kv_2"][0], MEM_UNITS // 2)
            sp_units(sp, k, d["e_w_in_2"][0], DELTA_UNITS, DQ)
            for at in EVEN_COLUMNS:
                sp_unit(sp, k, d["e_w_in_2"][0], 0, k.block0["sp"], 0, at if at < MQ else at + W_MEM - MQ)
                k.block0["sp"] += BLOCKS
            sp_units(sp, k, d["e_w_out_2"][0], OUT_UNITS)
            sp_units(sp, k, d["o_w_in_2"][0], IN_UNITS - ODD_UNITS, MQ)
            sp_units(sp, k, d["o_w_in_2"][0], ODD_UNITS)
            sp_units(sp, k, d["o_w_out_2"][0], OUT_UNITS)
            for c in range(OUT_UNITS):
                sp.wait_ge(k.stats_ready, FIRST_SUMS + OUT_UNITS + c + 1)
                cols = slice(c * NC, (c + 1) * NC)
                sp.dma_start(tokens(k.out[0])[:, :, cols], k.x[:, :, cols]).then_inc(*k.stored.up(16))
            sp.wait_ge(*k.stored.now())

        @block.gpsimd
        def _(pool):
            pool.sem_inc(k.relu2_ready, 2)
            nc.gpsimd.memset(k.eps[:, 0:1], LN_EPS)
            nc.gpsimd.memset(k.eps[:, 1:2], EPS).then_inc(*k.eps_set.up())
            with nc.allow_non_contiguous_dma(reason="positions"):
                pool.dma_start(k.pos_i[:], d["positions"].rearrange("a (t p) -> p (a t)", p=P)).then_inc(*k.pos_in.up(16))
            pool.dma_start(k.inv_freq[:], d["c_inv_freq"][0].partition_broadcast(P)).then_inc(*k.pos_in.up(16))
            for l in range(DEPTH):
                if l:
                    pool.wait_ge(*k.turned.next("pool", BLOCKS))
                pool_first_rows(pool, k, l)
                pool_conv(pool, k)
                pool_hgrn(pool, k)
                pool_retention(pool, k, l)
                pool.wait_ge(*k.turned.next("pool", BLOCKS if l else 2 * BLOCKS))
                pool_rows(pool, k, d["ln1_g"][l], d["ln1_b"][l])
                pool.wait_ge(*k.turned.next("pool", BLOCKS))
                pool_rows(pool, k, d["ln2_g"][l], d["ln2_b"][l])
                if l == DEPTH - 1:
                    pool.dma_start(k.mem[:], tokens(d["mem_2"][0])).then_inc(*k.mem_in.up(16))
                    pool.dma_start(k.mem_gain[:], d["mem_norm_g_2"].partition_broadcast(P)).then_inc(*k.mem_in.up(16))
                k.block0["pool"] += (IN_UNITS + OUT_UNITS) * BLOCKS
                pool_feed_forward(pool, k, l)
            pool.wait_ge(*k.normed.next("pool", BLOCKS))
            pool_rows(pool, k, d["e_ln_g_2"][0])
            with nc.allow_non_contiguous_dma(reason="24 columns"):
                gates = d["e_w_in_2"][0].rearrange("(kt p) n -> p kt n", p=P)[:, :, W_GATES:W_GATES + DN_GATES]
                pool.dma_start(k.gw_raw[:], gates).then_inc(*k.gw_in.up(16))
            pool.wait_ge(*k.turned.next("pool", 2 * BLOCKS))
            pool_even_rows(pool, k)
            pool_delta(pool, k)
            pool.wait_ge(*k.turned.next("pool", BLOCKS))
            pool_rows(pool, k, d["o_ln_g_2"][0])
            pool.wait_ge(*k.turned.next("pool", BLOCKS))
            pool_odd_rows(pool, k)
            pool_odd_attention(pool, k)

        @block.scalar
        def _(act):
            for c in range(HI_SLOTS):
                act_split(act, k, 0, c)
            act.wait_ge(*k.eps_set.next("act"))
            for l in range(DEPTH):
                act_turn(act, k)
                split_units(act, k, "act", act_split, CONV_UNITS, act_take_proj(act, k))
                run = Meanwhile(act, k, "act", act_split, IN_UNITS - CONV_UNITS, act_take_proj(act, k, HQ))
                act_conv(act, k, l, run)
                if l == 0:
                    act_positions(act, k)
                act_hgrn(act, k, l, run)
                act_retention(act, k, l, run)
                act_turn(act, k)
                split_units(act, k, "act", act_split, OUT_UNITS)
                act_layer_norm(act, k)
                act_turn(act, k)
                act_feed_forward(act, k, l, act_memory(act, k) if l == DEPTH - 1 else None)
                if l < DEPTH - 1:
                    act_layer_norm(act, k)
            run = Meanwhile(act, k, "act", act_split, MEM_UNITS, act_take_memory(act, k))
            run(1)
            act_layer_norm(act, k)
            run(10)
            act.wait_ge(*k.normed.next("act", BLOCKS))
            act_rms(act, k, k.x, k.normed_x)
            run(6)
            act_gate_split(act, k)
            run.rest()
            act_turn(act, k)
            split_units(act, k, "act", act_split, DELTA_UNITS, act_take_proj(act, k, DQ))
            run = Meanwhile(act, k, "act", act_split, IN_UNITS - DELTA_UNITS, act_take_columns(act, k, EVEN_COLUMNS))
            act_even_inputs(act, k, run)
            act_even_attention(act, k)
            act_delta(act, k)
            act_turn(act, k)
            split_units(act, k, "act", act_split, OUT_UNITS)
            act_root_mean_square(act, k)
            act_turn(act, k)
            split_units(act, k, "act", act_split, IN_UNITS - ODD_UNITS, act_take_proj(act, k, MQ))
            act_odd_attention(act, k, Meanwhile(act, k, "act", act_split, ODD_UNITS, act_take_proj(act, k)))
            act_turn(act, k)
            split_units(act, k, "act", act_split, OUT_UNITS, last=True)

        @block.vector
        def _(dve):
            dve.sem_inc(k.lo_ready, BLOCKS)
            dve.sem_inc(k.evacuated, 2 * BLOCKS)
            dve.sem_inc(k.f_lo_ready, 2)
            dve.wait_ge(*k.consts_in.next("dve", 16))
            dve.wait_ge(*k.x_in.next("dve", 16))
            nc.vector.memset(k.rstd[:], 0.0).then_inc(*k.turn_source.up(BLOCKS))
            for c in range(HI_SLOTS):
                dve_split(dve, k, 0, c)
            for l in range(DEPTH):
                if l == 0:
                    dve_turn(dve, k)
                dve_scale_residual(dve, k)
                split_units(dve, k, "dve", dve_split, CONV_UNITS)
                run = Meanwhile(dve, k, "dve", dve_split, IN_UNITS - CONV_UNITS)
                if l == 0:
                    dve_positions(dve, k)
                dve_conv(dve, k, l, run)
                dve_hgrn(dve, k, l, run)
                dve_retention(dve, k, l, run)
                dve_turn(dve, k)
                split_units(dve, k, "dve", dve_split, OUT_UNITS, dve_take_residual(dve, k))
                dve_layer_norm(dve, k, OUT_UNITS, k.turn_source, after=dve_turn_behind(dve, k))
                dve_scale_residual(dve, k)
                dve_feed_forward(dve, k, l, dve_memory(dve, k) if l == DEPTH - 1 else None)
                if l < DEPTH - 1:
                    dve_layer_norm(dve, k, FF_GROUPS * OUT_UNITS, k.turn_source, after=dve_turn_behind(dve, k))
            run = Meanwhile(dve, k, "dve", dve_split, MEM_UNITS)
            dve_layer_norm(dve, k, FF_GROUPS * OUT_UNITS, k.normed, run)
            run(14 - run.done)
            dve.wait_ge(*k.row_in.next("dve", 16))
            dve_rms(dve, k, k.x, k.normed_x, k.gain, run)
            run(20 - run.done)
            dve_gate_split(dve, k)
            run.rest()
            dve_turn(dve, k)
            split_units(dve, k, "dve", dve_split, DELTA_UNITS)
            dve_gate_columns(dve, k)
            dve_even_inputs(dve, k, Meanwhile(dve, k, "dve", dve_split, IN_UNITS - DELTA_UNITS))
            dve_even_attention(dve, k)
            dve_delta(dve, k)
            dve_turn(dve, k)
            split_units(dve, k, "dve", dve_split, OUT_UNITS, dve_take_residual(dve, k))
            dve.wait_ge(*k.row_in.next("dve", 16))
            dve_mean_square(dve, k, OUT_UNITS)
            dve_rms(dve, k, k.x, k.normed_x, k.gain, after=dve_turn_behind(dve, k))
            split_units(dve, k, "dve", dve_split, IN_UNITS - ODD_UNITS)
            dve_odd_attention(dve, k, Meanwhile(dve, k, "dve", dve_split, ODD_UNITS))
            dve_turn(dve, k)
            split_units(dve, k, "dve", dve_split, OUT_UNITS, dve_take_residual(dve, k), last=True)

        @block.tensor
        def _(pe):
            pe.sem_inc(k.block_done, HI_SLOTS)
            pe.sem_inc(k.f_turned, 2)
            pe.wait_ge(*k.consts_in.next("pe", 16))
            for l in range(DEPTH):
                pe_units(pe, k, CONV_UNITS, x_tile(k))
                run = Meanwhile(pe, k, "pe", pe_block, IN_UNITS - CONV_UNITS)
                pe_conv(pe, k, l, run)
                pe_hgrn(pe, k, l, run)
                pe_retention(pe, k, l, run)
                pe_units(pe, k, OUT_UNITS, first_mix_tile(k))
                pe_feed_forward(pe, k, l, x_tile(k), pe_memory(pe, k) if l == DEPTH - 1 else None)
            pe_turn_end(pe, k)
            pe_units(pe, k, MEM_UNITS)
            pe_units(pe, k, DELTA_UNITS, rows_tile(k.normed_x))
            pe_gate_columns(pe, k)
            pe_even_inputs(pe, k, Meanwhile(pe, k, "pe", pe_block, IN_UNITS - DELTA_UNITS))
            pe_even_attention(pe, k)
            pe_delta(pe, k)
            pe_units(pe, k, OUT_UNITS, even_mix_tile(k))
            pe_units(pe, k, IN_UNITS - ODD_UNITS, rows_tile(k.normed_x))
            pe_odd_attention(pe, k, Meanwhile(pe, k, "pe", pe_block, ODD_UNITS))
            pe_units(pe, k, OUT_UNITS, odd_mix_tile(k))

    for old, made in k.taken_over:
        assert old.made == made, old.sem


INPUTS = ("x", "positions", "w_in", "w_dw", "b_dw", "conv_ln_g", "conv_ln_b", "hgrn_lb", "hgrn_norm_g", "ret_gn_g", "ret_gn_b",
          "w_out", "ln1_g", "ln1_b", "w_ff1", "w_ff2", "ln2_g", "ln2_b", "mem_2", "mem_norm_g_2", "e_ln_g_2", "e_w_in_2",
          "e_w_mem_kv_2", "e_w_out_2", "na_q_norm_2", "na_k_norm_2", "na_rpb_2", "dn_conv_w_2", "dn_a_log_2", "dn_dt_bias_2",
          "dn_out_norm_2", "e_mem_q_norm_2", "e_mem_k_norm_2", "o_ln_g_2", "o_w_in_2", "o_w_mem_kv_2", "o_w_out_2",
          "df_q_norm_2", "df_k_norm_2", "df_lambda_2", "df_subln_2", "o_mem_q_norm_2", "o_mem_k_norm_2")


def kernel(**inputs):
    import concourse.bacc as bacc
    from concourse.bass_utils import run_bass_kernel_spmd

    nc = bacc.Bacc("TRN2", target_bir_lowering=False, num_devices=1)
    arrays = {name: np.ascontiguousarray(inputs[name]) for name in INPUTS}
    arrays.update(constants())
    dram = {name: nc.dram_tensor(f"in_{name}_dram", a.shape, mybir.dt.from_np(a.dtype), kind="ExternalInput").ap()
            for name, a in arrays.items()}
    out = nc.dram_tensor("out_0_dram", (1, SEQ, D), F32, kind="ExternalOutput").ap()
    two_blocks_kernel(nc, dram, out)
    result = run_bass_kernel_spmd(nc, [{f"in_{name}_dram": a for name, a in arrays.items()}], core_ids=[0])
    return result.results[0]["out_0_dram"]
```
